# Optimizing a Trainium2 kernel written in Bass

```python
import jax, jax.numpy as jnp
from jax import lax
import numpy as np
import math
import jax
import jax.numpy as jnp

D_MODEL = 1024
BATCH = 1
SEQ = 256
DEPTH = 2

HEAD_DIM = 64
POOL_WIDTH = D_MODEL // 4
POOL_WINDOWS = (2, 4, 8, 16)
N_POOL_GROUPS = len(POOL_WINDOWS)
POOL_GC = POOL_WIDTH // N_POOL_GROUPS
ATTN_WIDTH = D_MODEL - POOL_WIDTH
N_ATTN_HEADS = ATTN_WIDTH // HEAD_DIM
DIL_PATTERNS = ((128, 1), (512, 4), (2048, 16))
HEADS_PER_PATTERN = N_ATTN_HEADS // len(DIL_PATTERNS)
ROT_DIM = HEAD_DIM // 4
ROPE_THETA = 500000.0
BLK = 128
D_FF = 4 * D_MODEL
PLE_DIM = 256
EPS = 1e-6


def rmsnorm(x, g):
    xf = x.astype(jnp.float32)
    y = xf * lax.rsqrt(jnp.mean(xf * xf, axis=-1, keepdims=True) + EPS)
    return (y * g.astype(jnp.float32)).astype(x.dtype)

def rotary_tables(positions, dtype):
    inv_freq = ROPE_THETA ** (-jnp.arange(0, ROT_DIM, 2, dtype=jnp.float32) / ROT_DIM)
    ang = positions.astype(jnp.float32)[..., None] * inv_freq
    return jnp.cos(ang)[:, :, None, :].astype(dtype), jnp.sin(ang)[:, :, None, :].astype(dtype)

def apply_partial_rotary(x, cos, sin):
    half = ROT_DIM // 2
    x1 = x[..., :half]
    x2 = x[..., half:ROT_DIM]
    rot = jnp.concatenate([x1 * cos - x2 * sin, x2 * cos + x1 * sin], axis=-1)
    return jnp.concatenate([rot, x[..., ROT_DIM:]], axis=-1)

def pool_mixer(u, w, scale):
    B, S, _ = u.shape
    ug = u.reshape(B, S, N_POOL_GROUPS, POOL_GC).astype(jnp.float32)
    c = lax.cumsum(ug, axis=1)
    c0 = jnp.pad(c, ((0, 0), (1, 0), (0, 0), (0, 0)))
    t = jnp.arange(S, dtype=jnp.int32)
    win = jnp.array(POOL_WINDOWS, dtype=jnp.int32)
    lo = jnp.maximum(t[:, None] + 1 - win[None, :], 0)
    c_lo = jnp.take_along_axis(c0, lo[None, :, :, None], axis=1)
    cnt = (t[:, None] + 1 - lo).astype(jnp.float32)
    y = ((c - c_lo) / cnt[None, :, :, None] - ug).astype(u.dtype)
    y = jnp.einsum('bsgc,gcd->bsgd', y, w).reshape(B, S, POOL_WIDTH)
    return y * scale

def dilated_window_attention(q, k, v, window, dil):
    B, S, H, Dh = q.shape
    steps = window // dil
    L = -(-S // (dil * BLK)) * BLK
    pad = L * dil - S
    nb = L // BLK

    def to_strided(a):
        a = jnp.pad(a, ((0, 0), (0, pad), (0, 0), (0, 0)))
        a = a.reshape(B, L, dil, H, Dh).transpose(0, 2, 1, 3, 4)
        return a.reshape(B, dil, nb, BLK, H, Dh)

    def with_prev(a):
        prev = jnp.pad(a[:, :, :-1], ((0, 0), (0, 0), (1, 0), (0, 0), (0, 0), (0, 0)))
        return jnp.concatenate([prev, a], axis=3)

    qs = to_strided(q)
    kb = with_prev(to_strided(k))
    vb = with_prev(to_strided(v))
    s = jnp.einsum('brnqhd,brnkhd->brnhqk', qs, kb,
                   preferred_element_type=jnp.float32) * (HEAD_DIM ** -0.5)
    qi = jnp.arange(nb)[:, None] * BLK + jnp.arange(BLK)[None, :]
    ki = jnp.arange(nb)[:, None] * BLK - BLK + jnp.arange(2 * BLK)[None, :]
    dist = qi[:, :, None] - ki[:, None, :]
    valid = (dist >= 0) & (dist <= steps) & (ki[:, None, :] >= 0)
    s = jnp.where(valid[None, None, :, None], s, -jnp.inf)
    m = jnp.max(s, axis=-1, keepdims=True)
    e = jnp.exp(s - m)
    l = jnp.sum(e, axis=-1, keepdims=True)
    o = jnp.einsum('brnhqk,brnkhd->brnqhd', e / l, vb.astype(jnp.float32))
    lse = (m + jnp.log(l))[..., 0]
    o = o.reshape(B, dil, L, H, Dh).transpose(0, 2, 1, 3, 4).reshape(B, L * dil, H, Dh)[:, :S]
    lse = lse.transpose(0, 1, 2, 4, 3).reshape(B, dil, L, H).transpose(0, 2, 1, 3)
    lse = lse.reshape(B, L * dil, H)[:, :S]
    return o, lse

def dilated_mixer(q, k, v):
    outs, lses = [], []
    for g, (window, dil) in enumerate(DIL_PATTERNS):
        sl = slice(g * HEADS_PER_PATTERN, (g + 1) * HEADS_PER_PATTERN)
        o, lse = dilated_window_attention(q[:, :, sl], k[:, :, sl], v[:, :, sl], window, dil)
        outs.append(o)
        lses.append(lse)
    wts = jax.nn.softmax(jnp.stack(lses, axis=0), axis=0)
    o = jnp.concatenate([outs[g] * wts[g][..., None] for g in range(len(DIL_PATTERNS))], axis=2)
    B, S = q.shape[0], q.shape[1]
    return o.reshape(B, S, ATTN_WIDTH).astype(q.dtype)

def first_inputs(seed: int = 0) -> dict:
    key = jax.random.key(seed)
    ks = jax.random.split(key, 16)
    f32 = jnp.float32
    n_in = POOL_WIDTH + 3 * ATTN_WIDTH
    return {
        "x": jax.random.normal(ks[0], (BATCH, SEQ, D_MODEL), f32),
        "p": jax.random.normal(ks[1], (DEPTH, BATCH, SEQ, PLE_DIM), f32),
        "positions": jnp.broadcast_to(jnp.arange(SEQ, dtype=jnp.int32), (BATCH, SEQ)),
        "norm1": 1.0 + 0.02 * jax.random.normal(ks[2], (DEPTH, D_MODEL), f32),
        "w_in": jax.random.normal(ks[3], (DEPTH, D_MODEL, n_in), f32) * D_MODEL ** -0.5,
        "pool_w": jax.random.normal(ks[4], (DEPTH, N_POOL_GROUPS, POOL_GC, POOL_GC), f32) * POOL_GC ** -0.5,
        "pool_scale": 1.0 + 0.02 * jax.random.normal(ks[5], (DEPTH, POOL_WIDTH), f32),
        "w_out": jax.random.normal(ks[6], (DEPTH, POOL_WIDTH + ATTN_WIDTH, D_MODEL), f32) * (POOL_WIDTH + ATTN_WIDTH) ** -0.5,
        "norm2": 1.0 + 0.02 * jax.random.normal(ks[7], (DEPTH, D_MODEL), f32),
        "w_up": jax.random.normal(ks[8], (DEPTH, D_MODEL, D_FF), f32) * D_MODEL ** -0.5,
        "w_down": jax.random.normal(ks[9], (DEPTH, D_FF, D_MODEL), f32) * D_FF ** -0.5,
        "norm3": 1.0 + 0.02 * jax.random.normal(ks[10], (DEPTH, D_MODEL), f32),
        "w_gate": jax.random.normal(ks[11], (DEPTH, D_MODEL, D_MODEL), f32) * D_MODEL ** -0.5,
        "w_ple": jax.random.normal(ks[12], (DEPTH, PLE_DIM, D_MODEL), f32) * PLE_DIM ** -0.5,
        "final_norm": 1.0 + 0.02 * jax.random.normal(ks[13], (D_MODEL,), f32),
    }

def first_block(x, p, positions, norm1, w_in, pool_w, pool_scale, w_out, norm2, w_up, w_down,
              norm3, w_gate, w_ple, final_norm):
    B, S, _ = x.shape
    cos, sin = rotary_tables(positions, x.dtype)
    h = x
    for i in range(DEPTH):
        hn = rmsnorm(h, norm1[i])
        z = hn @ w_in[i]
        u = z[..., :POOL_WIDTH]
        q, k, v = jnp.split(z[..., POOL_WIDTH:], 3, axis=-1)
        q = apply_partial_rotary(q.reshape(B, S, N_ATTN_HEADS, HEAD_DIM), cos, sin)
        k = apply_partial_rotary(k.reshape(B, S, N_ATTN_HEADS, HEAD_DIM), cos, sin)
        v = v.reshape(B, S, N_ATTN_HEADS, HEAD_DIM)
        pool_out = pool_mixer(u, pool_w[i], pool_scale[i])
        attn_out = dilated_mixer(q, k, v)
        h = h + jnp.concatenate([pool_out, attn_out], axis=-1) @ w_out[i]
        hn = rmsnorm(h, norm2[i])
        h = h + jnp.square(jax.nn.relu(hn @ w_up[i])) @ w_down[i]
        gate = jax.nn.sigmoid(rmsnorm(h, norm3[i]) @ w_gate[i])
        h = h + gate * (p[i] @ w_ple[i])
    return rmsnorm(h, final_norm)


DEPTH_2 = 1

GRID_W = 64
CTX_LEN = 256
DN_HEADS = 4
DN_DK = 128
DN_DV = 128
DN_KEY = DN_HEADS * DN_DK
DN_VAL = DN_HEADS * DN_DV
DN_CONV = 3
CHUNK = 64
SC_WIDTH = 512
SC_CONV = 3
FN_GROUPS = 4
FN_GROUP_DIM = 128
FN_WIDTH = FN_GROUPS * FN_GROUP_DIM
N_BRANCH = 3
D_FF_2 = ((8 * D_MODEL // 3 + 255) // 256) * 256
IN_SIZES = (2 * DN_KEY + DN_VAL, DN_VAL, 4 * DN_HEADS, 3 * SC_WIDTH, FN_WIDTH)
N_IN = 2 * DN_KEY + DN_VAL + DN_VAL + 4 * DN_HEADS + 3 * SC_WIDTH + FN_WIDTH


def split_cols(p, sizes):
    out = []
    start = 0
    for s in sizes:
        out.append(p[..., start:start + s])
        start += s
    return out

def rmsnorm_2(t, gain):
    tf = t.astype(jnp.float32)
    y = tf * lax.rsqrt(jnp.mean(tf * tf, axis=-1, keepdims=True) + EPS) * gain.astype(jnp.float32)
    return y.astype(t.dtype)

def modulate(t, gain, shift, scale):
    return rmsnorm_2(t, gain) * (1 + scale) + shift

def l2norm(t):
    tf = t.astype(jnp.float32)
    return tf * lax.rsqrt(jnp.sum(tf * tf, axis=-1, keepdims=True) + EPS)

def dwconv(u, w):
    k = w.shape[0]
    return lax.conv_general_dilated(
        u, w[:, None, :].astype(u.dtype), window_strides=(1,), padding=[(k // 2, k // 2)],
        dimension_numbers=("NWC", "WIO", "NWC"), feature_group_count=u.shape[-1])

def conv_seq(u, w):
    return dwconv(u, w)

def conv_grid_rows(u, w):
    bsz, length, ch = u.shape
    rows = length // GRID_W
    return dwconv(u.reshape(bsz * rows, GRID_W, ch), w).reshape(bsz, length, ch)

def gated_delta_chunked(q, k, v, beta, g, s0):
    bsz, length, heads, _ = q.shape
    dv = v.shape[-1]
    n = length // CHUNK

    def blocks(t):
        t = t.astype(jnp.float32).reshape((bsz, n, CHUNK, heads) + t.shape[3:])
        return jnp.moveaxis(t, 3, 1)

    q, k, v, beta, g = (blocks(t) for t in (q, k, v, beta, g))
    g = jnp.cumsum(g, axis=-1)
    idx = jnp.arange(CHUNK)
    lower = idx[:, None] >= idx[None, :]
    strict = idx[:, None] > idx[None, :]
    decay = jnp.exp(jnp.where(lower, g[..., :, None] - g[..., None, :], -jnp.inf))
    kb = k * beta[..., None]
    a = jnp.where(strict, jnp.einsum("bhnid,bhnjd->bhnij", kb, k) * decay, 0.0)
    eye = jnp.eye(CHUNK, dtype=jnp.float32)
    t_inv = lax.linalg.triangular_solve(a + eye, jnp.broadcast_to(eye, a.shape), left_side=True,
                                        lower=True, unit_diagonal=True)
    u = t_inv @ (v * beta[..., None])
    w = t_inv @ (kb * jnp.exp(g)[..., None])
    attn = jnp.einsum("bhnid,bhnjd->bhnij", q, k) * decay
    qg = q * jnp.exp(g)[..., None]
    g_last = g[..., -1]
    kd = k * jnp.exp(g_last[..., None] - g)[..., None]

    def step(s, inp):
        u_i, w_i, qg_i, kd_i, attn_i, gl_i = inp
        v_new = u_i - jnp.einsum("bhcd,bhde->bhce", w_i, s)
        o_i = jnp.einsum("bhcd,bhde->bhce", qg_i, s) + jnp.einsum("bhij,bhje->bhie", attn_i, v_new)
        s = s * jnp.exp(gl_i)[..., None, None] + jnp.einsum("bhcd,bhce->bhde", kd_i, v_new)
        return s, o_i

    xs = tuple(jnp.moveaxis(t, 2, 0) for t in (u, w, qg, kd, attn, g_last))
    s_final, o = lax.scan(step, s0, xs)
    o = jnp.transpose(o, (1, 0, 3, 2, 4)).reshape(bsz, length, heads, dv)
    return o, s_final

def deltanet_prep(p_qkv, p_ba, conv_fn, conv_w, a_log, dt_bias):
    qkv = jax.nn.silu(conv_fn(p_qkv, conv_w))
    bsz, length, _ = qkv.shape
    q, k, v = split_cols(qkv, (DN_KEY, DN_KEY, DN_VAL))
    q = l2norm(q.reshape(bsz, length, DN_HEADS, DN_DK)) * (DN_DK ** -0.5)
    k = l2norm(k.reshape(bsz, length, DN_HEADS, DN_DK))
    v = v.reshape(bsz, length, DN_HEADS, DN_DV)
    ba = p_ba.astype(jnp.float32)
    beta = jax.nn.sigmoid(ba[..., :2 * DN_HEADS]).reshape(bsz, length, 2, DN_HEADS)
    alpha = ba[..., 2 * DN_HEADS:].reshape(bsz, length, 2, DN_HEADS)
    g = -jnp.exp(a_log.astype(jnp.float32)) * jax.nn.softplus(alpha + dt_bias.astype(jnp.float32))
    return q, k, v, beta, g

def bidir_gated_delta(dn_ctx, dn_lat):
    qc, kc, vc, bc, gc = dn_ctx
    ql, kl, vl, bl, gl = dn_lat
    s0 = jnp.zeros((qc.shape[0], DN_HEADS, DN_DK, DN_DV), jnp.float32)
    outs_c = []
    outs_l = []
    for d in range(2):
        rev = (lambda t: jnp.flip(t, axis=1)) if d == 1 else (lambda t: t)
        oc, s_ctx = gated_delta_chunked(rev(qc), rev(kc), rev(vc), rev(bc[:, :, d]), rev(gc[:, :, d]), s0)
        ol, _ = gated_delta_chunked(rev(ql), rev(kl), rev(vl), rev(bl[:, :, d]), rev(gl[:, :, d]), s_ctx)
        outs_c.append(rev(oc))
        outs_l.append(rev(ol))
    return (outs_c[0] + outs_c[1]).astype(vc.dtype), (outs_l[0] + outs_l[1]).astype(vl.dtype)

def fourier_mix(u):
    bsz, length, _ = u.shape
    uf = u.astype(jnp.float32).reshape(bsz, length, FN_GROUPS, FN_GROUP_DIM)
    y = jnp.fft.fftn(uf, axes=(1, 3), norm="ortho").real
    return y.reshape(bsz, length, FN_WIDTH).astype(u.dtype)

def branch_merge(h, o_dn, z, sc_p, fn_u, conv_fn, onorm_g, sc_conv_w, w_dn_out, w_sc_out, w_fn_out,
                 w_gate, b_gate, w_o):
    bsz, length, _ = h.shape
    zf = jax.nn.silu(z.reshape(bsz, length, DN_HEADS, DN_DV))
    y_dn = (rmsnorm_2(o_dn, onorm_g) * zf).reshape(bsz, length, DN_VAL) @ w_dn_out
    sb, scc, sx = split_cols(sc_p, (SC_WIDTH, SC_WIDTH, SC_WIDTH))
    y_sc = (sb * conv_fn(scc * sx, sc_conv_w)) @ w_sc_out
    y_fn = fourier_mix(fn_u) @ w_fn_out
    gates = jax.nn.sigmoid((h @ w_gate + b_gate).astype(jnp.float32)).astype(h.dtype)
    gates = gates.reshape(bsz, length, N_BRANCH, D_MODEL)
    merged = gates[:, :, 0] * y_dn + gates[:, :, 1] * y_sc + gates[:, :, 2] * y_fn
    return merged @ w_o

def swiglu(h, w_ffn_in, w_ffn_out):
    a, b = split_cols(h @ w_ffn_in, (D_FF_2, D_FF_2))
    return (jax.nn.silu(a) * b) @ w_ffn_out

def second_inputs(seed: int = 0) -> dict:
    key = jax.random.key(seed)
    ks = jax.random.split(key, 24)
    f32 = jnp.float32

    def nrm(k, shape, fan_in, s=1.0):
        return jax.random.normal(k, shape, f32) * (s * fan_in ** -0.5)

    def gain(k, shape):
        return 1.0 + 0.02 * jax.random.normal(k, shape, f32)

    dt = jnp.exp(jax.random.uniform(ks[10], (DEPTH_2, 2, DN_HEADS), f32, math.log(1e-3), math.log(1e-1)))
    return {
        "x": jax.random.normal(ks[0], (BATCH, SEQ, D_MODEL), f32),
        "c": jax.random.normal(ks[1], (BATCH, D_MODEL), f32),
        "ctx": jax.random.normal(ks[2], (BATCH, CTX_LEN, D_MODEL), f32),
        "c_ctx": jax.random.normal(ks[3], (D_MODEL,), f32),
        "w_mod": nrm(ks[4], (DEPTH_2, D_MODEL, 6 * D_MODEL), D_MODEL, 0.5),
        "b_mod": 0.02 * jax.random.normal(ks[5], (DEPTH_2, 6 * D_MODEL), f32),
        "norm1_g": gain(ks[6], (DEPTH_2, D_MODEL)),
        "w_in": nrm(ks[7], (DEPTH_2, D_MODEL, N_IN), D_MODEL),
        "dn_conv_w": nrm(ks[8], (DEPTH_2, DN_CONV, 2 * DN_KEY + DN_VAL), DN_CONV),
        "dn_a_log": jnp.log(jax.random.uniform(ks[9], (DEPTH_2, 2, DN_HEADS), f32, 1.0, 16.0)),
        "dn_dt_bias": jnp.log(jnp.expm1(dt)),
        "dn_onorm_g": gain(ks[11], (DEPTH_2, DN_DV)),
        "w_dn_out": nrm(ks[12], (DEPTH_2, DN_VAL, D_MODEL), DN_VAL),
        "sc_conv_w": nrm(ks[13], (DEPTH_2, SC_CONV, SC_WIDTH), SC_CONV),
        "w_sc_out": nrm(ks[14], (DEPTH_2, SC_WIDTH, D_MODEL), SC_WIDTH),
        "w_fn_out": nrm(ks[15], (DEPTH_2, FN_WIDTH, D_MODEL), FN_WIDTH),
        "w_gate": nrm(ks[16], (DEPTH_2, D_MODEL, N_BRANCH * D_MODEL), D_MODEL),
        "b_gate": 0.02 * jax.random.normal(ks[17], (DEPTH_2, N_BRANCH * D_MODEL), f32),
        "w_o": nrm(ks[18], (DEPTH_2, D_MODEL, D_MODEL), D_MODEL),
        "norm2_g": gain(ks[19], (DEPTH_2, D_MODEL)),
        "w_ffn_in": nrm(ks[20], (DEPTH_2, D_MODEL, 2 * D_FF_2), D_MODEL),
        "w_ffn_out": nrm(ks[21], (DEPTH_2, D_FF_2, D_MODEL), D_FF_2),
        "final_g": gain(ks[22], (D_MODEL,)),
    }

def second_block(x, c, ctx, c_ctx, w_mod, b_mod, norm1_g, w_in, dn_conv_w, dn_a_log, dn_dt_bias,
              dn_onorm_g, w_dn_out, sc_conv_w, w_sc_out, w_fn_out, w_gate, b_gate, w_o, norm2_g,
              w_ffn_in, w_ffn_out, final_g):
    xc = ctx
    for layer in range(DEPTH_2):
        last = layer == DEPTH_2 - 1
        mod = jax.nn.silu(c) @ w_mod[layer] + b_mod[layer]
        sh1, sc1, g1, sh2, sc2, g2 = jnp.split(mod[:, None, :], 6, axis=-1)
        mod_c = jax.nn.silu(c_ctx) @ w_mod[layer] + b_mod[layer]
        csh1, csc1, cg1, csh2, csc2, cg2 = jnp.split(mod_c, 6)

        h = modulate(x, norm1_g[layer], sh1, sc1)
        hc = modulate(xc, norm1_g[layer], csh1, csc1)
        qkv, z, ba, sc_p, fn_u = split_cols(h @ w_in[layer], IN_SIZES)
        qkv_c, z_c, ba_c, sc_pc, fn_uc = split_cols(hc @ w_in[layer], IN_SIZES)
        dn_lat = deltanet_prep(qkv, ba, conv_grid_rows, dn_conv_w[layer], dn_a_log[layer], dn_dt_bias[layer])
        dn_ctx = deltanet_prep(qkv_c, ba_c, conv_seq, dn_conv_w[layer], dn_a_log[layer], dn_dt_bias[layer])
        o_ctx, o_lat = bidir_gated_delta(dn_ctx, dn_lat)
        mix = branch_merge(h, o_lat, z, sc_p, fn_u, conv_grid_rows, dn_onorm_g[layer], sc_conv_w[layer],
                           w_dn_out[layer], w_sc_out[layer], w_fn_out[layer], w_gate[layer],
                           b_gate[layer], w_o[layer])
        x = x + g1 * mix
        if not last:
            mix_c = branch_merge(hc, o_ctx, z_c, sc_pc, fn_uc, conv_seq, dn_onorm_g[layer],
                                 sc_conv_w[layer], w_dn_out[layer], w_sc_out[layer], w_fn_out[layer],
                                 w_gate[layer], b_gate[layer], w_o[layer])
            xc = xc + cg1 * mix_c
            xc = xc + cg2 * swiglu(modulate(xc, norm2_g[layer], csh2, csc2), w_ffn_in[layer], w_ffn_out[layer])

        x = x + g2 * swiglu(modulate(x, norm2_g[layer], sh2, sc2), w_ffn_in[layer], w_ffn_out[layer])
    return rmsnorm_2(x, final_g)


def setup_inputs(seed=0):
    out = dict(first_inputs(seed))
    for name, value in second_inputs(seed + 1).items():
        if name != "x":
            out[name + "_2"] = value
    return out


def reference(
    x, p, positions, norm1, w_in, pool_w, pool_scale, w_out, norm2, w_up, w_down, norm3, w_gate,
    w_ple, final_norm, c_2, ctx_2, c_ctx_2, w_mod_2, b_mod_2, norm1_g_2, w_in_2, dn_conv_w_2,
    dn_a_log_2, dn_dt_bias_2, dn_onorm_g_2, w_dn_out_2, sc_conv_w_2, w_sc_out_2, w_fn_out_2,
    w_gate_2, b_gate_2, w_o_2, norm2_g_2, w_ffn_in_2, w_ffn_out_2, final_g_2,
):
    x = first_block(
        x, p, positions, norm1, w_in, pool_w, pool_scale, w_out, norm2, w_up, w_down, norm3,
        w_gate, w_ple, final_norm,
    )
    return second_block(
        x, c_2, ctx_2, c_ctx_2, w_mod_2, b_mod_2, norm1_g_2, w_in_2, dn_conv_w_2, dn_a_log_2,
        dn_dt_bias_2, dn_onorm_g_2, w_dn_out_2, sc_conv_w_2, w_sc_out_2, w_fn_out_2, w_gate_2,
        b_gate_2, w_o_2, norm2_g_2, w_ffn_in_2, w_ffn_out_2, final_g_2,
    )


_drawn_inputs = setup_inputs


def setup_inputs(seed=0):
    import zlib

    import numpy as np

    out = dict(_drawn_inputs(seed))
    spreads = {}
    factors = {'norm1': 4.89,
     'pool_scale': 5.317,
     'norm3': 200.0,
     'ctx_2': 34.408,
     'c_ctx_2': 52.512,
     'norm1_g_2': 6.743,
     'dn_onorm_g_2': 178.795,
     'b_gate_2': 8.0,
     'norm2_g_2': 64.0,
     'final_g_2': 28.112,
     'norm2': 7.203,
     'dn_a_log_2': 3.393,
     'dn_dt_bias_2': 3.375,
     'w_fn_out_2': 3.956}
    for name, (base, spread) in spreads.items():
        noise = np.random.default_rng([zlib.crc32(name.encode()), seed]).standard_normal(out[name].shape)
        drawn = base * np.exp(spread * noise) if base else spread * noise
        out[name] = jnp.asarray(drawn.astype(out[name].dtype))
    for name, factor in factors.items():
        out[name] = (out[name] * factor).astype(out[name].dtype)
    return out
```

```python
from contextlib import ExitStack

import numpy as np

import concourse.bass as bass
from concourse import mybir

F32 = mybir.dt.float32
F32R = mybir.dt.float32r
I32 = mybir.dt.int32
ALU = mybir.AluOpType
ACT = mybir.ActivationFunctionType
AX = mybir.AxisListType

P = 128
T = 256
TT = T // P
D = 1024
KT = D // P
DEPTH = 2
HEAD = 64
GROUPS = ((128, 1), (512, 4), (2048, 16))
HPG = 4
POOL_WINDOWS = (2, 4, 8, 16)
ROT = HEAD // 4
THETA = 500000.0
FF = 4096
FF2 = 2816
DN_H = 4
GRID_W = 64
EPS = 1e-6
BIG = 1e30
LEVELS = 7
QSCALE = HEAD ** -0.5
TWO_PI = 2.0 * np.pi
MAGIC = 1.5 * 2.0 ** 23
PI_A = 6.28125
PI_B = 0.0019350051879882812
PI_C = float(TWO_PI - PI_A - PI_B)

RAW = 4
PIECES = 4
CH = 2048
PW = CH // 2

MOD_CHUNKS = 6 * D // 256
MOD_FIRST = 2 * D // 256
CTX_CHUNKS = 4
LAYER_CHUNKS = 52
UPS = FF // 256


def const_columns():
    at, out = 0, {}
    for name, width in (
        ("ident", P), ("ones", P), ("rot", P), ("eps", 1), ("ln_q", 1), ("inv_freq", 1), ("pad", 1),
        ("mask", 3 * 384), ("inv_cnt", 2 * T),
        ("cum0", P), ("cum1", P), ("up0", P), ("up1", P), ("lo0", P), ("lo1", P),
        ("pair0", P), ("pair1", P), ("lvl0", 64 * (LEVELS - 1)), ("lvl1", 64 * (LEVELS - 1)),
        ("dft_cos", 2 * T), ("dft_nsin", 2 * T), ("dft_ch", 2 * P),
    ):
        out[name] = (at, width)
        at += width
    return out, at


def level_columns(d, l):
    f = np.arange(P)
    return f[(f >> l & 1) == (1 - d)]


def const_tables():
    cols, total = const_columns()
    a = np.zeros((P, total), np.float64)

    def put(name, v):
        s, w = cols[name]
        a[:, s:s + w] = v

    p = np.arange(P)[:, None]
    f = np.arange(P)[None, :]
    put("ident", p == f)
    put("ones", 1.0)
    rot = np.zeros((P, P))
    half = ROT // 2
    inv = np.zeros((P, 1))
    for m in range(P):
        d = m % HEAD
        if d < half:
            rot[m + half, m] = -1.0
        elif d < ROT:
            rot[m - half, m] = 1.0
        if d < ROT:
            inv[m, 0] = np.float32(THETA) ** np.float32(-2.0 * (d % half) / ROT)
    put("rot", rot)
    put("inv_freq", inv)
    put("eps", EPS)
    put("ln_q", np.log(P ** -0.5))
    mask = np.zeros((P, 3, 384))
    for g, (window, dil) in enumerate(GROUPS):
        for qt in range(TT):
            k = np.arange(P * (qt + 1))[None, :]
            dist = p + P * qt - k
            ok = (dist >= 0) & (dist % dil == 0) & (dist // dil <= window // dil)
            mask[:, g, P * qt:P * qt + k.size] = np.where(ok, 0.0, -BIG)
    put("mask", mask.reshape(P, -1))
    t = np.arange(T)
    cnt = np.zeros((P, 2, T))
    for i in range(2):
        for h in range(2):
            cnt[HEAD * h:HEAD * (h + 1), i] = 1.0 / np.minimum(t + 1, POOL_WINDOWS[2 * i + h])
    put("inv_cnt", cnt.reshape(P, -1))
    put("cum0", p <= f)
    put("cum1", p >= f)
    put("up0", np.where(f >= p, BIG, -BIG))
    put("up1", np.where(f <= p, BIG, -BIG))
    put("lo0", np.where(f < p, -BIG, BIG))
    put("lo1", np.where(f > p, -BIG, BIG))
    put("pair0", (p % 2 == 1) & (f == p - 1))
    put("pair1", (p % 2 == 0) & (f == p + 1))
    for d in range(2):
        lv = np.zeros((P, LEVELS - 1, 64))
        for l in range(1, LEVELS):
            c = level_columns(d, l)[None, :]
            lv[:, l - 1] = (p >> (l + 1) == c >> (l + 1)) & ((p >> l & 1) == d)
        put(f"lvl{d}", lv.reshape(P, -1))
    tt = np.arange(TT)[None, :, None] * P + np.arange(P)[:, None, None]
    ang = TWO_PI * ((tt * t[None, None, :]) % T) / T
    put("dft_cos", (np.cos(ang) / np.sqrt(T)).reshape(P, -1))
    put("dft_nsin", (-np.sin(ang) / np.sqrt(T)).reshape(P, -1))
    ang = TWO_PI * ((p * f) % P) / P
    put("dft_ch", np.concatenate([np.cos(ang), np.sin(ang)], 1) / np.sqrt(P))
    return a.astype(np.float32)


LAYER_VECS = (("norm1", KT), ("norm2", KT), ("norm3", KT), ("pool_scale", 2))
LV = sum(n for _, n in LAYER_VECS)
TILE_A = (("final_norm", KT), ("norm1_g_2", KT), ("norm2_g_2", KT), ("final_g_2", KT),
          ("b_gate_2", 24), ("c_2", KT), ("c_ctx_2", KT))
TILE_B = (("b_mod_2", 48), ("dn_conv_w_2", 36), ("sc_conv_w_2", 12), ("dn_onorm_g_2", 1))


def vec_columns():
    out, at = {}, DEPTH * LV
    for name, n in TILE_A:
        out[name] = at
        at += n
    rows_a = at
    for name, n in TILE_B:
        out[name] = at
        at += n
    return out, rows_a, at


Q2, K2, V2, Z2, BA2, SB2, SC2, SX2, FN2 = 0, 512, 1024, 1536, 2048, 2064, 2576, 3088, 3600


CTX_TOLD = dict(act=8, conv1=8, conv=4, silu=4, ba=1, ba2=1, sq=2, kn=2, rs=2, g=1, gcol=1, ecol=1, bcol=1, tok=1, tg=4,
                dl=4, el=4, T=4, X0=4, X=4 * LEVELS, Z=4 * (LEVELS - 1), T2=4 * (LEVELS - 2), vb=4, kd=4, uw=4, vnew=2,
                state=4, hi=8, mt=8)


class Banks:

    def __init__(self, full, free):
        self.full, self.free = full, free
        self.uses, self.fulls, self.per = {}, {}, {}
        self.n_use = [0] * 8
        self.n_full = [0] * 8

    def section(self, name, uses, times=1):
        start_u, start_f = list(self.n_use), list(self.n_full)
        for use, bank, own in uses:
            assert (name, use) not in self.uses, use
            self.uses[name, use] = (bank, self.n_use[bank])
            self.fulls[name, use] = (bank, self.n_full[bank] + 1)
            self.n_use[bank] += 1
            self.n_full[bank] += own
        per_u = [b - a for a, b in zip(start_u, self.n_use)]
        per_f = [b - a for a, b in zip(start_f, self.n_full)]
        self.per[name] = (per_u, per_f)
        if times > 1:
            assert all(n > 0 for n in start_u)
            self.n_use = [b + p * (times - 1) for b, p in zip(self.n_use, per_u)]
            self.n_full = [b + p * (times - 1) for b, p in zip(self.n_full, per_f)]

    def bank(self, sec, use):
        return self.uses[sec, use][0]

    def claim(self, eng, sec, use, layer=0):
        b, n = self.uses[sec, use]
        v = n + layer * self.per[sec][0][b]
        if not (isinstance(v, int) and v == 0):
            eng.wait_ge(self.free[b], v)
        return b

    def wait_full(self, eng, sec, use, layer=0):
        b, n = self.fulls[sec, use]
        eng.wait_ge(self.full[b], n + layer * self.per[sec][1][b])
        return b


def bank_schedule(banks):

    def ring(order):
        n = [0]

        def take():
            n[0] += 1
            return order[(n[0] - 1) % len(order)]
        return take

    uses = []
    r = ring([0, 1, 2, 4, 5, 6, 7])
    own = lambda name: uses.append((name, r(), 1))
    lin = lambda name: uses.append((name, r(), 0))
    uses.append(("mod", 3, 0))
    own("vec")
    for c in range(4):
        own(f"x{c}")
    for c in range(4):
        own(f"ctx{c}")
    own("rows")
    own("norm")
    delta_uses("ctx", own, lin)
    banks.section("pre", uses)

    uses = []
    low, high = ring([0, 1, 2, 3]), ring([4, 5, 6, 7])
    own = lambda name: uses.append((name, low(), 1))
    lin = lambda name: uses.append((name, high(), 0))
    lin("qk0")
    own("ssq1")
    own("p")
    for s in range(1, 7):
        lin(f"qk{s}" if s < 6 else "v0")
        own(f"rot{s - 1}")
    for i in range(6):
        own(f"s{heads(0)[i]}")
    lin("v1")
    for i in range(6):
        own(f"s{heads(1)[i]}")
    lin("v2")
    lin("u")
    for kind, x in ATT:
        own({"T": f"pT{x}", "V": f"pv{x}", "pool": "pool"}[kind])
    for c in range(4):
        lin(f"out{c}")
    lin("up0")
    lin("up1")
    uses.append(("ssq2", high(), 1))
    for b in range(4):
        uses.append((f"down{b}", b, 0))
    for j in range(2, UPS):
        lin(f"up{j}")
    for b in range(4):
        uses.append((f"ple{b}", 4 + b, 0))
    for b in range(4):
        if b == 2:
            uses.append(("ssq3", 3, 1))
        uses.append((f"gate{b}", b, 0))
    banks.section("layer", uses, DEPTH)

    uses = []
    r = ring(range(8))
    own = lambda name: uses.append((name, r(), 1))
    lin = lambda name: uses.append((name, r(), 0))
    own("final")
    own("norm1")
    delta_uses("lat", own, lin)
    own("onorm0")
    own("onorm1")
    for c in range(6):
        lin(f"sc{c}")
    for c in range(2):
        lin(f"fn{c}")
    for g in range(4):
        for t in range(TT):
            own(f"fch{g}{t}")
    for c in range(2):
        own(f"fpos{c}")
    for b in range(3):
        for c in range(4):
            lin(f"gate{b}{c}")
        for c in range(4):
            lin(f"y{b}{c}")
    for c in range(4):
        lin(f"wo{c}")
    own("norm2")
    low, high = ring([0, 1, 2, 3]), ring([4, 5, 6, 7])
    for b in range(4):
        uses.append((f"ffo{b}", b, 0))
    for j in range(FF2 // 256):
        for n in "ab":
            uses.append((f"ff{n}{j}", high(), 0))
    uses.append(("final2", 4, 1))
    for c in range(4):
        own(f"y_out{c}")
    banks.section("post", uses)


def delta_uses(part, own, lin):
    lat = part == "lat"
    for c in range(2 if lat else 0):
        lin("lat_q%d" % c)
    for c in range(2):
        lin(f"{part}_k{c}")
    for c in range(2):
        lin(f"{part}_v{c}")
    own(f"{part}_ba")
    if lat:
        for c in range(2):
            lin(f"lat_z{c}")
    for c in range(4 if lat else 2):
        own(f"{part}_l2{c}")
    own(f"{part}_cum")
    for n in range(TT):
        own(f"{part}_kt{n}")
        own(f"{part}_vt{n}")
    for g in range(4):
        own(f"{part}_grow{g}")
        own(f"{part}_kk{g}")
        if lat:
            own(f"lat_qk{g}")
    for g in range(4):
        own(f"{part}_x0{g}")
    for l in range(1, LEVELS):
        for g in range(4):
            own(f"{part}_z{l}{g}")
        for g in range(4):
            own(f"{part}_xz{l}{g}")
        if l < LEVELS - 1:
            for g in range(4):
                own(f"{part}_t{l}{g}")
    for g in range(4):
        own(f"{part}_u{g}")
        if lat or g in (1, 2):
            own(f"{part}_w{g}")
    for step in range(2):
        for d in range(2):
            if lat or step == 1:
                own(f"{part}_ws{step}{d}")
        for d in range(2):
            if lat:
                own(f"lat_o{step}{d}")
            if step == 0 or not lat:
                own(f"{part}_s{step}{d}")


def heads(b):
    return [HPG * g + 2 * b + i for g in range(3) for i in range(2)]


def attention_order():
    pairs = [(b, g) for b in range(2) for g in range(3)]
    out = []
    for i, (b, g) in enumerate(pairs):
        out += [("T", HPG * g + 2 * b), ("T", HPG * g + 2 * b + 1)]
        if i:
            out.append(("V", 2 * pairs[i - 1][1] + pairs[i - 1][0]))
        if i == 1:
            out.append(("pool", 0))
    return out + [("V", 2 * g + b)]


ATT = attention_order()
T_ORDER = [x for k, x in ATT if k == "T"]
V_ORDER = [x for k, x in ATT if k == "V"]


def group_of(d, step):
    return 2 * d + (step if d == 0 else 1 - step)


def two_blocks(nc, a, out):
    K, NK = const_columns()
    V, ROWS_A, NV = vec_columns()
    with ExitStack() as ctx:
        def sb(name, shape, dt=F32):
            return ctx.enter_context(nc.sbuf_tensor(name, shape, dt))

        sems = {}

        def S(name):
            if name not in sems:
                sems[name] = ctx.enter_context(nc.semaphore(name))
            return sems[name]

        kt = sb("consts_sb", [P, NK])
        vec = sb("vec_cols", [P, NV])
        raw = sb("w_raw", [P, RAW, CH])
        whi = sb("w_hi", [P, PIECES, PW], F32R)
        wlo = sb("w_lo", [P, PIECES, PW], F32R)
        xhi = sb("act_hi", [P, KT, T], F32R)
        xlo = sb("act_lo", [P, KT, T], F32R)
        yhi = sb("side_hi", [P, 4, T], F32R)
        ylo = sb("side_lo", [P, 4, T], F32R)
        phi = sb("ple_hi", [P, 2, T], F32R)
        plo = sb("ple_lo", [P, 2, T], F32R)
        ba_hi = sb("w_ba_hi", [P, KT, 16], F32R)
        ba_lo = sb("w_ba_lo", [P, KT, 16], F32R)
        h = sb("h", [P, KT, T])
        rope_c = sb("rope_cos", [P, T])
        rope_s = sb("rope_sin", [P, T])
        state = sb("state", [P, 2, DN_H, P])
        modc = sb("mod_cols", [P, 48, 2])
        gains = sb("mod_gains", [P, 3, KT])
        dn_rows = sb("dn_rows", [P, 16])
        neg_a = sb("neg_exp_a", [P, 8])
        cur_vec = sb("layer_vecs", [P, LV])
        rstd_w = sb("rstd", [P, T + 4])
        rstd = rstd_w[:, 0:T]
        rstd_b = sb("rstd_b", [P, 2 * T])
        ARENA = 22400
        arena = sb("arena", [P, ARENA])
        ps = [ctx.enter_context(nc.psum_tensor(f"bank{b}", [P, 512], F32)) for b in range(8)]

        class Arena:

            def __init__(self, at=0):
                self.at = at

            def __call__(self, *shape):
                n = int(np.prod(shape))
                v = arena[:, self.at:self.at + n]
                self.at += n
                assert self.at <= ARENA, self.at
                if len(shape) == 2:
                    v = v.rearrange("p (a b) -> p a b", a=shape[0])
                elif len(shape) == 3:
                    v = v.rearrange("p (a b c) -> p a b c", a=shape[0], b=shape[1])
                return v

        def col(name, i=0, n=1):
            s = K[name][0] + i
            return kt[:, s:s + n]

        def vcol(name, i=0):
            return vec[:, V[name] + i:V[name] + i + 1]

        ident, ones = col("ident", 0, P), col("ones", 0, P)
        eps_col, lnq_col = col("eps"), col("ln_q")

        A = Arena()
        small = A(1280)
        pre_x = A(KT, T)
        sil = A(12, T)
        q_n, k_n, v_n = sil[:, 0:4, :], sil[:, 4:8, :], sil[:, 8:12, :]
        ktok = A(TT, DN_H, P)
        vtok = A(TT, DN_H, P)
        z_n = A(4, T)
        g_A = A(4, 512)
        g_X = A(4, 512)
        g_T = A(4, 512)
        g_dec = A(4, 512)
        g_q = A(4, 512)
        scr = [A(512) for _ in range(3)]
        DELTA_END = A.at
        g_kd = pre_x.rearrange("p a b -> p (a b)").rearrange("p (g n) -> p g n", g=4)
        xtok = g_A.rearrange("p a b -> p (a b)").rearrange("p (t d) -> p t d", t=2)
        ctok = g_X.rearrange("p a b -> p (a b)").rearrange("p (t d) -> p t d", t=2)
        xc = g_T.rearrange("p a b -> p (a b)").rearrange("p (k t) -> p k t", k=KT)

        S("landed0"), S("landed1"), S("landed2"), S("landed3")
        landed = [S(f"landed{i}") for i in range(RAW)]
        hi_ready, lo_ready, pieces_done, mod_done = S("hi_ready"), S("lo_ready"), S("pieces_done"), S("mod_done")
        banks = Banks([S(f"bank_full{b}") for b in range(8)], [S(f"bank_free{b}") for b in range(8)])
        bank_schedule(banks)
        block = ctx.enter_context(nc.Block())

        def k_all(w, c, n=256):
            return w[:, c:c + n].rearrange("(k p) n -> p k n", p=P)

        def k_rows(w, r, c=0, n=D):
            return w[r:r + 256, c:c + n].rearrange("(k p) n -> p k n", p=P)

        w_in2 = a["w_in_2"][0]
        mod_src = [k_all(a["w_mod_2"][0], 256 * m) for m in range(MOD_CHUNKS)]
        ctx_src = [k_all(w_in2, c) for c in (K2, K2 + 256, V2, V2 + 256)]

        def layer_src(layer):
            w_in, w_out = a["w_in"][layer], a["w_out"][layer]
            w_up, w_down = a["w_up"][layer], a["w_down"][layer]
            src = []
            for g in range(3):
                src += [k_all(w_in, 256 + 768 + 256 * g), k_all(w_in, 256 + 256 * g)]
            src += [k_all(w_in, 256 + 1536 + 256 * g) for g in range(3)]
            src += [k_all(w_in, 0)]
            src += [k_all(w_out, 256 * c) for c in range(4)]
            up = [k_all(w_up, 256 * j) for j in range(UPS)]
            down = [k_rows(w_down, 256 * j) for j in range(UPS)]
            src += up[0:2]
            for j in range(UPS):
                src += [down[j]] + up[j + 2:j + 3]
            src += [k_all(a["w_ple"][layer], 512 * c, 512) for c in range(2)]
            src += [k_all(a["w_gate"][layer], 256 * c) for c in range(4)]
            assert len(src) == LAYER_CHUNKS
            return src

        post_src = [k_all(w_in2, c) for c in (0, 256, K2, K2 + 256, V2, V2 + 256, Z2, Z2 + 256)]
        post_src += [k_all(w_in2, c + e) for c in (SB2, SC2, SX2, FN2) for e in (0, 256)]
        for b, name in ((2, "w_fn_out_2"), (1, "w_sc_out_2"), (0, "w_dn_out_2")):
            post_src += [k_all(a["w_gate_2"][0], D * b + 256 * c) for c in range(4)]
            post_src += [k_all(a[name][0], 512 * c, 512) for c in range(2)]
        post_src += [k_all(a["w_o_2"][0], 256 * c) for c in range(4)]
        ffn = []
        for j in range(FF2 // 256):
            ffn += [k_all(a["w_ffn_in_2"][0], 256 * j), k_all(a["w_ffn_in_2"][0], FF2 + 256 * j)]
            if j:
                ffn += [k_rows(a["w_ffn_out_2"][0], 256 * (j - 1))]
        ffn += [k_rows(a["w_ffn_out_2"][0], FF2 - 256)]
        post_src += ffn
        C_LAYER, S_LAYER = MOD_CHUNKS + CTX_CHUNKS, CTX_CHUNKS
        C_POST, S_POST = C_LAYER + DEPTH * LAYER_CHUNKS, S_LAYER + DEPTH * LAYER_CHUNKS
        POST_CHUNKS = len(post_src)
        assert C_LAYER % RAW == S_LAYER % 2 == LAYER_CHUNKS % RAW == 0
        S_END = S_POST + POST_CHUNKS

        def half_chunk(local):
            return local in (46, 47)

        class Where:

            def __init__(self, s0, c0, layer=0, per=0, sec="pre"):
                self.s0, self.c0, self.layer, self.per, self.sec = s0, c0, layer, per, sec

            def split(self, l):
                return self.layer * self.per + self.s0 + l

            def pieces(self, l, half=0):
                return self.layer * (2 * self.per) + 2 * (self.s0 + l) + half + 1

            def loads(self, l):
                return self.layer * (16 * self.per // RAW) + 16 * ((self.c0 + l) // RAW + 1)

            def nth(self, n, per):
                return self.layer * per + n

        def width(w, l):
            return PW // 2 if w.sec == "layer" and half_chunk(l) else PW

        def split_hi(act, w, l):
            n = width(w, l)
            for half in range(2):
                slot = (2 * l + half) % PIECES
                if half == 0:
                    act.wait_ge(landed[l % RAW], w.loads(l))
                v = w.pieces(l, half) - PIECES
                if not isinstance(v, int) or v > 0:
                    act.wait_ge(pieces_done, v)
                nc.scalar.activation(whi[:, slot, 0:n], raw[:, l % RAW, n * half:n * (half + 1)],
                                     ACT.Copy).then_inc(hi_ready, 1)

        def split_lo(dve, w, l):
            n = width(w, l)
            for half in range(2):
                slot = (2 * l + half) % PIECES
                dve.wait_ge(hi_ready, w.pieces(l, half))
                nc.vector.tensor_tensor(wlo[:, slot, 0:n], raw[:, l % RAW, n * half:n * (half + 1)],
                                        whi[:, slot, 0:n].bitcast(F32), ALU.subtract).then_inc(lo_ready, 1)

        def three(pe, o, ahi, alo, bhi, blo, start, stop=False):
            nc.tensor.matmul(o, ahi, bhi, start=start, stop=False, skip_group_check=True)
            nc.tensor.matmul(o, ahi, blo, start=False, stop=False, skip_group_check=True)
            return nc.tensor.matmul(o, alo, bhi, start=False, stop=stop, skip_group_check=True)

        def project(pe, w, l, out_tile, kts, act_hi, act_lo, wait_act=None, first=True, last=True):
            n = width(w, l)
            kp = max(kts // 2, 1)
            ms = n // kp // P
            for half in range(2):
                slot = (2 * l + half) % PIECES
                pe.wait_ge(lo_ready, w.pieces(l, half))
                for m in range(ms):
                    bank, c = out_tile(m)
                    o = ps[bank][:, c:c + T]
                    for k in range(kp):
                        f = half * kp + k
                        if wait_act and m == 0:
                            wait_act(f)
                        at = k * ms * P + m * P
                        mm = three(pe, o, whi[:, slot, at:at + P], wlo[:, slot, at:at + P],
                                   act_hi[:, f, :], act_lo[:, f, :],
                                   start=first and half == 0 and k == 0 and c == 0,
                                   stop=last and half == 1 and k == kp - 1)
                mm.then_inc(pieces_done, 1)

        def project_tokens(pe, w, l, bank):
            for half in range(2):
                slot = (2 * l + half) % PIECES
                pe.wait_ge(lo_ready, w.pieces(l, half))
                for t in range(TT):
                    o = ps[bank][:, T * t:T * (t + 1)]
                    for k in range(4):
                        f = 4 * half + k
                        mm = three(pe, o, xhi[:, f, P * t:P * (t + 1)], xlo[:, f, P * t:P * (t + 1)],
                                   whi[:, slot, 256 * k:256 * (k + 1)], wlo[:, slot, 256 * k:256 * (k + 1)],
                                   start=half == 0 and k == 0 and t == 0, stop=half == 1 and k == 3)
                mm.then_inc(pieces_done, 1)

        def wide(v, n):
            return v.unsqueeze(1).broadcast_to([P, n, T])

        def per_head(v):
            return v.unsqueeze(2).broadcast_to([P, DN_H, P])

        def all_heads(v):
            return v.unsqueeze(1).broadcast_to([P, DN_H, v.shape[1]])

        def h4(v):
            return v.rearrange("p (h n) -> p h n", h=DN_H)

        def pair(b):
            return ps[b][:, :].rearrange("p (m t) -> p m t", m=2)

        sg = small[:, 0:256]
        ba_beta = sg[:, 0:16].rearrange("p (n c) -> p n c", n=2)
        ba_g = sg[:, 16:32].rearrange("p (n c) -> p n c", n=2)
        ba_t1 = sg[:, 32:48].rearrange("p (n c) -> p n c", n=2)
        ba_t2 = sg[:, 48:64].rearrange("p (n c) -> p n c", n=2)
        gcol = sg[:, 64:80].rearrange("p (g c) -> p g c", g=4)
        gtot = sg[:, 80:96].rearrange("p (g c) -> p g c", g=4)
        kd_col = sg[:, 96:112].rearrange("p (g c) -> p g c", g=4)
        bg_col = sg[:, 112:128].rearrange("p (g c) -> p g c", g=4)
        eg_col = sg[:, 128:144].rearrange("p (g c) -> p g c", g=4)
        et_col = sg[:, 144:160].rearrange("p (g c) -> p g c", g=4)
        z_sm = small[:, 256:1280].rearrange("p (g n) -> p g n", g=4)

        def chunk_of(g):
            return g // 2, g % 2

        def beta_of(g):
            d, n = chunk_of(g)
            return ba_beta[:, n, 4 * d:4 * d + 4]

        def lvl_cols(x, d, l):
            v = x.rearrange("p h (n s b) -> p h n s b", s=2, b=1 << l)
            return v[:, :, :, 1 - d, :]

        def lvl_shape(z, l):
            return z.rearrange("p (h n b) -> p h n b", h=DN_H, b=1 << l)

        def tok(x, n):
            return x[:, :, P * n:P * (n + 1)]

        conv = [scr[0], scr[1]]
        conv_names = {"q": 0, "k": 4, "v": 8}
        ctx_tiles = [("k", 0), ("k", 1), ("v", 0), ("v", 1)]
        lat_tiles = [("q", 0), ("q", 1)] + ctx_tiles

        def tiles_of(part):
            return ctx_tiles if part == "ctx" else lat_tiles

        def steps_of(part):
            return 2

        def pe_delta(pe, part, w, l0, sec, between):
            lat = part == "lat"
            told = lambda name, n: (S("dn_" + name), n + (CTX_TOLD[name] if lat else 0))
            W = lambda use: banks.wait_full(pe, sec, f"{part}_{use}")
            C = lambda use: banks.claim(pe, sec, f"{part}_{use}")
            F = lambda mm, b: mm.then_inc(banks.full[b], 1)
            l = l0
            for i, (name, c) in enumerate(tiles_of(part)):
                b = C(f"{name}{c}")
                project(pe, w, l, lambda m: (b, T * m), KT, xhi, xlo,
                        (lambda f: pe.wait_ge(*told("act", f + 1))) if i == 0 else None)
                l += 1
            b = C("ba")
            pe.wait_ge(S("w_ba_split"), 2)
            for t in range(TT):
                for k in range(KT):
                    mm = three(pe, ps[b][:, 16 * t:16 * t + 16], xhi[:, k, P * t:P * (t + 1)],
                               xlo[:, k, P * t:P * (t + 1)], ba_hi[:, k, :], ba_lo[:, k, :],
                               start=k == 0, stop=k == KT - 1)
            F(mm, b)
            if lat:
                for c in range(2):
                    b = C(f"z{c}")
                    project(pe, w, l, lambda m: (b, T * m), KT, xhi, xlo)
                    l += 1
            for i in range(4 if lat else 2):
                pe.wait_ge(*told("sq", i + 1))
                b = C(f"l2{i}")
                F(nc.tensor.matmul(ps[b][:, :], ones, scr[i % 2], start=True, stop=True), b)
            between(2)
            pe.wait_ge(*told("g", 1))
            b = C("cum")
            for g in range(4):
                d, n = chunk_of(g)
                gg = ba_g[:, n, 4 * d:4 * d + 4]
                nc.tensor.matmul(ps[b][:, 4 * g:4 * g + 4], col(f"cum{d}", 0, P), gg, start=True, stop=True)
                mm = nc.tensor.matmul(ps[b][:, 16 + 4 * g:20 + 4 * g], ones, gg, start=True, stop=True)
            F(mm, b)
            for n in range(TT):
                pe.wait_ge(*told("kn", 2))
                b = C(f"kt{n}")
                for hh in range(DN_H):
                    mm = nc.tensor.transpose(ps[b][:, P * hh:P * (hh + 1)], k_n[:, hh, P * n:P * (n + 1)], ident)
                F(mm, b)
                b = C(f"vt{n}")
                for hh in range(DN_H):
                    mm = nc.tensor.transpose(ps[b][:, P * hh:P * (hh + 1)], v_n[:, hh, P * n:P * (n + 1)], ident)
                F(mm, b)
            between(2)
            for g in range(4):
                d, n = chunk_of(g)
                pe.wait_ge(*told("tg", g + 1))
                b = C(f"grow{g}")
                F(nc.tensor.matmul(ps[b][:, :], ones, g_X[:, g, :], start=True, stop=True), b)
                b = C(f"kk{g}")
                for hh in range(DN_H):
                    kk = k_n[:, hh, P * n:P * (n + 1)]
                    mm = nc.tensor.matmul(ps[b][:, P * hh:P * (hh + 1)], kk, kk, start=True, stop=True)
                F(mm, b)
                if lat:
                    b = C(f"qk{g}")
                    if g == 0:
                        pe.wait_ge(S("lat_qn"), 2)
                    for hh in range(DN_H):
                        mm = nc.tensor.matmul(ps[b][:, P * hh:P * (hh + 1)], k_n[:, hh, P * n:P * (n + 1)],
                                              q_n[:, hh, P * n:P * (n + 1)], start=True, stop=True)
                    F(mm, b)
                between(1)
            for g in range(4):
                pe.wait_ge(*told("T", g + 1))
                b = C(f"x0{g}")
                for hh in range(DN_H):
                    mm = nc.tensor.transpose(ps[b][:, P * hh:P * (hh + 1)], h4(g_T[:, g, :])[:, hh, :], ident)
                F(mm, b)
            for lv in range(1, LEVELS):
                for g in range(4):
                    d, n = chunk_of(g)
                    pe.wait_ge(*told("X", 4 * (lv - 1) + g + 1))
                    b = C(f"z{lv}{g}")
                    xs = lvl_cols(h4(g_X[:, g, :]), d, lv)
                    for hh in range(DN_H):
                        mm = nc.tensor.matmul(ps[b][:, 64 * hh:64 * (hh + 1)], h4(g_A[:, g, :])[:, hh, :],
                                              xs[:, hh], start=True, stop=True)
                    F(mm, b)
                between(1)
                for g in range(4):
                    pe.wait_ge(*told("Z", 4 * (lv - 1) + g + 1))
                    if lv > 1:
                        pe.wait_ge(*told("T2", 4 * (lv - 2) + g + 1))
                    b = C(f"xz{lv}{g}")
                    for hh in range(DN_H):
                        mm = nc.tensor.matmul(ps[b][:, 64 * hh:64 * (hh + 1)], h4(g_T[:, g, :])[:, hh, :],
                                              z_sm[:, g, 64 * hh:64 * (hh + 1)], start=True, stop=True)
                    F(mm, b)
                if lv < LEVELS - 1:
                    for g in range(4):
                        pe.wait_ge(*told("X", 4 * lv + g + 1))
                        b = C(f"t{lv}{g}")
                        for hh in range(DN_H):
                            mm = nc.tensor.transpose(ps[b][:, P * hh:P * (hh + 1)], h4(g_X[:, g, :])[:, hh, :], ident)
                        F(mm, b)
            for g in range(4):
                pe.wait_ge(*told("X", 4 * (LEVELS - 1) + g + 1))
                pe.wait_ge(*told("vb", g + 1))
                b = C(f"u{g}")
                for hh in range(DN_H):
                    mm = nc.tensor.matmul(ps[b][:, P * hh:P * (hh + 1)], h4(g_X[:, g, :])[:, hh, :],
                                          h4(scr_vb(g))[:, hh, :], start=True, stop=True)
                F(mm, b)
                if lat or g in (1, 2):
                    b = C(f"w{g}")
                    for hh in range(DN_H):
                        mm = nc.tensor.matmul(ps[b][:, P * hh:P * (hh + 1)], h4(scr_kb(g))[:, hh, :],
                                              h4(g_X[:, g, :])[:, hh, :], start=True, stop=True)
                    F(mm, b)
                between(1)
            ns = 0
            for step in range(2):
                for d in range(2):
                    g = group_of(d, step)
                    if lat or step == 1:
                        if step == 1:
                            pe.wait_ge(*told("state", d + 1))
                        elif lat:
                            pe.wait_ge(S("dn_state"), 4)
                        pe.wait_ge(*told("uw", 4))
                        b = C(f"ws{step}{d}")
                        for hh in range(DN_H):
                            mm = nc.tensor.matmul(ps[b][:, P * hh:P * (hh + 1)], h4(g_T[:, g, :])[:, hh, :],
                                                  state[:, d, hh, :], start=True, stop=True)
                        F(mm, b)
                for d in range(2):
                    g = group_of(d, step)
                    vnew = h4(g_A[:, g, :])
                    pe.wait_ge(*told("uw", 4))
                    if lat or step == 1:
                        ns += 1
                        pe.wait_ge(*told("vnew", ns))
                    if lat:
                        if step == 0 and d == 0:
                            pe.wait_ge(S("lat_qg"), 4)
                            pe.wait_ge(S("lat_attn"), 4)
                        b = C(f"o{step}{d}")
                        for hh in range(DN_H):
                            o = ps[b][:, P * hh:P * (hh + 1)]
                            nc.tensor.matmul(o, state[:, d, hh, :], h4(g_q[:, g, :])[:, hh, :], start=True, stop=False)
                            mm = nc.tensor.matmul(o, vnew[:, hh, :], h4(g_dec[:, g, :])[:, hh, :],
                                                  start=False, stop=True)
                        F(mm, b)
                    if step == 0 or not lat:
                        pe.wait_ge(*told("kd", 4))
                        b = C(f"s{step}{d}")
                        for hh in range(DN_H):
                            mm = nc.tensor.matmul(ps[b][:, P * hh:P * (hh + 1)], h4(g_kd[:, g, :])[:, hh, :],
                                                  vnew[:, hh, :], start=True, stop=True)
                        F(mm, b)
            return l

        def scr_vb(g):
            return g_vb[:, g % 2, :]

        def scr_kb(g):
            return g_kb[:, g % 2, :]

        g_vb = sil.rearrange("p a b -> p (a b)")[:, 2048:3072].rearrange("p (g n) -> p g n", g=2)
        g_kb = z_kb = Arena(DELTA_END)(2, 512)

        def act_delta(act, part, w, l0, sec):
            lat = part == "lat"
            told = lambda name, n: (S("dn_" + name), n + (CTX_TOLD[name] if lat else 0))
            W = lambda use: banks.wait_full(act, sec, f"{part}_{use}")
            bank = lambda use: banks.bank(sec, f"{part}_{use}")
            free = lambda ins, b: ins.then_inc(banks.free[b], 1)
            l = l0
            for i, (name, c) in enumerate(tiles_of(part)):
                split_hi(act, w, l + 1) if w.s0 + l + 1 < w.end else None
                b = bank(f"{name}{c}")
                act.wait_ge(pieces_done, w.pieces(l, 1))
                if i >= 2:
                    act.wait_ge(*told("silu", i - 1))
                tile = conv_names[name] + 2 * c
                for m in range(2):
                    nc.scalar.activation(conv[i % 2][:, T * m:T * (m + 1)], ps[b][:, T * m:T * (m + 1)],
                                         ACT.Identity, scale=vcol("dn_conv_w_2", 12 + tile + m)).then_inc(
                                             S("dn_conv1"), 1)
                act.wait_ge(*told("conv", i + 1))
                nc.scalar.activation(sil[:, tile:tile + 2, :], conv[i % 2].rearrange("p (m t) -> p m t", m=2),
                                     ACT.Silu).then_inc(S("dn_silu"), 1)
                l += 1
            if lat:
                for c in range(2):
                    split_hi(act, w, l + 1)
                    act.wait_ge(pieces_done, w.pieces(l, 1))
                    free(nc.scalar.activation(z_n[:, 2 * c:2 * c + 2, :], pair(bank(f"z{c}")), ACT.Silu),
                         bank(f"z{c}"))
                    l += 1
                act.drain().then_inc(S("lat_z"), 1)
            act.wait_ge(*told("ba", 1))
            nc.scalar.activation(ba_t1, ba_t1, ACT.Exp, scale=-1.0)
            nc.scalar.activation(ba_t2, ba_t2, ACT.Exp, scale=-1.0)
            act.drain()
            nc.scalar.activation(ba_t2, ba_t2, ACT.Ln, bias=1.0).then_inc(S("dn_ba2"), 1)
            for i in range(4 if lat else 2):
                b = W(f"l2{i}")
                if i >= 1:
                    act.wait_ge(*(told("kn", i) if not lat else told("kn", i - 2) if i > 2 else (S("lat_qn"), i)))
                free(nc.scalar.activation(rstd_b[:, :], ps[b][:, :], ACT.Ln, bias=eps_col), b)
                act.drain()
                if lat and i < 2:
                    nc.scalar.activation(rstd_b[:, :], rstd_b[:, :], ACT.Exp, scale=-0.5, bias=lnq_col).then_inc(
                        S("dn_rs"), 1)
                else:
                    nc.scalar.activation(rstd_b[:, :], rstd_b[:, :], ACT.Exp, scale=-0.5).then_inc(S("dn_rs"), 1)
            act.wait_ge(*told("gcol", 1))
            nc.scalar.activation(eg_col, gcol, ACT.Exp)
            nc.scalar.activation(kd_col, kd_col, ACT.Exp)
            nc.scalar.activation(et_col, gtot, ACT.Exp)
            act.drain().then_inc(S("dn_ecol"), 1)
            for n in range(TT):
                b = W(f"kt{n}")
                free(nc.scalar.activation(ktok[:, n], h4(ps[b][:, :]), ACT.Copy), b)
                b = W(f"vt{n}")
                free(nc.scalar.activation(vtok[:, n], h4(ps[b][:, :]), ACT.Copy), b)
            act.drain().then_inc(S("dn_tok"), 1)
            for g in range(4):
                if lat:
                    b = W(f"grow{g}")
                    nc.scalar.activation(g_q[:, g, :], ps[b][:, :], ACT.Exp).then_inc(S("lat_egrow"), 1)
                act.wait_ge(*told("dl", g + 1))
                nc.scalar.activation(scr[1], scr[1], ACT.Exp, scale=-1.0).then_inc(S("dn_el"), 1)
                if lat:
                    act.wait_ge(S("lat_du"), g + 1)
                    nc.scalar.activation(g_dec[:, g, :], g_dec[:, g, :], ACT.Exp).then_inc(S("lat_eu"), 1)
            for g in range(4):
                b = W(f"x0{g}")
                free(nc.scalar.activation(g_X[:, g, :], ps[b][:, :], ACT.Copy), b)
                act.drain().then_inc(S("dn_X0"), 1)
            for lv in range(1, LEVELS - 1):
                for g in range(4):
                    b = W(f"t{lv}{g}")
                    free(nc.scalar.activation(g_T[:, g, :], ps[b][:, :], ACT.Copy), b)
                    act.drain().then_inc(S("dn_T2"), 1)
            for g in range(4):
                b = W(f"u{g}")
                free(nc.scalar.activation(g_A[:, g, :], ps[b][:, :], ACT.Copy), b)
                if lat or g in (1, 2):
                    b = W(f"w{g}")
                    free(nc.scalar.activation(g_T[:, g, :], ps[b][:, :], ACT.Copy), b)
                act.drain().then_inc(S("dn_uw"), 1)
            return l

        def dve_delta(dve, part, w, l0, sec):
            lat = part == "lat"
            told = lambda name, n: (S("dn_" + name), n + (CTX_TOLD[name] if lat else 0))
            W = lambda use: banks.wait_full(dve, sec, f"{part}_{use}")
            bank = lambda use: banks.bank(sec, f"{part}_{use}")
            free = lambda ins, b: ins.then_inc(banks.free[b], 1)
            row = GRID_W if lat else T
            l = l0
            for i, (name, c) in enumerate(tiles_of(part)):
                split_lo(dve, w, l + 1) if w.s0 + l + 1 < w.end else None
                b = bank(f"{name}{c}")
                tile = conv_names[name] + 2 * c
                view = lambda v: v.rearrange("p (r w) -> p r w", w=row)
                dve.wait_ge(*told("conv1", 2 * i + 2))
                for m in range(2):
                    y, x = view(conv[i % 2][:, T * m:T * (m + 1)]), view(ps[b][:, T * m:T * (m + 1)])
                    nc.vector.scalar_tensor_tensor(y[:, :, 1:row], x[:, :, 0:row - 1], vcol("dn_conv_w_2", tile + m),
                                                   y[:, :, 1:row], ALU.mult, ALU.add)
                dve.drain()
                for m in range(2):
                    y, x = view(conv[i % 2][:, T * m:T * (m + 1)]), view(ps[b][:, T * m:T * (m + 1)])
                    ins = nc.vector.scalar_tensor_tensor(y[:, :, 0:row - 1], x[:, :, 1:row],
                                                         vcol("dn_conv_w_2", 24 + tile + m), y[:, :, 0:row - 1],
                                                         ALU.mult, ALU.add)
                free(ins, b)
                dve.drain().then_inc(S("dn_conv"), 1)
                l += 1
            if lat:
                for c in range(2):
                    split_lo(dve, w, l + 1)
                    l += 1
            b = W("ba")
            ba = ps[b][:, 0:32].rearrange("p (n c) -> p n c", n=2)
            two = lambda v: v.unsqueeze(1).broadcast_to([P, 2, 8])
            nc.vector.tensor_scalar(ba_t1, ba[:, :, 0:8], -88.0, None, ALU.max)
            free(nc.vector.tensor_tensor(ba_g, ba[:, :, 8:16], two(dn_rows[:, 8:16]), ALU.add), b)
            dve.drain()
            nc.vector.tensor_scalar(ba_t2, ba_g, -1.0, None, ALU.mult)
            dve.drain()
            nc.vector.tensor_tensor(ba_t2, ba_t2, ba_g, ALU.max)
            dve.drain().then_inc(S("dn_ba"), 1)
            nq = 4 if lat else 2
            first = 0 if lat else 4
            dve.wait_ge(*told("silu", len(tiles_of(part))))
            for i in range(nq):
                v = sil[:, first + 2 * i:first + 2 * i + 2, :]
                if i >= 2:
                    W(f"l2{i - 2}")
                nc.vector.tensor_tensor(scr[i % 2].rearrange("p (m t) -> p m t", m=2), v, v, ALU.mult).then_inc(
                    S("dn_sq"), 1)
            dve.wait_ge(*told("ba2", 1))
            nc.vector.tensor_scalar(ba_t1, ba_t1, 1.0, None, ALU.add)
            nc.vector.scalar_tensor_tensor(ba_g, ba_g, 0.0, ba_t2, ALU.max, ALU.add)
            dve.drain()
            nc.vector.reciprocal(ba_beta, ba_t1)
            nc.vector.tensor_tensor(ba_g, ba_g, two(neg_a[:, :]), ALU.mult)
            dve.drain().then_inc(S("dn_g"), 1)
            for i in range(nq):
                v = sil[:, first + 2 * i:first + 2 * i + 2, :]
                dve.wait_ge(*told("rs", i + 1))
                nc.vector.tensor_tensor(v, v, rstd_b[:, :].rearrange("p (m t) -> p m t", m=2), ALU.mult).then_inc(
                    S("lat_qn" if lat and i < 2 else "dn_kn"), 1)
            b = W("cum")
            both = ps[b][:, 0:32].rearrange("p (s g c) -> p s g c", s=2, g=4)
            nc.vector.tensor_copy(gcol, both[:, 0])
            free(nc.vector.tensor_copy(gtot, both[:, 1]), b)
            dve.drain()
            nc.vector.tensor_tensor(kd_col, gtot, gcol, ALU.subtract)
            dve.drain().then_inc(S("dn_gcol"), 1)
            dve.wait_ge(*told("ecol", 1))
            for g in range(4):
                nc.vector.tensor_tensor(bg_col[:, g, :], beta_of(g), eg_col[:, g, :], ALU.mult)
            dve.drain().then_inc(S("dn_bcol"), 1)
            for g in range(4):
                d, n = chunk_of(g)
                b = W(f"grow{g}")
                if lat:
                    dve.wait_ge(S("lat_egrow"), g + 1)
                free(nc.vector.tensor_tensor(h4(scr[0]), h4(ps[b][:, :]), per_head(gcol[:, g, :]), ALU.subtract), b)
                dve.drain()
                nc.vector.tensor_tensor(h4(scr[1]), h4(scr[0]), all_heads(col(f"lo{d}", 0, P)), ALU.max).then_inc(
                    S("dn_dl"), 1)
                if lat:
                    nc.vector.tensor_tensor(h4(g_dec[:, g, :]), h4(scr[0]), all_heads(col(f"up{d}", 0, P)),
                                            ALU.min).then_inc(S("lat_du"), 1)
                b = W(f"kk{g}")
                dve.wait_ge(*told("el", g + 1))
                free(nc.vector.tensor_tensor(g_A[:, g, :], ps[b][:, :], scr[1], ALU.mult), b)
                dve.drain()
                nc.vector.tensor_tensor(h4(g_A[:, g, :]), h4(g_A[:, g, :]), per_head(beta_of(g)), ALU.mult)
                dve.drain()
                nc.vector.tensor_tensor(h4(scr[2]), h4(g_A[:, g, :]), all_heads(col(f"pair{d}", 0, P)), ALU.mult)
                dve.drain()
                nc.vector.tensor_tensor(h4(g_T[:, g, :]), all_heads(ident), h4(scr[2]), ALU.subtract).then_inc(
                    S("dn_T"), 1)
                if lat:
                    b = W(f"qk{g}")
                    dve.wait_ge(S("lat_eu"), g + 1)
                    free(nc.vector.tensor_tensor(g_dec[:, g, :], ps[b][:, :], g_dec[:, g, :], ALU.mult), b)
                    dve.drain().then_inc(S("lat_attn"), 1)
            for g in range(4):
                dve.wait_ge(*told("X0", g + 1))
                dve.drain().then_inc(S("dn_X"), 1)
            for lv in range(1, LEVELS):
                for g in range(4):
                    d, n = chunk_of(g)
                    b = W(f"z{lv}{g}")
                    m = col(f"lvl{d}", 64 * (lv - 1), 64)
                    free(nc.vector.tensor_tensor(z_sm[:, g, :].rearrange("p (h c) -> p h c", h=DN_H),
                                                 ps[b][:, 0:256].rearrange("p (h c) -> p h c", h=DN_H),
                                                 all_heads(m), ALU.mult), b)
                    dve.drain().then_inc(S("dn_Z"), 1)
                for g in range(4):
                    d, n = chunk_of(g)
                    b = W(f"xz{lv}{g}")
                    z4 = lvl_shape(ps[b][:, 0:256], lv)
                    for hh in range(DN_H):
                        xs = lvl_cols(h4(g_X[:, g, :]), d, lv)[:, hh]
                        ins = nc.vector.tensor_tensor(xs, xs, z4[:, hh], ALU.subtract)
                    free(ins, b)
                    dve.drain().then_inc(S("dn_X"), 1)
            nv = 0
            for step in range(2):
                for d in range(2):
                    g = group_of(d, step)
                    if lat or step == 1:
                        b = W(f"ws{step}{d}")
                        dve.wait_ge(*told("uw", 4))
                        free(nc.vector.tensor_tensor(g_A[:, g, :], g_A[:, g, :], ps[b][:, :], ALU.subtract), b)
                        dve.drain().then_inc(S("dn_vnew"), 1)
                for d in range(2):
                    g = group_of(d, step)
                    if lat:
                        b = W(f"o{step}{d}")
                        n = g % 2
                        o = tok(o_n, n)
                        if step == 0:
                            free(nc.vector.tensor_copy(o, h4(ps[b][:, :])), b)
                        else:
                            free(nc.vector.tensor_tensor(o, o, h4(ps[b][:, :]), ALU.add), b)
                        dve.drain()
                    if step == 0 or not lat:
                        b = W(f"s{step}{d}")
                        st = state[:, d]
                        if step == 0 and not lat:
                            free(nc.vector.tensor_copy(st, h4(ps[b][:, :])), b)
                        else:
                            nc.vector.tensor_tensor(st, st, per_head(et_col[:, g, :]), ALU.mult)
                            dve.drain()
                            free(nc.vector.tensor_tensor(st, st, h4(ps[b][:, :]), ALU.add), b)
                        dve.drain().then_inc(S("dn_state"), 1)
            return l

        o_n = v_n

        def pool_delta(pool, part):
            lat = part == "lat"
            told = lambda name, n: (S("dn_" + name), n + (CTX_TOLD[name] if lat else 0))
            g_v = nc.gpsimd
            pool.wait_ge(*told("g", 1))
            for g in range(4):
                d, n = chunk_of(g)
                g_v.tensor_tensor(h4(g_X[:, g, :]), all_heads(col(f"cum{d}", 0, P)),
                                  per_head(ba_g[:, n, 4 * d:4 * d + 4]), ALU.mult).then_inc(S("dn_tg"), 1)
            pool.wait_ge(*told("ecol", 1))
            pool.wait_ge(*told("tok", 1))
            for g in range(4):
                d, n = chunk_of(g)
                g_v.tensor_tensor(h4(g_kd[:, g, :]), ktok[:, n], per_head(kd_col[:, g, :]), ALU.mult).then_inc(
                    S("dn_kd"), 1)
            if lat:
                pool.wait_ge(S("lat_qn"), 2)
                for g in range(4):
                    d, n = chunk_of(g)
                    pool.wait_ge(S("lat_egrow"), g + 1)
                    g_v.tensor_tensor(h4(g_q[:, g, :]), tok(q_n, n), h4(g_q[:, g, :]), ALU.mult).then_inc(
                        S("lat_qg"), 1)
            pool.wait_ge(*told("bcol", 1))
            for g in range(4):
                d, n = chunk_of(g)
                if g >= 2:
                    pool.wait_ge(*told("uw", g - 1))
                g_v.tensor_tensor(h4(scr_vb(g)), vtok[:, n], per_head(beta_of(g)), ALU.mult)
                g_v.tensor_tensor(h4(scr_kb(g)), ktok[:, n], per_head(bg_col[:, g, :]), ALU.mult)
                pool.drain().then_inc(S("dn_vb"), 1)

        L = Arena()
        q_r, k_r = L(6, T), L(6, T)
        v_t = L(TT, 768)
        z_raw = [L(2, T) for _ in range(2)]
        z_cos = [L(2, T) for _ in range(2)]
        z_sin = [L(2, T) for _ in range(2)]
        tab_c, tab_s = L(T), L(T)
        prob = L(12, 384)
        probT = L(4, 384)
        stat = L(8, 24)
        mx, sm, nb, dm, ex, wl, fac = (stat[:, i, :].rearrange("p (g b i q) -> p g b i q", g=3, b=2, i=2)
                                       for i in range(7))
        top = stat[:, 7, 0:8].rearrange("p (b n) -> p b n", b=2)
        tot = stat[:, 7, 8:16].rearrange("p (b n) -> p b n", b=2)
        rtot = stat[:, 7, 16:24].rearrange("p (b n) -> p b n", b=2)
        PADW = 16
        win = [L(2, PADW + T) for _ in range(5)]
        p_tok = L(TT, 256)
        red = L(T)
        relu = [L(2, T) for _ in range(2)]
        relu2 = [L(2, T) for _ in range(2)]
        sq = prob.rearrange("p a b -> p (a b)")[:, 0:KT * T].rearrange("p (k t) -> p k t", k=KT)
        gate_t = relu
        rstd_col = rstd_b[:, 0:2]
        inv_ms = rstd_b[:, T:2 * T]

        def up_at(j):
            return 14 + j if j < 2 else 13 + 2 * j

        def down_at(j):
            return 16 + 2 * j if j < UPS - 1 else 45

        KIND = {up_at(j): ("up", j) for j in range(UPS)} | {down_at(j): ("down", j) for j in range(UPS)}

        def layer_where(layer):
            w = Where(S_LAYER, C_LAYER, layer, LAYER_CHUNKS, "layer")
            return w

        pre_w = Where(0, MOD_FIRST)
        pre_w.end = CTX_CHUNKS
        post_w = Where(S_POST, C_POST, sec="post")
        post_w.end = S_END

        def more(w, l):
            return w.s0 + l + 1 < w.end

        rows_ab = scr[0][:, 0:256]
        pos_i = scr[0][0:1, 256:512].bitcast(I32)
        w_ba = scr[2][:, 0:128].rearrange("p (k n) -> p k n", k=KT)
        pos_f = scr[2][0:1, 128:384]
        dn_row = scr[2][0:1, 384:400]
        silu_c = sg[:, 160:176].rearrange("p (j k) -> p j k", j=2)
        pool_w = sb("pool_blocks", [P, 2, P])

        two_k = lambda g, i: g.rearrange("p a b -> p (a b)")[:, 1024 * i:1024 * (i + 1)].rearrange(
            "p (k t) -> p k t", k=4)
        sc_b, sc_c = two_k(g_A, 0), two_k(g_A, 1)
        sc_p, sc_y = two_k(g_X, 0), two_k(g_X, 1)
        fn_u = two_k(g_T, 0)
        fn_ch = g_dec.rearrange("p a b -> p (a b)").rearrange("p (t g n) -> p t g n", t=2, g=4)
        gate = g_q.rearrange("p a b -> p (a b)").rearrange("p (k t) -> p k t", k=KT)
        merged = pre_x
        y_rows = xtok
        mt = xc
        ff_s = [scr[0].rearrange("p (m t) -> p m t", m=2), scr[1].rearrange("p (m t) -> p m t", m=2)]
        ff_p = [z_kb[:, i, :].rearrange("p (m t) -> p m t", m=2) for i in range(2)]

        @block.tensor
        def _(pe):
            claim = lambda sec, use, layer=0: banks.claim(pe, sec, use, layer)
            full = lambda mm, b: mm.then_inc(banks.full[b], 1)
            tr = lambda o, x: nc.tensor.transpose(o, x, ident)
            mods = [0]

            def mod_chunk():
                m = mods[0]
                mods[0] += 1
                raw_index = m if m < MOD_FIRST else m + CTX_CHUNKS
                pe.wait_ge(landed[raw_index % RAW], 16 * (raw_index // RAW + 1))
                wv = raw[:, raw_index % RAW, :].rearrange("p (k n) -> p k n", k=KT)
                for i in range(2):
                    c = 2 * (2 * m + i)
                    for k in range(KT):
                        mm = nc.tensor.matmul(ps[3][:, c:c + 2], wv[:, k, P * i:P * (i + 1)], silu_c[:, :, k],
                                              start=k == 0, stop=k == KT - 1)
                mm.then_inc(mod_done, 1)

            def between(n):
                for _ in range(n):
                    if mods[0] < MOD_CHUNKS:
                        mod_chunk()

            pe.wait_ge(S("consts"), 16)
            pe.wait_ge(S("rows_landed"), 16 * 2)
            b = claim("pre", "vec")
            nc.tensor.transpose(ps[b][:, 0:ROWS_A], rows_ab[0:ROWS_A, 0:P], ident[0:ROWS_A, 0:ROWS_A])
            nb_rows = NV - ROWS_A
            full(nc.tensor.transpose(ps[b][:, ROWS_A:NV], rows_ab[0:nb_rows, P:2 * P], ident[0:nb_rows, 0:nb_rows]), b)
            for name, src in (("x", xtok), ("ctx", ctok)):
                pe.wait_ge(S(f"{name}_landed"), 16)
                for c in range(4):
                    b = claim("pre", f"{name}{c}")
                    for i in range(2):
                        for t in range(TT):
                            at = P * (2 * c + i)
                            mm = tr(ps[b][:, T * i + P * t:T * i + P * (t + 1)], src[:, t, at:at + P])
                    full(mm, b)
            pe.wait_ge(S("pos_ready"), 1)
            b = claim("pre", "rows")
            nc.tensor.matmul(ps[b][:, 0:T], ones[0:1, :], pos_f, start=True, stop=True)
            full(nc.tensor.matmul(ps[b][:, T:T + 16], ones[0:1, :], dn_row, start=True, stop=True), b)
            pe.wait_ge(S("silu_c"), 1)
            for _ in range(MOD_FIRST):
                mod_chunk()
            pe.wait_ge(S("pre_ssq"), 1)
            b = claim("pre", "norm")
            full(nc.tensor.matmul(ps[b][:, 0:T], ones, z_n[:, 0, :], start=True, stop=True), b)
            pe_delta(pe, "ctx", pre_w, 0, "pre", between)
            between(MOD_CHUNKS)

            with pe.Fori(0, DEPTH) as layer:
                w = layer_where(layer)
                W = lambda use: banks.wait_full(pe, "layer", use, layer)
                C = lambda use: claim("layer", use, layer)
                wait = lambda name, n, per: pe.wait_ge(S(name), w.nth(n, per))

                def ssq(use, n):
                    wait("ssq_in", n, 3)
                    b = C(use)
                    mm = nc.tensor.matmul(ps[b][:, 0:T], ones, red, start=True, stop=True)
                    if n == 1:
                        for t in range(TT):
                            mm = nc.tensor.matmul(ps[b][:, T + 2 * t:T + 2 * t + 2], red[:, P * t:P * (t + 1)],
                                                  ones[:, 0:2], start=True, stop=True)
                    full(mm, b)

                def rotate(s):
                    wait("z_raw", s + 1, 6)
                    b = C(f"rot{s}")
                    full(nc.tensor.matmul(ps[b][:, :], col("rot", 0, P),
                                          z_raw[s % 2].rearrange("p m t -> p (m t)"), start=True, stop=True), b)

                def scores(batch):
                    for hd in heads(batch):
                        wait("qk_ready", 2 * (hd // HPG) + 2, 6)
                        b = C(f"s{hd}")
                        lo, m = HEAD * (hd % 2), hd // 2
                        qh, kh = q_r[lo:lo + HEAD, m, :], k_r[lo:lo + HEAD, m, :]
                        nc.tensor.matmul(ps[b][:, 0:P], qh[:, 0:P], kh[:, 0:P], start=True, stop=True)
                        full(nc.tensor.matmul(ps[b][:, P:P + T], qh[:, P:T], kh, start=True, stop=True), b)

                for s in range(6):
                    b = C(f"qk{s}")
                    project(pe, w, s, lambda m: (b, T * m), KT, xhi, xlo,
                            (lambda f: wait("n1_act", f + 1, KT)) if s == 0 else None)
                    if s == 0:
                        ssq("ssq1", 1)
                        wait("side_landed", 16 * 3, 16 * 3)
                        b = C("p")
                        for k in range(2):
                            for t in range(TT):
                                mm = tr(ps[b][:, T * k + P * t:T * k + P * (t + 1)], p_tok[:, t, P * k:P * (k + 1)])
                        full(mm, b)
                    else:
                        rotate(s - 1)
                b = C("v0")
                project_tokens(pe, w, 6, b)
                rotate(5)
                scores(0)
                b = C("v1")
                project_tokens(pe, w, 7, b)
                scores(1)
                b = C("v2")
                project_tokens(pe, w, 8, b)
                b = C("u")
                project(pe, w, 9, lambda m: (b, T * m), KT, xhi, xlo)
                for kind, x in ATT:
                    if kind == "T":
                        i = T_ORDER.index(x)
                        wait("prob_ready", i + 1, 12)
                        b = C(f"pT{x}")
                        e = prob[:, x, :]
                        tr(ps[b][:, 0:P], e[:, 0:P])
                        tr(ps[b][:, P:2 * P], e[:, P:2 * P])
                        full(tr(ps[b][:, 2 * P:3 * P], e[:, 2 * P:3 * P]), b)
                    elif kind == "V":
                        n = V_ORDER.index(x)
                        wait("probT_ready", 2 * n + 2, 12)
                        wait("v_ready", 3, 3)
                        b = C(f"pv{x}")
                        for i in range(2):
                            hd = 2 * x + i
                            pt = probT[:, T_ORDER.index(hd) % 4, :]
                            vh = v_t[:, :, HEAD * hd:HEAD * (hd + 1)]
                            o = ps[b][HEAD * i:HEAD * (i + 1), :]
                            nc.tensor.matmul(o[:, 0:T], vh[:, 0, :], pt[:, 0:T], start=True, stop=False,
                                             skip_group_check=True)
                            mm = nc.tensor.matmul(o[:, P:T], vh[:, 1, :], pt[:, T:T + P], start=False, stop=True,
                                                  skip_group_check=True)
                        full(mm, b)
                    else:
                        wait("pool_y", 1, 1)
                        b = C("pool")
                        for i in range(2):
                            mm = nc.tensor.matmul(ps[b][:, T * i:T * (i + 1)], pool_w[:, i, :],
                                                  win[0][:, i, PADW:], start=True, stop=True)
                        full(mm, b)
                for c in range(4):
                    b = C(f"out{c}")
                    if c == 0:
                        wait("cat_act", 7, 7)
                    project(pe, w, 10 + c, lambda m: (b, T * m), KT, xhi, xlo)
                for s in range(14, 46):
                    kind, j = KIND[s]
                    if kind == "up":
                        b = C(f"up{j}")
                        project(pe, w, s, lambda m: (b, T * m), KT, xhi, xlo,
                                (lambda f: wait("n2_act", f + 1, KT)) if j == 0 else None)
                        if j == 1:
                            ssq("ssq2", 2)
                    else:
                        if j == 0:
                            for b in range(4):
                                C(f"down{b}")
                        wait("relu_act", j + 1, UPS)
                        project(pe, w, s, lambda m: (m // 2, T * (m % 2)), 2, yhi[:, 2 * (j % 2):2 * (j % 2) + 2, :],
                                ylo[:, 2 * (j % 2):2 * (j % 2) + 2, :], first=j == 0, last=j == UPS - 1)
                wait("p_act", 1, 1)
                for c in range(2):
                    for i in range(2):
                        C(f"ple{2 * c + i}")
                    project(pe, w, 46 + c, lambda m: (4 + 2 * c + m // 2, T * (m % 2)), 2, phi, plo)
                for c in range(4):
                    if c == 2:
                        ssq("ssq3", 3)
                    b = C(f"gate{c}")
                    project(pe, w, 48 + c, lambda m: (b, T * m), KT, xhi, xlo,
                            (lambda f: wait("n3_act", f + 1, KT)) if c == 0 else None)

            w = post_w
            C = lambda use: claim("post", use)

            def ssq_post(use, n):
                pe.wait_ge(S("post_ssq"), n)
                b = C(use)
                full(nc.tensor.matmul(ps[b][:, 0:T], ones, z_n[:, 0, :], start=True, stop=True), b)

            ssq_post("final", 1)
            ssq_post("norm1", 2)
            l = pe_delta(pe, "lat", w, 0, "post", lambda n: None)
            for i in range(2):
                pe.wait_ge(S("o_sq"), i + 1)
                b = C(f"onorm{i}")
                full(nc.tensor.matmul(ps[b][:, :], ones, scr[i], start=True, stop=True), b)
            for use in [f"sc{c}" for c in range(6)] + [f"fn{c}" for c in range(2)]:
                b = C(use)
                project(pe, w, l, lambda m: (b, T * m), KT, xhi, xlo)
                l += 1
            for g in range(4):
                pe.wait_ge(S("fn_u"), g // 2 + 1)
                for t in range(TT):
                    b = C(f"fch{g}{t}")
                    full(nc.tensor.matmul(ps[b][:, 0:T], fn_u[:, g, P * t:P * (t + 1)], col("dft_ch", 0, T),
                                          start=True, stop=True), b)
            for c in range(2):
                pe.wait_ge(S("fn_ch"), 4 * (c + 1))
                b = C(f"fpos{c}")
                for i in range(2):
                    for t in range(TT):
                        o = ps[b][:, T * i:T * (i + 1)]
                        nc.tensor.matmul(o, fn_ch[:, t, 2 * c + i, 0:P], col("dft_cos", T * t, T),
                                         start=t == 0, stop=False, skip_group_check=True)
                        mm = nc.tensor.matmul(o, fn_ch[:, t, 2 * c + i, P:2 * P], col("dft_nsin", T * t, T),
                                              start=False, stop=t == TT - 1, skip_group_check=True)
                full(mm, b)
            for n in range(3):
                for c in range(4):
                    b = C(f"gate{n}{c}")
                    project(pe, w, l, lambda m: (b, T * m), KT, xhi, xlo)
                    l += 1
                pe.wait_ge(S("branch_act"), 2 * (n + 1))
                for i in range(2):
                    y0, y1 = C(f"y{n}{2 * i}"), C(f"y{n}{2 * i + 1}")
                    project(pe, w, l, lambda m: ((y0, y1)[m // 2], T * (m % 2)), 4, yhi, ylo)
                    l += 1
            for c in range(4):
                b = C(f"wo{c}")
                project(pe, w, l, lambda m: (b, T * m), KT, xhi, xlo,
                        (lambda f: pe.wait_ge(S("merged_act"), f + 1)) if c == 0 else None)
                l += 1
            ssq_post("norm2", 3)
            nff = FF2 // 256

            def ffn_out(j, l):
                if j == 0:
                    for b in range(4):
                        C(f"ffo{b}")
                pe.wait_ge(S("ff_act"), j + 1)
                project(pe, w, l, lambda m: (m // 2, T * (m % 2)), 2, yhi[:, 2 * (j % 2):2 * (j % 2) + 2, :],
                        ylo[:, 2 * (j % 2):2 * (j % 2) + 2, :], first=j == 0, last=j == nff - 1)

            for j in range(nff):
                for x in "ab":
                    b = C(f"ff{x}{j}")
                    project(pe, w, l, lambda m: (b, T * m), KT, xhi, xlo,
                            (lambda f: pe.wait_ge(S("n2_act_2"), f + 1)) if j == 0 and x == "a" else None)
                    l += 1
                if j:
                    ffn_out(j - 1, l)
                    l += 1
            ffn_out(nff - 1, l)
            ssq_post("final2", 4)
            for half in range(2):
                for t in range(TT):
                    c = 2 * half + t
                    pe.wait_ge(S("y_cols"), 4 * (half + 1))
                    b = C(f"y_out{c}")
                    for k in range(4):
                        mm = tr(ps[b][:, P * k:P * (k + 1)], h[:, 4 * half + k, P * t:P * (t + 1)])
                    full(mm, b)

        @block.scalar
        def _(act):
            full = lambda sec, use, layer=0: banks.wait_full(act, sec, use, layer)
            free = lambda ins, b: ins.then_inc(banks.free[b], 1)

            def rms(b, n, scale, out, power=-0.5):
                free(nc.scalar.activation(out, ps[b][:, 0:n], ACT.Ln, scale=scale, bias=eps_col), b)
                act.drain()
                return nc.scalar.activation(out, out, ACT.Exp, scale=power)

            act.dma_start(rows_ab[0:ROWS_A, 0:P], a["vec_rows"][0:ROWS_A, :]).then_inc(S("rows_landed"), 16)
            act.dma_start(rows_ab[0:NV - ROWS_A, P:2 * P], a["vec_rows"][ROWS_A:NV, :]).then_inc(S("rows_landed"), 16)
            split_at = K["mask"][0]
            act.dma_start(kt[:, 0:split_at], a["consts"][:, 0:split_at]).then_inc(S("consts"), 16)
            act.dma_start(pos_i, a["positions"]).then_inc(S("small_landed"), 16)
            act.dma_start(dn_row, a["dn_row"]).then_inc(S("small_landed"), 16)
            act.dma_start(w_ba, k_all(w_in2, BA2, 16)).then_inc(S("small_landed"), 16)
            act.dma_start(xtok, a["x"][0].rearrange("(t p) d -> p t d", p=P)).then_inc(S("x_landed"), 16)
            act.dma_start(ctok, a["ctx_2"][0].rearrange("(t p) d -> p t d", p=P)).then_inc(S("ctx_landed"), 16)
            act.dma_start(kt[:, split_at:NK], a["consts"][:, split_at:NK]).then_inc(S("tables"), 16)

            b = full("pre", "vec")
            free(nc.scalar.activation(vec[:, :], ps[b][:, 0:NV], ACT.Copy), b)
            act.drain().then_inc(S("vec_ready"), 1)
            cc = V["c_2"]
            nc.scalar.activation(silu_c, vec[:, cc:cc + 16].rearrange("p (j k) -> p j k", j=2),
                                 ACT.Silu).then_inc(S("silu_c"), 1)
            act.wait_ge(S("small_landed"), 48)
            nc.scalar.activation(ba_hi[:, :, :], w_ba, ACT.Copy).then_inc(S("w_ba_hi"), 1)
            for c in range(4):
                b = full("pre", f"ctx{c}")
                free(nc.scalar.activation(xc[:, 2 * c:2 * c + 2, :], pair(b), ACT.Copy), b)
                act.drain().then_inc(S("xc_ready"), 1)
            act.wait_ge(S("rope_arg"), 1)
            nc.scalar.activation(rope_s[:, :], rope_s[:, :], ACT.Sin)
            nc.scalar.activation(rope_c[:, :], rope_c[:, :], ACT.Sin)
            nc.scalar.activation(neg_a[:, :], dn_rows[:, 0:8], ACT.Exp)
            act.drain().then_inc(S("rope_done"), 1)
            b = full("pre", "norm")
            rms(b, T, 1.0 / D, rstd[:, :]).then_inc(S("pre_rstd"), 1)
            for c in range(2):
                split_hi(act, pre_w, c) if c == 0 else None
            for k in range(KT):
                act.wait_ge(S("dn_mt"), k + 1)
                nc.scalar.activation(xhi[:, k, :], mt[:, k, :], ACT.Identity,
                                     bias=modc[:, k, 1:2]).then_inc(S("dn_hi"), 1)
            act_delta(act, "ctx", pre_w, 0, "pre")
            split_hi(act, Where(S_LAYER, C_LAYER), 0)

            with act.Fori(0, DEPTH) as layer:
                w = layer_where(layer)
                W = lambda use: full("layer", use, layer)
                bank = lambda use: banks.bank("layer", use)
                wait = lambda name, n, per: act.wait_ge(S(name), w.nth(n, per))
                done = lambda s: act.wait_ge(pieces_done, w.pieces(s, 1))

                def norm_hi(name, at, ready):
                    for k in range(KT):
                        ready(k)
                        nc.scalar.activation(xhi[:, k, :], h[:, k, :], ACT.Identity,
                                             scale=cur_vec[:, at + k:at + k + 1]).then_inc(S(name + "_hi"), 1)

                norm_hi("n1", 0, lambda k: wait("cur_vec", 1, 1) if k == 0 else None)
                split_hi(act, w, 1)
                b = W("ssq1")
                free(nc.scalar.activation(rstd_w[:, :], ps[b][:, 0:T + 4], ACT.Ln, scale=1.0 / D, bias=eps_col), b)
                act.drain()
                nc.scalar.activation(rstd_w[:, :], rstd_w[:, :], ACT.Exp, scale=-0.5).then_inc(S("rstd_1"), 1)
                b = W("p")
                nc.scalar.activation(phi[:, :, :], pair(b), ACT.Copy).then_inc(S("p_hi"), 1)
                for s in range(6):
                    if s:
                        split_hi(act, w, s + 1)
                    done(s)
                    if s >= 2:
                        wait("z_cos", s - 1, 6)
                        W(f"rot{s - 2}")
                    free(nc.scalar.activation(z_raw[s % 2], pair(bank(f"qk{s}")), ACT.Copy), bank(f"qk{s}"))
                    act.drain().then_inc(S("z_raw"), 1)

                def values(c):
                    done(6 + c)
                    b = bank(f"v{c}")
                    for t in range(TT):
                        ins = nc.scalar.activation(v_t[:, t, 256 * c:256 * (c + 1)], ps[b][:, T * t:T * (t + 1)],
                                                   ACT.Copy, scale=rstd_w[:, T + 2 * t:T + 2 * t + 1])
                    free(ins, b)
                    act.drain().then_inc(S("v_ready"), 1)

                def exps(batch):
                    for n, hd in enumerate(heads(batch)):
                        wait("max_ready", 6 * batch + n + 1, 12)
                        g, i = hd // HPG, hd % 2
                        for t in range(TT):
                            e = prob[:, hd, P * t:P * t + P * (t + 1)]
                            nc.scalar.activation(e, e, ACT.Exp, scale=QSCALE, bias=nb[:, g, batch, i, t:t + 1],
                                                 accum_out=sm[:, g, batch, i, t:t + 1])
                    wait("top_ready", batch + 1, 2)
                    nc.scalar.activation(ex[:, :, batch], dm[:, :, batch], ACT.Exp, scale=QSCALE)
                    act.drain().then_inc(S("exp_ready"), 1)

                split_hi(act, w, 7)
                values(0)
                split_hi(act, w, 8)
                exps(0)
                values(1)
                split_hi(act, w, 9)
                exps(1)
                values(2)
                split_hi(act, w, 10)
                split_hi(act, w, 11)
                for kind, x in ATT:
                    if kind == "T":
                        i = T_ORDER.index(x)
                        if i >= 4:
                            W(f"pv{V_ORDER[(i - 4) // 2]}")
                        b = W(f"pT{x}")
                        free(nc.scalar.activation(probT[:, i % 4, :], ps[b][:, 0:384], ACT.Copy), b)
                        act.drain().then_inc(S("probT_ready"), 1)
                    elif kind == "V":
                        b = W(f"pv{x}")
                        nc.scalar.activation(xhi[:, 2 + x, :], ps[b][:, 0:T], ACT.Copy).then_inc(S("cat_hi"), 1)
                    else:
                        b = W("pool")
                        for i in range(2):
                            ins = nc.scalar.activation(xhi[:, i, :], ps[b][:, T * i:T * (i + 1)], ACT.Copy,
                                                       scale=cur_vec[:, 24 + i:25 + i])
                        ins.then_inc(S("cat_hi"), 1)
                for c in range(1, 4):
                    split_hi(act, w, 11 + c)
                done(13)
                norm_hi("n2", KT, lambda k: wait("h2_ready", k // 2 + 1, 4) if k % 2 == 0 else None)
                for s in range(14, 46):
                    split_hi(act, w, s + 1)
                    kind, j = KIND[s]
                    if kind == "down":
                        continue
                    done(s)
                    b = bank(f"up{j}")
                    free(nc.scalar.activation(relu[j % 2], pair(b), ACT.Relu), b)
                    act.drain().then_inc(S("relu"), 1)
                    wait("relu2", j + 1, UPS)
                    nc.scalar.activation(yhi[:, 2 * (j % 2):2 * (j % 2) + 2, :], relu2[j % 2],
                                         ACT.Copy).then_inc(S("relu_hi"), 1)
                    if j == 1:
                        b = W("ssq2")
                        rms(b, T, 1.0 / D, inv_ms, -1.0).then_inc(S("inv_ms"), 1)
                split_hi(act, w, 47)
                norm_hi("n3", 2 * KT, lambda k: wait("h3_ready", k // 2 + 1, 4) if k % 2 == 0 else None)
                split_hi(act, w, 48)
                split_hi(act, w, 49)
                split_hi(act, w, 50)
                b = W("ssq3")
                rms(b, T, 1.0 / D, rstd[:, :]).then_inc(S("rstd_3"), 1)
                for c in range(4):
                    if c >= 2:
                        split_hi(act, w, 49 + c)
                    wait("gate_in", c + 1, 4)
                    nc.scalar.activation(gate_t[c % 2], gate_t[c % 2], ACT.Sigmoid).then_inc(S("gate_out"), 1)

            w = post_w
            W = lambda use: full("post", use)
            bank = lambda use: banks.bank("post", use)
            done = lambda l: act.wait_ge(pieces_done, w.pieces(l, 1))
            nxt = lambda l: split_hi(act, w, l + 1) if more(w, l) else None
            rms(W("final"), T, 1.0 / D, rstd[:, :]).then_inc(S("post_rstd"), 1)
            act.wait_ge(S("h_final"), 1)
            rms(W("norm1"), T, 1.0 / D, rstd[:, :]).then_inc(S("post_rstd"), 1)
            for k in range(KT):
                act.wait_ge(S("dn_mt"), CTX_TOLD["mt"] + k + 1)
                nc.scalar.activation(xhi[:, k, :], mt[:, k, :], ACT.Identity,
                                     bias=modc[:, k, 0:1]).then_inc(S("dn_hi"), 1)
            l = act_delta(act, "lat", w, 0, "post")
            for i in range(2):
                b = W(f"onorm{i}")
                if i:
                    act.wait_ge(S("o_normed"), 1)
                rms(b, 512, 1.0 / P, rstd_b[:, :]).then_inc(S("o_rstd"), 1)
            for c in range(6):
                nxt(l)
                if c < 4:
                    done(l)
                    b = bank(f"sc{c}")
                    dst = (sc_b, sc_c)[c // 2]
                    free(nc.scalar.activation(dst[:, 2 * (c % 2):2 * (c % 2) + 2, :], pair(b), ACT.Copy), b)
                    if c == 3:
                        act.drain().then_inc(S("sc_bc"), 1)
                l += 1
            for c in range(2):
                nxt(l)
                done(l)
                b = bank(f"fn{c}")
                free(nc.scalar.activation(fn_u[:, 2 * c:2 * c + 2, :], pair(b), ACT.Copy), b)
                act.drain().then_inc(S("fn_u"), 1)
                l += 1
            act.wait_ge(S("sc_p"), 1)
            for k in range(4):
                nc.scalar.activation(sc_y[:, k, :], sc_p[:, k, :], ACT.Identity, scale=vcol("sc_conv_w_2", 4 + k))
            act.drain().then_inc(S("sc_conv1"), 1)
            for g in range(4):
                for t in range(TT):
                    b = W(f"fch{g}{t}")
                    free(nc.scalar.activation(fn_ch[:, t, g, :], ps[b][:, 0:T], ACT.Copy), b)
                    act.drain().then_inc(S("fn_ch"), 1)
            for c in range(2):
                b = W(f"fpos{c}")
                nc.scalar.activation(yhi[:, 2 * c:2 * c + 2, :], pair(b), ACT.Copy).then_inc(S("branch_hi"), 1)
            for n, br in enumerate((2, 1, 0)):
                for c in range(4):
                    nxt(l)
                    done(l)
                    b = bank(f"gate{n}{c}")
                    if n and c == 0:
                        act.wait_ge(S("y_merged"), 4 * n)
                    for m in range(2):
                        ins = nc.scalar.activation(gate[:, 2 * c + m, :], ps[b][:, T * m:T * (m + 1)], ACT.Sigmoid,
                                                   bias=vcol("b_gate_2", KT * br + 2 * c + m))
                    free(ins, b)
                    act.drain().then_inc(S("gate_sig"), 1)
                    if n and c == 0:
                        src = (sc_y, o_n)[n - 1]
                        act.wait_ge(S("sc_done") if n == 1 else S("o_done"), 1)
                        for i in range(2):
                            nc.scalar.activation(yhi[:, 2 * i:2 * i + 2, :], src[:, 2 * i:2 * i + 2, :],
                                                 ACT.Copy).then_inc(S("branch_hi"), 1)
                    l += 1
                for i in range(2):
                    nxt(l)
                    l += 1
            for k in range(KT):
                act.wait_ge(S("y_merged"), 8 + k // 2 + 1)
                nc.scalar.activation(xhi[:, k, :], merged[:, k, :], ACT.Copy).then_inc(S("merged_hi"), 1)
            for c in range(4):
                nxt(l)
                l += 1
            rms(W("norm2"), T, 1.0 / D, rstd[:, :]).then_inc(S("post_rstd"), 1)
            for k in range(KT):
                act.wait_ge(S("n2_mt"), k + 1)
                nc.scalar.activation(xhi[:, k, :], mt[:, k, :], ACT.Identity,
                                     bias=modc[:, 24 + k, 0:1]).then_inc(S("n2_hi_2"), 1)
            for j in range(FF2 // 256):
                nxt(l)
                done(l)
                b = bank(f"ffa{j}")
                if j >= 2:
                    act.wait_ge(S("ff_p"), j - 1)
                free(nc.scalar.activation(ff_s[j % 2], pair(b), ACT.Silu), b)
                act.drain().then_inc(S("ff_s"), 1)
                l += 1
                nxt(l)
                act.wait_ge(S("ff_p"), j + 1)
                nc.scalar.activation(yhi[:, 2 * (j % 2):2 * (j % 2) + 2, :], ff_p[j % 2], ACT.Copy).then_inc(
                    S("ff_hi"), 1)
                l += 1
                if j:
                    nxt(l)
                    l += 1
            nxt(l)
            rms(W("final2"), T, 1.0 / D, rstd[:, :]).then_inc(S("post_rstd"), 1)
            for c in range(4):
                if c % 2 == 0:
                    b = W(f"y_out{c}")
                    free(nc.scalar.activation(y_rows[:, c % 2, 512 * (c // 2):512 * (c // 2 + 1)], ps[b][:, :],
                                              ACT.Copy), b)
                    act.drain().then_inc(S(f"y_rows{c // 2}"), 1)

        @block.vector
        def _(dve):
            v = nc.vector
            full = lambda sec, use, layer=0: banks.wait_full(dve, sec, use, layer)
            free = lambda ins, b: ins.then_inc(banks.free[b], 1)

            def squares(src, dst, out, name):
                v.tensor_tensor(dst, src, src, ALU.mult)
                dve.drain()
                v.tensor_reduce(out, dst.rearrange("p k t -> p t k"), AX.X, ALU.add).then_inc(S(name), 1)

            def scaled(src, gain, name):
                for k in range(KT):
                    v.scalar_tensor_tensor(mt[:, k, :], src[:, k, :], gain(k), rstd[:, :], ALU.mult,
                                           ALU.mult).then_inc(S(name), 1)

            def shifted_lo(shift, hi_name, act_name, before=0):
                for k in range(KT):
                    dve.wait_ge(S(hi_name), before + k + 1)
                    v.scalar_tensor_tensor(xlo[:, k, :], mt[:, k, :], shift(k), xhi[:, k, :].bitcast(F32), ALU.add,
                                           ALU.subtract).then_inc(S(act_name), 1)

            dve.wait_ge(S("small_landed"), 48)
            v.tensor_copy(pos_f, pos_i).then_inc(S("pos_ready"), 1)
            dve.wait_ge(S("w_ba_hi"), 1)
            v.tensor_tensor(ba_lo[:, :, :], w_ba, ba_hi[:, :, :].bitcast(F32), ALU.subtract).then_inc(S("w_ba_split"), 2)
            for c in range(4):
                b = full("pre", f"x{c}")
                free(v.tensor_copy(h[:, 2 * c:2 * c + 2, :], pair(b)), b)
            b = full("pre", "rows")
            v.tensor_copy(dn_rows[:, :], ps[b][:, T:T + 16])
            free(v.tensor_scalar(rope_s[:, :], ps[b][:, 0:T], col("inv_freq"), None, ALU.mult), b)
            dve.drain()
            turns = rstd[:, 0:T]
            v.tensor_scalar(turns, rope_s[:, :], 1.0 / TWO_PI, MAGIC, ALU.mult, ALU.add)
            dve.drain()
            v.tensor_scalar(turns, turns, MAGIC, None, ALU.subtract)
            for part in (PI_A, PI_B, PI_C):
                dve.drain()
                v.scalar_tensor_tensor(rope_s[:, :], turns, -part, rope_s[:, :], ALU.mult, ALU.add)
            dve.drain()
            v.tensor_scalar(rope_c[:, :], rope_s[:, :], np.pi / 2, None, ALU.add)
            dve.drain()
            v.tensor_scalar(turns, rope_c[:, :], np.pi, TWO_PI, ALU.is_gt, ALU.mult)
            dve.drain()
            v.tensor_tensor(rope_c[:, :], rope_c[:, :], turns, ALU.subtract)
            dve.drain()
            edge = 3.1415925
            v.tensor_scalar(rope_c[:, :], rope_c[:, :], edge, -edge, ALU.min, ALU.max)
            v.tensor_scalar(rope_s[:, :], rope_s[:, :], edge, -edge, ALU.min, ALU.max)
            dve.drain().then_inc(S("rope_arg"), 1)
            dve.wait_ge(S("xc_ready"), 4)
            squares(xc, pre_x, z_n[:, 0, :], "pre_ssq")
            dve.wait_ge(S("rope_done"), 1)
            v.tensor_scalar(neg_a[:, :], neg_a[:, :], -1.0, None, ALU.mult)

            def modulation(lo, hi):
                bm = vec[:, V["b_mod_2"] + lo:V["b_mod_2"] + hi].unsqueeze(2).broadcast_to([P, hi - lo, 2])
                return v.tensor_tensor(modc[:, lo:hi, :], ps[3][:, 2 * lo:2 * hi].rearrange("p (m j) -> p m j", j=2),
                                       bm, ALU.add)

            def gain_of(i, norm, tile, j):
                n = V[norm]
                v.scalar_tensor_tensor(gains[:, i, :], modc[:, tile:tile + KT, j], 1.0, vec[:, n:n + KT], ALU.add, ALU.mult)

            dve.wait_ge(mod_done, MOD_FIRST)
            dve.wait_ge(S("vec_ready"), 1)
            modulation(0, 16)
            dve.drain()
            gain_of(0, "norm1_g_2", 8, 0)
            gain_of(1, "norm1_g_2", 8, 1)
            dve.drain()
            dve.wait_ge(S("pre_rstd"), 1)
            scaled(xc, lambda k: gains[:, 1, k:k + 1], "dn_mt")
            split_lo(dve, pre_w, 0)
            shifted_lo(lambda k: modc[:, k, 1:2], "dn_hi", "dn_act")
            dve.wait_ge(S("tables"), 16)
            dve_delta(dve, "ctx", pre_w, 0, "pre")
            dve.wait_ge(mod_done, MOD_CHUNKS)
            free(modulation(16, 48), 3)
            dve.drain()
            gain_of(2, "norm2_g_2", 32, 0)
            for x in win:
                v.memset(x[:, :, 0:PADW], 0.0)
            dve.drain().then_inc(S("pads"), 1)
            split_lo(dve, Where(S_LAYER, C_LAYER), 0)

            with dve.Fori(0, DEPTH) as layer:
                w = layer_where(layer)
                W = lambda use: full("layer", use, layer)
                bank = lambda use: banks.bank("layer", use)
                wait = lambda name, n, per: dve.wait_ge(S(name), w.nth(n, per))
                done = lambda s: dve.wait_ge(pieces_done, w.pieces(s, 1))

                def norm_lo(name, at):
                    for k in range(KT):
                        wait(name + "_hi", k + 1, KT)
                        v.scalar_tensor_tensor(xlo[:, k, :], h[:, k, :], cur_vec[:, at + k:at + k + 1],
                                               xhi[:, k, :].bitcast(F32), ALU.mult, ALU.subtract).then_inc(
                                                   S(name + "_act"), 1)

                v.tensor_copy(cur_vec[:, :], vec[:, 0:DEPTH * LV].rearrange("p (l n) -> p l n", l=DEPTH)[:, layer, :])
                dve.drain().then_inc(S("cur_vec"), 1)
                norm_lo("n1", 0)
                squares(h[:, :, :], sq, red, "ssq_in")
                split_lo(dve, w, 1)
                wait("rstd_1", 1, 1)
                v.tensor_tensor(tab_c, rope_c[:, :], rstd_w[:, 0:T], ALU.mult)
                v.tensor_tensor(tab_s, rope_s[:, :], rstd_w[:, 0:T], ALU.mult)
                dve.drain().then_inc(S("tab_ready"), 1)
                b = W("p")
                wait("p_hi", 1, 1)
                free(v.tensor_tensor(plo[:, :, :], pair(b), phi[:, :, :].bitcast(F32), ALU.subtract), b)
                dve.drain().then_inc(S("p_act"), 1)

                def rotated(s):
                    b = W(f"rot{s}")
                    free(v.tensor_tensor(z_sin[s % 2], pair(b), wide(tab_s, 2), ALU.mult), b)
                    dve.drain()
                    wait("z_cos", s + 1, 6)
                    dst = (k_r, q_r)[s % 2][:, 2 * (s // 2):2 * (s // 2) + 2, :]
                    v.tensor_tensor(dst, z_sin[s % 2], z_cos[s % 2], ALU.add).then_inc(S("qk_ready"), 1)

                def maxima(batch):
                    for hd in heads(batch):
                        b = W(f"s{hd}")
                        g, i = hd // HPG, hd % 2
                        mask = col("mask", 384 * g, 384)
                        v.tensor_tensor(prob[:, hd, 0:P], ps[b][:, 0:P], mask[:, 0:P], ALU.add)
                        ins = v.tensor_tensor_reduce(prob[:, hd, P:384], ps[b][:, P:384], mask[:, P:384], 1.0, -3e38,
                                                     ALU.add, ALU.max, mx[:, g, batch, i, 1:2])
                        dve.drain()
                        v.tensor_reduce(mx[:, g, batch, i, 0:1], prob[:, hd, 0:P], AX.X, ALU.max)
                        free(ins, b)
                        dve.drain()
                        v.tensor_scalar(nb[:, g, batch, i, :], mx[:, g, batch, i, :], -QSCALE, None,
                                        ALU.mult).then_inc(S("max_ready"), 1)
                    flat = lambda x, g: x[:, g, batch].rearrange("p i q -> p (i q)")
                    v.tensor_tensor(top[:, batch], flat(mx, 0), flat(mx, 1), ALU.max)
                    dve.drain()
                    v.tensor_tensor(top[:, batch], top[:, batch], flat(mx, 2), ALU.max)
                    dve.drain()
                    for g in range(3):
                        v.tensor_tensor(flat(dm, g), flat(mx, g), top[:, batch], ALU.subtract)
                    dve.drain().then_inc(S("top_ready"), 1)

                def weights(batch):
                    flat = lambda x, g: x[:, g, batch].rearrange("p i q -> p (i q)")
                    wait("exp_ready", batch + 1, 2)
                    for g in range(3):
                        v.tensor_tensor(flat(wl, g), flat(ex, g), flat(sm, g), ALU.mult)
                    dve.drain()
                    v.tensor_tensor(tot[:, batch], flat(wl, 0), flat(wl, 1), ALU.add)
                    dve.drain()
                    v.tensor_tensor(tot[:, batch], tot[:, batch], flat(wl, 2), ALU.add)
                    dve.drain()
                    v.reciprocal(rtot[:, batch], tot[:, batch])
                    dve.drain()
                    for g in range(3):
                        v.tensor_tensor(flat(fac, g), flat(ex, g), rtot[:, batch], ALU.mult)
                    dve.drain()
                    for hd in heads(batch):
                        g, i = hd // HPG, hd % 2
                        for t in range(TT):
                            e = prob[:, hd, P * t:P * t + P * (t + 1)]
                            ins = v.tensor_scalar(e, e, fac[:, g, batch, i, t:t + 1], None, ALU.mult)
                        dve.drain().then_inc(S("prob_ready"), 1)

                for s in range(6):
                    if s:
                        split_lo(dve, w, s + 1)
                        rotated(s - 1)
                split_lo(dve, w, 7)
                rotated(5)
                split_lo(dve, w, 8)
                maxima(0)
                split_lo(dve, w, 9)
                maxima(1)
                weights(0)
                split_lo(dve, w, 10)
                done(9)
                b = bank("u")
                free(v.tensor_tensor(win[0][:, :, PADW:], pair(b), wide(rstd_w[:, 0:T], 2), ALU.mult), b)
                dve.drain().then_inc(S("u_ready"), 1)
                split_lo(dve, w, 11)
                weights(1)
                for n, (kind, x) in enumerate([kx for kx in ATT if kx[0] != "T"]):
                    wait("cat_hi", n + 1, 7)
                    if kind == "V":
                        b = bank(f"pv{x}")
                        free(v.tensor_tensor(xlo[:, 2 + x, :], ps[b][:, 0:T], xhi[:, 2 + x, :].bitcast(F32),
                                             ALU.subtract), b)
                    else:
                        b = bank("pool")
                        for i in range(2):
                            ins = v.scalar_tensor_tensor(xlo[:, i, :], ps[b][:, T * i:T * (i + 1)],
                                                         cur_vec[:, 24 + i:25 + i], xhi[:, i, :].bitcast(F32),
                                                         ALU.mult, ALU.subtract)
                        free(ins, b)
                    dve.drain().then_inc(S("cat_act"), 1)
                dve.drain().then_inc(S("side_free"), 1)
                for c in range(4):
                    if c:
                        split_lo(dve, w, 11 + c)
                    done(10 + c)
                    b = bank(f"out{c}")
                    hc = h[:, 2 * c:2 * c + 2, :]
                    free(v.tensor_tensor(hc, hc, pair(b), ALU.add), b)
                    dve.drain().then_inc(S("h2_ready"), 1)
                norm_lo("n2", KT)
                split_lo(dve, w, 15)
                squares(h[:, :, :], sq, red, "ssq_in")
                for s in range(14, 46):
                    if s > 14:
                        split_lo(dve, w, s + 1)
                    kind, j = KIND[s]
                    if kind == "down":
                        continue
                    wait("relu", j + 1, UPS)
                    v.tensor_tensor(relu2[j % 2], relu[j % 2], relu[j % 2], ALU.mult).then_inc(S("relu2"), 1)
                    wait("relu_hi", j + 1, UPS)
                    y2 = slice(2 * (j % 2), 2 * (j % 2) + 2)
                    v.tensor_tensor(ylo[:, y2, :], relu2[j % 2], yhi[:, y2, :].bitcast(F32), ALU.subtract).then_inc(
                        S("relu_act"), 1)
                split_lo(dve, w, 47)
                wait("inv_ms", 1, 1)
                done(45)
                for c in range(4):
                    b = bank(f"down{c}")
                    hc = h[:, 2 * c:2 * c + 2, :]
                    free(v.tensor_tensor(relu[c % 2], pair(b), wide(inv_ms, 2), ALU.mult), b)
                    dve.drain()
                    v.tensor_tensor(hc, hc, relu[c % 2], ALU.add)
                    dve.drain().then_inc(S("h3_ready"), 1)
                norm_lo("n3", 2 * KT)
                split_lo(dve, w, 48)
                squares(h[:, :, :], sq, red, "ssq_in")
                split_lo(dve, w, 49)
                split_lo(dve, w, 50)
                wait("rstd_3", 1, 1)
                for c in range(4):
                    if c >= 2:
                        split_lo(dve, w, 49 + c)
                    done(48 + c)
                    b = bank(f"gate{c}")
                    free(v.tensor_tensor(gate_t[c % 2], pair(b), wide(rstd[:, :], 2), ALU.mult), b)
                    dve.drain().then_inc(S("gate_in"), 1)
                    wait("gate_out", c + 1, 4)
                    b = bank(f"ple{c}")
                    hc = h[:, 2 * c:2 * c + 2, :]
                    free(v.tensor_tensor(gate_t[c % 2], gate_t[c % 2], pair(b), ALU.mult), b)
                    dve.drain()
                    v.tensor_tensor(hc, hc, gate_t[c % 2], ALU.add)
                    dve.drain()

            w = post_w
            W = lambda use: full("post", use)
            bank = lambda use: banks.bank("post", use)
            done = lambda l: dve.wait_ge(pieces_done, w.pieces(l, 1))
            nxt = lambda l: split_lo(dve, w, l + 1) if more(w, l) else None
            squares(h[:, :, :], pre_x, z_n[:, 0, :], "post_ssq")
            dve.wait_ge(S("post_rstd"), 1)
            for k in range(KT):
                v.scalar_tensor_tensor(h[:, k, :], h[:, k, :], vcol("final_norm", k), rstd[:, :], ALU.mult, ALU.mult)
            dve.drain().then_inc(S("h_final"), 1)
            squares(h[:, :, :], pre_x, z_n[:, 0, :], "post_ssq")
            dve.wait_ge(S("post_rstd"), 2)
            scaled(h, lambda k: gains[:, 0, k:k + 1], "dn_mt")
            shifted_lo(lambda k: modc[:, k, 0:1], "dn_hi", "dn_act", 8)
            l = dve_delta(dve, "lat", w, 0, "post")
            for i in range(2):
                o2 = o_n[:, 2 * i:2 * i + 2, :]
                v.tensor_tensor(ff_s[i], o2, o2, ALU.mult).then_inc(S("o_sq"), 1)
            for i in range(2):
                o2 = o_n[:, 2 * i:2 * i + 2, :]
                dve.wait_ge(S("o_rstd"), i + 1)
                v.tensor_tensor(o2, o2, rstd_b[:, :].rearrange("p (m t) -> p m t", m=2), ALU.mult).then_inc(
                    S("o_normed"), 1)
            dve.drain()
            dve.wait_ge(S("lat_z"), 1)
            v.scalar_tensor_tensor(o_n, o_n, vcol("dn_onorm_g_2"), z_n, ALU.mult, ALU.mult).then_inc(S("o_done"), 1)
            for c in range(6):
                nxt(l)
                if c >= 4:
                    done(l)
                    if c == 4:
                        dve.wait_ge(S("sc_bc"), 1)
                    b = bank(f"sc{c}")
                    s2 = slice(2 * (c % 2), 2 * (c % 2) + 2)
                    free(v.tensor_tensor(sc_p[:, s2, :], pair(b), sc_c[:, s2, :], ALU.mult), b)
                l += 1
            dve.drain().then_inc(S("sc_p"), 1)
            for c in range(2):
                nxt(l)
                l += 1
            grid = lambda x: x.rearrange("p (r w) -> p r w", w=GRID_W)
            dve.wait_ge(S("sc_conv1"), 1)
            for tap in (0, 2):
                for k in range(4):
                    x, y = grid(sc_p[:, k, :]), grid(sc_y[:, k, :])
                    to, of = (slice(1, GRID_W), slice(0, GRID_W - 1)) if tap == 0 else (slice(0, GRID_W - 1), slice(1, GRID_W))
                    v.scalar_tensor_tensor(y[:, :, to], x[:, :, of], vcol("sc_conv_w_2", 4 * tap + k), y[:, :, to],
                                           ALU.mult, ALU.add)
                dve.drain()
            v.tensor_tensor(sc_y, sc_y, sc_b, ALU.mult).then_inc(S("sc_done"), 1)
            dve.drain()
            for c in range(2):
                b = bank(f"fpos{c}")
                dve.wait_ge(S("branch_hi"), c + 1)
                free(v.tensor_tensor(ylo[:, 2 * c:2 * c + 2, :], pair(b), yhi[:, 2 * c:2 * c + 2, :].bitcast(F32),
                                     ALU.subtract), b)
                dve.drain().then_inc(S("branch_act"), 1)
            for n in range(3):
                for c in range(4):
                    nxt(l)
                    if n and c == 0:
                        src = (sc_y, o_n)[n - 1]
                        for i in range(2):
                            dve.wait_ge(S("branch_hi"), 2 * n + i + 1)
                            s2 = slice(2 * i, 2 * i + 2)
                            v.tensor_tensor(ylo[:, s2, :], src[:, s2, :], yhi[:, s2, :].bitcast(F32),
                                            ALU.subtract).then_inc(S("branch_act"), 1)
                    l += 1
                for i in range(2):
                    nxt(l)
                    done(l)
                    dve.wait_ge(S("gate_sig"), 4 * (n + 1))
                    for c in (2 * i, 2 * i + 1):
                        b = bank(f"y{n}{c}")
                        s2 = slice(2 * c, 2 * c + 2)
                        if n == 0:
                            free(v.tensor_tensor(merged[:, s2, :], pair(b), gate[:, s2, :], ALU.mult), b)
                        else:
                            free(v.tensor_tensor(ff_s[c % 2], pair(b), gate[:, s2, :], ALU.mult), b)
                            dve.drain()
                            v.tensor_tensor(merged[:, s2, :], merged[:, s2, :], ff_s[c % 2], ALU.add)
                        dve.drain().then_inc(S("y_merged"), 1)
                    l += 1
            for k in range(KT):
                dve.wait_ge(S("merged_hi"), k + 1)
                v.tensor_tensor(xlo[:, k, :], merged[:, k, :], xhi[:, k, :].bitcast(F32), ALU.subtract).then_inc(
                    S("merged_act"), 1)

            def residual(b, c, tile):
                for m in range(2):
                    k = 2 * c + m
                    ins = v.scalar_tensor_tensor(h[:, k, :], ps[b][:, T * m:T * (m + 1)], modc[:, tile + k, 0:1],
                                                 h[:, k, :], ALU.mult, ALU.add)
                free(ins, b)

            for c in range(4):
                nxt(l)
                done(l)
                residual(bank(f"wo{c}"), c, 16)
                l += 1
            dve.drain()
            squares(h[:, :, :], pre_x, z_n[:, 0, :], "post_ssq")
            dve.wait_ge(S("post_rstd"), 3)
            scaled(h, lambda k: gains[:, 2, k:k + 1], "n2_mt")
            shifted_lo(lambda k: modc[:, 24 + k, 0:1], "n2_hi_2", "n2_act_2")
            for j in range(FF2 // 256):
                nxt(l)
                l += 1
                nxt(l)
                done(l)
                dve.wait_ge(S("ff_s"), j + 1)
                b = bank(f"ffb{j}")
                if j >= 2:
                    dve.drain()
                free(v.tensor_tensor(ff_p[j % 2], ff_s[j % 2], pair(b), ALU.mult), b)
                dve.drain().then_inc(S("ff_p"), 1)
                dve.wait_ge(S("ff_hi"), j + 1)
                y2 = slice(2 * (j % 2), 2 * (j % 2) + 2)
                v.tensor_tensor(ylo[:, y2, :], ff_p[j % 2], yhi[:, y2, :].bitcast(F32), ALU.subtract).then_inc(
                    S("ff_act"), 1)
                l += 1
                if j:
                    nxt(l)
                    l += 1
            done(l)
            for b in range(4):
                residual(b, b, 40)
            dve.drain()
            squares(h[:, :, :], pre_x, z_n[:, 0, :], "post_ssq")
            dve.wait_ge(S("post_rstd"), 4)
            for k in range(KT):
                v.scalar_tensor_tensor(h[:, k, :], h[:, k, :], vcol("final_g_2", k), rstd[:, :], ALU.mult,
                                       ALU.mult).then_inc(S("y_cols"), 1)
            for c in range(4):
                if c % 2 == 1:
                    b = W(f"y_out{c}")
                    free(v.tensor_copy(y_rows[:, c % 2, 512 * (c // 2):512 * (c // 2 + 1)], ps[b][:, :]), b)
                    dve.drain().then_inc(S(f"y_rows{c // 2}"), 1)

        @block.gpsimd
        def _(pool):
            g = nc.gpsimd
            g.memset(pool_w[:, :, :], 0.0).then_inc(S("side_free"), 1)
            pool.wait_ge(S("tables"), 16)
            pool_delta(pool, "ctx")
            pool.wait_ge(S("pads"), 1)
            with pool.Fori(0, DEPTH) as layer:
                pool.wait_ge(S("tab_ready"), layer + 1)
                for s in range(6):
                    pool.wait_ge(S("z_raw"), layer * 6 + s + 1)
                    if s >= 2:
                        pool.wait_ge(S("qk_ready"), layer * 6 + s - 1)
                    g.tensor_tensor(z_cos[s % 2], z_raw[s % 2], wide(tab_c, 2), ALU.mult).then_inc(S("z_cos"), 1)
                pool.wait_ge(S("u_ready"), layer + 1)
                for n in range(4):
                    sh = 1 << n
                    g.tensor_tensor(win[n + 1][:, :, PADW:], win[n][:, :, PADW:], win[n][:, :, PADW - sh:PADW + T - sh],
                                    ALU.add)
                    pool.drain()
                cnt = col("inv_cnt", 0, 2 * T).rearrange("p (i t) -> p i t", i=2)
                for n in range(4):
                    i, e = n // 2, slice(HEAD * (n % 2), HEAD * (n % 2 + 1))
                    g.tensor_tensor(win[n + 1][e, i, PADW:], win[n + 1][e, i, PADW:], cnt[e, i, :], ALU.mult)
                pool.drain()
                for n in range(4):
                    i, e = n // 2, slice(HEAD * (n % 2), HEAD * (n % 2 + 1))
                    g.tensor_tensor(win[0][e, i, PADW:], win[n + 1][e, i, PADW:], win[0][e, i, PADW:], ALU.subtract)
                pool.drain().then_inc(S("pool_y"), 1)
            pool_delta(pool, "lat")

        @block.sync
        def _(sp):
            def load(slot, src, n=CH):
                shape = src.shape
                dst = raw[:, slot, 0:n].rearrange("p (k n) -> p k n", k=shape[1])
                sp.dma_start(dst, src).then_inc(landed[slot], 16)

            for m in range(MOD_FIRST):
                if m >= RAW:
                    sp.wait_ge(mod_done, m - RAW + 1)
                load(m % RAW, mod_src[m])
            for c in range(CTX_CHUNKS):
                sp.wait_ge(mod_done, MOD_FIRST - RAW + c + 1)
                load(c, ctx_src[c])
            for m in range(MOD_FIRST, MOD_CHUNKS):
                n = m - MOD_FIRST
                if n < RAW:
                    sp.wait_ge(lo_ready, 2 * (n + 1))
                else:
                    sp.wait_ge(mod_done, m - RAW + 1)
                load(m % RAW, mod_src[m])
            with sp.Fori(0, DEPTH) as layer:
                sp.wait_ge(S("side_free"), layer + 1)
                sp.wait_ge(S("consts"), 16)
                sp.dma_start(p_tok, a["p"][layer, 0].rearrange("(t q) d -> q t d", q=P)).then_inc(S("side_landed"), 16)
                for s in range(2):
                    e = slice(HEAD * s, HEAD * (s + 1))
                    sp.dma_start(pool_w[e, :, e], a["pool_w"][layer].rearrange("(i s) c d -> s c i d", s=2)[s]).then_inc(
                        S("side_landed"), 16)
                for l, src in enumerate(layer_src(layer)):
                    if l != 9:
                        sp.wait_ge(lo_ready, layer * (2 * LAYER_CHUNKS) + 2 * (S_LAYER + l + (l == 8) - RAW + 1))
                    sp.wait_ge(mod_done, min(MOD_CHUNKS - RAW + l + 1, MOD_CHUNKS))
                    load(l % RAW, src, CH // 2 if half_chunk(l) else CH)
            for l, src in enumerate(post_src):
                sp.wait_ge(lo_ready, 2 * (S_POST + l - RAW + 1))
                load(l % RAW, src)
            for c in range(2):
                sp.wait_ge(S(f"y_rows{c}"), 2)
                sp.dma_start(out[0].rearrange("(t p) d -> p t d", p=P)[:, :, 512 * c:512 * (c + 1)],
                             y_rows[:, :, 512 * c:512 * (c + 1)]).then_inc(S("stored"), 16)
            sp.wait_ge(S("stored"), 32)


_INS = ["x", "p", "positions", "w_in", "pool_w", "w_out", "w_up", "w_down", "w_gate", "w_ple", "ctx_2", "w_mod_2", "w_in_2",
        "w_dn_out_2", "w_sc_out_2", "w_fn_out_2", "w_gate_2", "w_o_2", "w_ffn_in_2", "w_ffn_out_2"]


def kernel(**inputs):
    import concourse.bacc as bacc
    from concourse.bass_utils import run_bass_kernel_spmd

    arrays = {name: np.ascontiguousarray(inputs[name]) for name in _INS}
    rows = [np.asarray(inputs[n])[l] for l in range(DEPTH) for n, _ in LAYER_VECS]
    rows += [np.asarray(inputs[n]) for n, _ in TILE_A + TILE_B]
    arrays["vec_rows"] = np.concatenate([r.reshape(-1, P) for r in rows], 0)
    arrays["dn_row"] = np.concatenate([np.asarray(inputs[n]).reshape(1, -1) for n in ("dn_a_log_2", "dn_dt_bias_2")], 1)
    arrays["consts"] = const_tables()
    nc = bacc.Bacc("TRN2", target_bir_lowering=False, num_devices=1, dynamic_dma_scratch_size=1024)
    aps = {n: nc.dram_tensor("in_" + n, v.shape, mybir.dt.from_np(v.dtype), kind="ExternalInput").ap()
           for n, v in arrays.items()}
    out = nc.dram_tensor("out", (1, T, D), F32, kind="ExternalOutput").ap()
    two_blocks(nc, aps, out)
    r = run_bass_kernel_spmd(nc, [{"in_" + n: v for n, v in arrays.items()}], core_ids=[0])
    return r.results[0]["out"]
```

```python
from contextlib import ExitStack

import numpy as np

import concourse.bass as bass
from concourse import mybir

F32 = mybir.dt.float32
F32R = mybir.dt.float32r
I32 = mybir.dt.int32
ALU = mybir.AluOpType
ACT = mybir.ActivationFunctionType
AX = mybir.AxisListType

P = 128
T = 256
TT = T // P
D = 1024
KT = D // P
DEPTH = 2
HEAD = 64
GROUPS = ((128, 1), (512, 4), (2048, 16))
HPG = 4
POOL_WINDOWS = (2, 4, 8, 16)
ROT = HEAD // 4
THETA = 500000.0
FF = 4096
FF2 = 2816
DN_H = 4
GRID_W = 64
EPS = 1e-6
BIG = 1e30
LEVELS = 7
QSCALE = HEAD ** -0.5
TWO_PI = 2.0 * np.pi
MAGIC = 1.5 * 2.0 ** 23
PI_A = 6.28125
PI_B = 0.0019350051879882812
PI_C = float(TWO_PI - PI_A - PI_B)

RAW = 4
PIECES = 4
CH = 2048
PW = CH // 2

MOD_CHUNKS = 6 * D // 256
MOD_FIRST = 2 * D // 256
CTX_CHUNKS = 4
LAYER_CHUNKS = 52
UPS = FF // 256
SSQ2_AT = 3


def const_columns():
    at, out = 0, {}
    for name, width in (
        ("ident", P), ("ones", P), ("rot", P), ("eps", 1), ("ln_q", 1), ("eps2", 1), ("even", 1), ("inv_freq", 1), ("pad", 1), ("mod_sum", 2),
        ("mask", 3 * 384), ("inv_cnt", 2 * T),
        ("cum0", P), ("cum1", P), ("up0", P), ("up1", P), ("lo0", P), ("lo1", P),
        ("pair0", P), ("pair1", P), ("lvl0", 64 * (LEVELS - 1)), ("lvl1", 64 * (LEVELS - 1)),
        ("dft_cos", 2 * T), ("dft_nsin", 2 * T), ("dft_ch", 2 * P),
    ):
        out[name] = (at, width)
        at += width
    return out, at


def level_columns(d, l):
    f = np.arange(P)
    return f[(f >> l & 1) == (1 - d)]


def const_tables():
    cols, total = const_columns()
    a = np.zeros((P, total), np.float64)

    def put(name, v):
        s, w = cols[name]
        a[:, s:s + w] = v

    p = np.arange(P)[:, None]
    f = np.arange(P)[None, :]
    put("ident", p == f)
    put("ones", 1.0)
    rot = np.zeros((P, P))
    half = ROT // 2
    inv = np.zeros((P, 1))
    for m in range(P):
        d = m % HEAD
        if d < half:
            rot[m + half, m] = -1.0
        elif d < ROT:
            rot[m - half, m] = 1.0
        if d < ROT:
            inv[m, 0] = np.float32(THETA) ** np.float32(-2.0 * (d % half) / ROT)
    put("rot", rot)
    put("inv_freq", inv)
    put("eps", EPS)
    put("eps2", EPS * EPS)
    put("mod_sum", p % 2 == np.arange(2)[None, :])
    put("ln_q", np.log(P ** -0.5))
    mask = np.zeros((P, 3, 384))
    for g, (window, dil) in enumerate(GROUPS):
        for qt in range(TT):
            k = np.arange(P * (qt + 1))[None, :]
            dist = p + P * qt - k
            ok = (dist >= 0) & (dist % dil == 0) & (dist // dil <= window // dil)
            mask[:, g, P * qt:P * qt + k.size] = np.where(ok, 0.0, -BIG)
    put("mask", mask.reshape(P, -1))
    t = np.arange(T)
    cnt = np.zeros((P, 2, T))
    for i in range(2):
        for h in range(2):
            cnt[HEAD * h:HEAD * (h + 1), i] = 1.0 / np.minimum(t + 1, POOL_WINDOWS[2 * i + h])
    put("inv_cnt", cnt.reshape(P, -1))
    put("cum0", p <= f)
    put("cum1", p >= f)
    put("up0", np.where(f >= p, BIG, -BIG))
    put("up1", np.where(f <= p, BIG, -BIG))
    put("lo0", np.where(f < p, -BIG, BIG))
    put("lo1", np.where(f > p, -BIG, BIG))
    put("pair0", (p % 2 == 1) & (f == p - 1))
    put("pair1", (p % 2 == 0) & (f == p + 1))
    for d in range(2):
        lv = np.zeros((P, LEVELS - 1, 64))
        for l in range(1, LEVELS):
            c = level_columns(d, l)[None, :]
            lv[:, l - 1] = (p >> (l + 1) == c >> (l + 1)) & ((p >> l & 1) == d)
        put(f"lvl{d}", lv.reshape(P, -1))
    tt = np.arange(TT)[None, :, None] * P + np.arange(P)[:, None, None]
    ang = TWO_PI * ((tt * t[None, None, :]) % T) / T
    put("dft_cos", (np.cos(ang) / np.sqrt(T)).reshape(P, -1))
    put("dft_nsin", (-np.sin(ang) / np.sqrt(T)).reshape(P, -1))
    ang = TWO_PI * ((p * f) % P) / P
    put("dft_ch", np.concatenate([np.cos(ang), np.sin(ang)], 1) / np.sqrt(P))
    return a.astype(np.float32)


LAYER_VECS = (("norm1", KT), ("norm2", KT), ("norm3", KT), ("pool_scale", 2))
LV = sum(n for _, n in LAYER_VECS)
TILE_A = (("final_norm", KT), ("norm1_g_2", KT), ("norm2_g_2", KT), ("final_g_2", KT),
          ("b_gate_2", 24), ("c_2", KT), ("c_ctx_2", KT))
TILE_B = (("b_mod_2", 48), ("dn_conv_w_2", 36), ("sc_conv_w_2", 12), ("dn_onorm_g_2", 1))


def vec_columns():
    out, at = {}, DEPTH * LV
    for name, n in TILE_A:
        out[name] = at
        at += n
    rows_a = at
    for name, n in TILE_B:
        out[name] = at
        at += n
    return out, rows_a, at


Q2, K2, V2, Z2, BA2, SB2, SC2, SX2, FN2 = 0, 512, 1024, 1536, 2048, 2064, 2576, 3088, 3600


FILL = {"ctx": dict(norm=2, tok=1, T3=1, z1=1, z2=1, z3=1, z4=1, z5=1, z6=1, x1=1, x2=1, x3=1, x4=1, x5=1, u0=1),
        "lat": dict(ba=2, norm=4, T0=1, T1=1, T2=1, T3=1, end=1)}
LAT_FILL = ["z0", "z1"] + [f"sc{c}" for c in range(6)] + ["fn0", "fn1"]


CTX_TOLD = dict(act=8, conv1=8, conv=4, silu=4, ba=1, ba2=1, sq=2, kn=2, rs=2, g=1, gcol=1, ecol=1, bcol=1, tok=1, tg=4,
                dl=4, el=4, T=4, X0=4, X=4 * LEVELS, Z=4 * (LEVELS - 1), T2=4 * (LEVELS - 2), A=4, vb=4, kd=4, uw=4, vnew=2,
                state=4, hi=8, mt=8)


class Banks:

    def __init__(self, full, free):
        self.full, self.free = full, free
        self.uses, self.fulls, self.per = {}, {}, {}
        self.n_use = [0] * 8
        self.n_full = [0] * 8

    def section(self, name, uses, times=1):
        start_u, start_f = list(self.n_use), list(self.n_full)
        for use, bank, own in uses:
            assert (name, use) not in self.uses, use
            self.uses[name, use] = (bank, self.n_use[bank])
            self.fulls[name, use] = (bank, self.n_full[bank] + 1)
            self.n_use[bank] += 1
            self.n_full[bank] += own
        per_u = [b - a for a, b in zip(start_u, self.n_use)]
        per_f = [b - a for a, b in zip(start_f, self.n_full)]
        self.per[name] = (per_u, per_f)
        if times > 1:
            assert all(n > 0 for n in start_u)
            self.n_use = [b + p * (times - 1) for b, p in zip(self.n_use, per_u)]
            self.n_full = [b + p * (times - 1) for b, p in zip(self.n_full, per_f)]

    def bank(self, sec, use):
        return self.uses[sec, use][0]

    def claim(self, eng, sec, use, layer=0):
        b, n = self.uses[sec, use]
        v = n + layer * self.per[sec][0][b]
        if not (isinstance(v, int) and v == 0):
            eng.wait_ge(self.free[b], v)
        return b

    def wait_full(self, eng, sec, use, layer=0):
        b, n = self.fulls[sec, use]
        eng.wait_ge(self.full[b], n + layer * self.per[sec][1][b])
        return b


def bank_schedule(banks):

    def ring(order):
        n = [0]

        def take():
            n[0] += 1
            return order[(n[0] - 1) % len(order)]
        return take

    uses = []
    r = ring([0, 1, 2, 4, 5])
    own = lambda name: uses.append((name, r(), 1))
    lin = lambda name: uses.append((name, r(), 0))
    uses.append(("mod", 3, 0))
    uses.append(("vec", 6, 1))
    for c in range(3):
        own(f"ctx{c}")
    uses.append(("ctx3", 7, 1))
    own("rows")
    own("norm")
    for c in range(4):
        own(f"x{c}")
    delta_uses("ctx", own, lin)
    banks.section("pre", uses)

    uses = []
    low, high = ring([0, 1, 2, 3]), ring([4, 5, 6, 7])
    own = lambda name: uses.append((name, low(), 1))
    lin = lambda name: uses.append((name, high(), 0))
    lin("qk0")
    own("p")
    for c in range(1, 6):
        lin(f"qk{c}")
        if c == 1:
            own("ssq1")
        own(f"rot{c - 1}")
    lin("v0")
    own("rot5")
    for n, after in enumerate(("v1", "u", None)):
        for hd in HEADS[4 * n:4 * n + 4]:
            own(f"s{hd}")
        if after:
            lin(after)
    for kind, x in ATT:
        if kind == "v2":
            lin("v2")
        else:
            own({"T": f"pT{x}", "V": f"pv{x}", "pool": "pool"}[kind])
    for c in range(4):
        lin(f"out{c}")
    lin("up0")
    lin("up1")
    for b in range(4):
        uses.append((f"down{b}", b, 0))
    for j in range(2, UPS):
        lin(f"up{j}")
        if j == SSQ2_AT:
            uses.append(("ssq2", high(), 1))
    for b in range(4):
        uses.append((f"ple{b}", 4 + b, 0))
    for b in range(4):
        if b == 2:
            uses.append(("ssq3", 3, 1))
        uses.append((f"gate{b}", b, 0))
    banks.section("layer", uses, DEPTH)

    uses = []
    r = ring(range(8))
    own = lambda name: uses.append((name, r(), 1))
    lin = lambda name: uses.append((name, r(), 0))
    own("norm1")
    own("final")
    delta_uses("lat", own, lin)
    for g in range(4):
        for t in range(TT):
            own(f"fch{g}{t}")
    own("onorm0")
    own("onorm1")
    for c in range(2):
        own(f"fpos{c}")
    for b in range(3):
        for c in range(4):
            lin(f"gate{b}{c}")
        for c in range(4):
            lin(f"y{b}{c}")
    for c in range(4):
        lin(f"wo{c}")
    own("norm2")
    low, high = ring([0, 1, 2, 3]), ring([4, 5, 6, 7])
    for b in range(4):
        uses.append((f"ffo{b}", b, 0))
    for j in range(FF2 // 256):
        for n in "ab":
            uses.append((f"ff{n}{j}", high(), 0))
    uses.append(("final2", 4, 1))
    for c in range(4):
        own(f"y_out{c}")
    banks.section("post", uses)


def delta_uses(part, own, lin):
    lat = part == "lat"
    for c in range(2 if lat else 0):
        lin("lat_q%d" % c)
    for c in range(2):
        lin(f"{part}_k{c}")
    for c in range(2):
        lin(f"{part}_v{c}")
    fillers = list(LAT_FILL)

    def fill(point):
        for _ in range(FILL["lat"].get(point, 0) if lat else 0):
            lin(fillers.pop(0))

    own(f"{part}_ba")
    fill("ba")
    for c in range(4 if lat else 2):
        own(f"{part}_l2{c}")
    own(f"{part}_cum")
    fill("norm")
    for n in range(TT):
        own(f"{part}_kt{n}")
        own(f"{part}_vt{n}")
    for g in range(4):
        own(f"{part}_grow{g}")
        own(f"{part}_kk{g}")
        if lat:
            own(f"lat_qk{g}")
        fill(f"T{g}")
    for g in range(4):
        own(f"{part}_x0{g}")
    for l in range(1, LEVELS):
        for g in range(4):
            own(f"{part}_z{l}{g}")
        for g in range(4):
            own(f"{part}_xz{l}{g}")
        if l < LEVELS - 1:
            for g in range(4):
                own(f"{part}_t{l}{g}")
    for g in range(4):
        own(f"{part}_u{g}")
        if lat or g in (1, 2):
            own(f"{part}_w{g}")
    for step in range(2):
        for d in range(2):
            if lat or step == 1:
                own(f"{part}_ws{step}{d}")
        for d in range(2):
            if lat:
                own(f"lat_o{step}{d}")
            if step == 0 or not lat:
                own(f"{part}_s{step}{d}")


def heads(b):
    return [HPG * g + 2 * b + i for g in range(3) for i in range(2)]


HEADS = heads(0) + heads(1)


def attention_order():
    pairs = [(b, g) for b in range(2) for g in range(3)]
    out = []
    out.append(("v2", 0))
    for i, (b, g) in enumerate(pairs):
        out += [("T", HPG * g + 2 * b), ("T", HPG * g + 2 * b + 1)]
        if i:
            out.append(("V", 2 * pairs[i - 1][1] + pairs[i - 1][0]))
        if i == 4:
            out.append(("pool", 0))
    return out + [("V", 2 * g + b)]


ATT = attention_order()
T_ORDER = [x for k, x in ATT if k == "T"]
V_ORDER = [x for k, x in ATT if k == "V"]


def group_of(d, step):
    return 2 * d + (step if d == 0 else 1 - step)


def two_blocks(nc, a, out):
    K, NK = const_columns()
    V, ROWS_A, NV = vec_columns()
    with ExitStack() as ctx:
        def sb(name, shape, dt=F32):
            return ctx.enter_context(nc.sbuf_tensor(name, shape, dt))

        sems = {}

        def S(name):
            if name not in sems:
                sems[name] = ctx.enter_context(nc.semaphore(name))
            return sems[name]

        kt = sb("consts_sb", [P, NK])
        vec = sb("vec_cols", [P, NV])
        raw = sb("w_raw", [P, RAW, CH])
        whi = sb("w_hi", [P, PIECES, PW], F32R)
        wlo = sb("w_lo", [P, PIECES, PW], F32R)
        xhi = sb("act_hi", [P, KT, T], F32R)
        xlo = sb("act_lo", [P, KT, T], F32R)
        yhi = sb("side_hi", [P, 4, T], F32R)
        ylo = sb("side_lo", [P, 4, T], F32R)
        phi = sb("ple_hi", [P, 2, T], F32R)
        plo = sb("ple_lo", [P, 2, T], F32R)
        ba_hi = sb("w_ba_hi", [P, KT, 16], F32R)
        ba_lo = sb("w_ba_lo", [P, KT, 16], F32R)
        h = sb("h", [P, KT, T])
        rope_c = sb("rope_cos", [P, T])
        rope_s = sb("rope_sin", [P, T])
        state = sb("state", [P, 2, DN_H, P])
        modc = sb("mod_cols", [P, 48, 2])
        final_g = sb("final_gains", [P, 2, KT])
        gains = sb("mod_gains", [P, 3, KT])
        dn_rows = sb("dn_rows", [P, 16])
        neg_a = sb("neg_exp_a", [P, 8])
        mod_in = sb("silu_c_split", [P, KT, 4], F32R)
        cur_vec = sb("layer_vecs", [P, LV + KT])
        rstd_w = sb("rstd", [P, T + 4])
        rstd = rstd_w[:, 0:T]
        rstd_b = sb("rstd_b", [P, 2 * T])
        ARENA = 22400
        arena = sb("arena", [P, ARENA])
        ps = [ctx.enter_context(nc.psum_tensor(f"bank{b}", [P, 512], F32)) for b in range(8)]

        all_hi, all_lo = ([x[:, k, :] for k in range(KT)] for x in (xhi, xlo))
        in_hi = [yhi[:, k, :] for k in range(4)] + all_hi[4:]
        in_lo = [ylo[:, k, :] for k in range(4)] + all_lo[4:]

        class Arena:

            def __init__(self, at=0):
                self.at = at

            def __call__(self, *shape):
                n = int(np.prod(shape))
                v = arena[:, self.at:self.at + n]
                self.at += n
                assert self.at <= ARENA, self.at
                if len(shape) == 2:
                    v = v.rearrange("p (a b) -> p a b", a=shape[0])
                elif len(shape) == 3:
                    v = v.rearrange("p (a b c) -> p a b c", a=shape[0], b=shape[1])
                return v

        def col(name, i=0, n=1):
            s = K[name][0] + i
            return kt[:, s:s + n]

        def vcol(name, i=0):
            return vec[:, V[name] + i:V[name] + i + 1]

        ident, ones = col("ident", 0, P), col("ones", 0, P)
        eps_col, lnq_col = col("eps"), col("ln_q")

        A = Arena()
        small = A(1280)
        pre_x = A(KT, T)
        sil = A(12, T)
        q_n, k_n, v_n = sil[:, 0:4, :], sil[:, 4:8, :], sil[:, 8:12, :]
        ktok = A(TT, DN_H, P)
        vtok = A(TT, DN_H, P)
        z_n = A(4, T)
        g_A = A(4, 512)
        g_X = A(4, 512)
        g_T = A(4, 512)
        g_dec = A(4, 512)
        g_q = A(4, 512)
        scr = [A(512) for _ in range(3)]
        DELTA_END = A.at
        mod_rows = z_n[:, 2:4, :]
        sc_b, sc_p = pre_x[:, 0:4, :], pre_x[:, 4:8, :]
        fn_u = [kt[:, K["mask"][0] + 512 * c:K["mask"][0] + 512 * (c + 1)].rearrange("p (k t) -> p k t", k=2)
                for c in range(2)]
        g_kd = sil[:, 0:8, :].rearrange("p a b -> p (a b)").rearrange("p (g n) -> p g n", g=4)
        xtok = g_A.rearrange("p a b -> p (a b)").rearrange("p (t d) -> p t d", t=2)
        ctok = g_X.rearrange("p a b -> p (a b)").rearrange("p (t d) -> p t d", t=2)
        xc = g_T.rearrange("p a b -> p (a b)").rearrange("p (k t) -> p k t", k=KT)

        S("landed0"), S("landed1"), S("landed2"), S("landed3")
        landed = [S(f"landed{i}") for i in range(RAW)]
        hi_ready, lo_ready, pieces_done = S("hi_ready"), S("lo_ready"), S("pieces_done")
        banks = Banks([S(f"bank_full{b}") for b in range(8)], [S(f"bank_free{b}") for b in range(8)])
        bank_schedule(banks)
        block = ctx.enter_context(nc.Block())

        def k_all(w, c, n=256):
            return w[:, c:c + n].rearrange("(k p) n -> p k n", p=P)

        def k_rows(w, r, c=0, n=D):
            return w[r:r + 256, c:c + n].rearrange("(k p) n -> p k n", p=P)

        w_in2 = a["w_in_2"][0]
        mod_src = [k_all(a["w_mod_2"][0], 256 * m) for m in range(MOD_CHUNKS)]
        ctx_src = [k_all(w_in2, c) for c in (K2, K2 + 256, V2, V2 + 256)]

        def layer_src(layer):
            w_in, w_out = a["w_in"][layer], a["w_out"][layer]
            w_up, w_down = a["w_up"][layer], a["w_down"][layer]
            src = []
            for g in range(3):
                src += [k_all(w_in, 256 + 768 + 256 * g), k_all(w_in, 256 + 256 * g)]
            v0, v1, v2 = (k_all(w_in, 256 + 1536 + 256 * g) for g in range(3))
            src += [v0, v1, k_all(w_in, 0), v2]
            src += [k_all(w_out, 256 * c) for c in range(4)]
            up = [k_all(w_up, 256 * j) for j in range(UPS)]
            down = [k_rows(w_down, 256 * j) for j in range(UPS)]
            src += up[0:2]
            for j in range(UPS):
                src += [down[j]] + up[j + 2:j + 3]
            src += [k_all(a["w_ple"][layer], 512 * c, 512) for c in range(2)]
            src += [k_all(a["w_gate"][layer], 256 * c) for c in range(4)]
            assert len(src) == LAYER_CHUNKS
            return src

        pre_src = mod_src[:MOD_FIRST] + ctx_src + mod_src[MOD_FIRST:]
        post_src = [k_all(w_in2, c) for c in (0, 256, K2, K2 + 256, V2, V2 + 256, Z2, Z2 + 256)]
        post_src += [k_all(w_in2, c + e) for c in (SB2, SC2, SX2, FN2) for e in (0, 256)]
        for b, name in ((2, "w_fn_out_2"), (1, "w_sc_out_2"), (0, "w_dn_out_2")):
            post_src += [k_all(a["w_gate_2"][0], D * b + 256 * c) for c in range(4)]
            post_src += [k_all(a[name][0], 512 * c, 512) for c in range(2)]
        post_src += [k_all(a["w_o_2"][0], 256 * c) for c in range(4)]
        ffn = []
        for j in range(FF2 // 256):
            ffn += [k_all(a["w_ffn_in_2"][0], 256 * j), k_all(a["w_ffn_in_2"][0], FF2 + 256 * j)]
            if j:
                ffn += [k_rows(a["w_ffn_out_2"][0], 256 * (j - 1))]
        ffn += [k_rows(a["w_ffn_out_2"][0], FF2 - 256)]
        post_src += ffn
        C_LAYER = len(pre_src)
        C_POST = C_LAYER + DEPTH * LAYER_CHUNKS
        C_END = C_POST + len(post_src)
        assert C_LAYER % RAW == LAYER_CHUNKS % RAW == 0

        def half_chunk(local):
            return local in (46, 47)

        class Where:

            def __init__(self, c0, layer=0, per=0, sec="pre"):
                self.c0, self.layer, self.per, self.sec = c0, layer, per, sec

            def pieces(self, l, half=0):
                return self.layer * (2 * self.per) + 2 * (self.c0 + l) + half + 1

            def loads(self, l):
                return self.layer * (16 * self.per // RAW) + 16 * ((self.c0 + l) // RAW + 1)

            def nth(self, n, per):
                return self.layer * per + n

        def width(w, l):
            return PW // 2 if w.sec == "layer" and half_chunk(l) else PW

        def split_hi(act, w, l):
            n = width(w, l)
            for half in range(2):
                slot = (2 * l + half) % PIECES
                if half == 0:
                    act.wait_ge(landed[l % RAW], w.loads(l))
                v = w.pieces(l, half) - PIECES
                if not isinstance(v, int) or v > 0:
                    act.wait_ge(pieces_done, v)
                nc.scalar.activation(whi[:, slot, 0:n], raw[:, l % RAW, n * half:n * (half + 1)],
                                     ACT.Copy).then_inc(hi_ready, 1)

        def split_lo(dve, w, l):
            n = width(w, l)
            for half in range(2):
                slot = (2 * l + half) % PIECES
                dve.wait_ge(hi_ready, w.pieces(l, half))
                nc.vector.tensor_tensor(wlo[:, slot, 0:n], raw[:, l % RAW, n * half:n * (half + 1)],
                                        whi[:, slot, 0:n].bitcast(F32), ALU.subtract).then_inc(lo_ready, 1)

        def ln_exp_tables():
            nc.scalar.preload_act_table_set("natural_log_exp_and_others")

        def three(pe, o, ahi, alo, bhi, blo, start, stop=False):
            nc.tensor.matmul(o, ahi, bhi, start=start, stop=False, skip_group_check=True)
            nc.tensor.matmul(o, ahi, blo, start=False, stop=False, skip_group_check=True)
            return nc.tensor.matmul(o, alo, bhi, start=False, stop=stop, skip_group_check=True)

        def tiles(x, first, n):
            return [x[:, first + i, :] for i in range(n)]

        def project(pe, w, l, out_tile, kts, act_hi, act_lo, wait_act=None, first=True, last=True):
            n = width(w, l)
            kp = max(kts // 2, 1)
            ms = n // kp // P
            for half in range(2):
                slot = (2 * l + half) % PIECES
                pe.wait_ge(lo_ready, w.pieces(l, half))
                for m in range(ms):
                    bank, c = out_tile(m)
                    o = ps[bank][:, c:c + T]
                    for k in range(kp):
                        f = half * kp + k
                        if wait_act and m == 0:
                            wait_act(f)
                        at = k * ms * P + m * P
                        mm = three(pe, o, whi[:, slot, at:at + P], wlo[:, slot, at:at + P],
                                   act_hi[f], act_lo[f],
                                   start=first and half == 0 and k == 0 and c == 0,
                                   stop=last and half == 1 and k == kp - 1)
                mm.then_inc(pieces_done, 1)

        def project_tokens(pe, w, l, bank):
            for half in range(2):
                slot = (2 * l + half) % PIECES
                pe.wait_ge(lo_ready, w.pieces(l, half))
                for t in range(TT):
                    o = ps[bank][:, T * t:T * (t + 1)]
                    for k in range(4):
                        f = 4 * half + k
                        mm = three(pe, o, in_hi[f][:, P * t:P * (t + 1)], in_lo[f][:, P * t:P * (t + 1)],
                                   whi[:, slot, 256 * k:256 * (k + 1)], wlo[:, slot, 256 * k:256 * (k + 1)],
                                   start=half == 0 and k == 0 and t == 0, stop=half == 1 and k == 3)
                mm.then_inc(pieces_done, 1)

        def wide(v, n):
            return v.unsqueeze(1).broadcast_to([P, n, T])

        def per_head(v):
            return v.unsqueeze(2).broadcast_to([P, DN_H, P])

        def all_heads(v):
            return v.unsqueeze(1).broadcast_to([P, DN_H, v.shape[1]])

        def h4(v):
            return v.rearrange("p (h n) -> p h n", h=DN_H)

        def pair(b):
            return ps[b][:, :].rearrange("p (m t) -> p m t", m=2)

        sg = small[:, 0:256]
        ba_beta = sg[:, 0:16].rearrange("p (n c) -> p n c", n=2)
        ba_g = sg[:, 16:32].rearrange("p (n c) -> p n c", n=2)
        ba_t1 = sg[:, 32:48].rearrange("p (n c) -> p n c", n=2)
        ba_t2 = sg[:, 48:64].rearrange("p (n c) -> p n c", n=2)
        gcol = sg[:, 64:80].rearrange("p (g c) -> p g c", g=4)
        gtot = sg[:, 80:96].rearrange("p (g c) -> p g c", g=4)
        kd_col = sg[:, 96:112].rearrange("p (g c) -> p g c", g=4)
        bg_col = sg[:, 112:128].rearrange("p (g c) -> p g c", g=4)
        eg_col = sg[:, 128:144].rearrange("p (g c) -> p g c", g=4)
        et_col = sg[:, 144:160].rearrange("p (g c) -> p g c", g=4)
        z_sm = small[:, 256:1280].rearrange("p (g n) -> p g n", g=4)

        def chunk_of(g):
            return g // 2, g % 2

        def beta_of(g):
            d, n = chunk_of(g)
            return ba_beta[:, n, 4 * d:4 * d + 4]

        def lvl_cols(x, d, l):
            v = x.rearrange("p h (n s b) -> p h n s b", s=2, b=1 << l)
            return v[:, :, :, 1 - d, :]

        def lvl_shape(z, l):
            return z.rearrange("p (h n b) -> p h n b", h=DN_H, b=1 << l)

        def tok(x, n):
            return x[:, :, P * n:P * (n + 1)]

        conv = [scr[0], scr[1]]
        conv_names = {"q": 0, "k": 4, "v": 8}
        ctx_tiles = [("k", 0), ("k", 1), ("v", 0), ("v", 1)]
        lat_tiles = [("q", 0), ("q", 1)] + ctx_tiles

        def tiles_of(part):
            return ctx_tiles if part == "ctx" else lat_tiles

        def steps_of(part):
            return 2

        def filler(part, step):
            left = dict(FILL[part])

            def fill(point, most=None):
                n = left.get(point, 0)
                n = n if most is None else min(n, most)
                left[point] = left.get(point, 0) - n
                for _ in range(n):
                    step()
            return fill

        def pe_delta(pe, part, w, l0, sec, fill):
            lat = part == "lat"
            told = lambda name, n: (S("dn_" + name), n + (CTX_TOLD[name] if lat else 0))
            W = lambda use: banks.wait_full(pe, sec, f"{part}_{use}")
            C = lambda use: banks.claim(pe, sec, f"{part}_{use}")
            F = lambda mm, b: mm.then_inc(banks.full[b], 1)
            l = l0
            for i, (name, c) in enumerate(tiles_of(part)):
                b = C(f"{name}{c}")
                project(pe, w, l, lambda m: (b, T * m), KT, all_hi, all_lo,
                        (lambda f: pe.wait_ge(*told("act", f + 1))) if i == 0 else None)
                l += 1
            b = C("ba")
            pe.wait_ge(S("w_ba_split"), 2)
            for t in range(TT):
                for k in range(KT):
                    mm = three(pe, ps[b][:, 16 * t:16 * t + 16], xhi[:, k, P * t:P * (t + 1)],
                               xlo[:, k, P * t:P * (t + 1)], ba_hi[:, k, :], ba_lo[:, k, :],
                               start=k == 0, stop=k == KT - 1)
            F(mm, b)
            fill("ba")
            for i in range(4 if lat else 2):
                pe.wait_ge(*told("sq", i + 1))
                b = C(f"l2{i}")
                F(nc.tensor.matmul(ps[b][:, :], ones, scr[i % 2], start=True, stop=True), b)
            pe.wait_ge(*told("g", 1))
            b = C("cum")
            for g in range(4):
                d, n = chunk_of(g)
                gg = ba_g[:, n, 4 * d:4 * d + 4]
                nc.tensor.matmul(ps[b][:, 4 * g:4 * g + 4], col(f"cum{d}", 0, P), gg, start=True, stop=True)
                mm = nc.tensor.matmul(ps[b][:, 16 + 4 * g:20 + 4 * g], ones, gg, start=True, stop=True)
            F(mm, b)
            fill("norm")
            for n in range(TT):
                pe.wait_ge(*told("kn", 2))
                b = C(f"kt{n}")
                for hh in range(DN_H):
                    mm = nc.tensor.transpose(ps[b][:, P * hh:P * (hh + 1)], k_n[:, hh, P * n:P * (n + 1)], ident)
                F(mm, b)
                b = C(f"vt{n}")
                for hh in range(DN_H):
                    mm = nc.tensor.transpose(ps[b][:, P * hh:P * (hh + 1)], v_n[:, hh, P * n:P * (n + 1)], ident)
                F(mm, b)
            fill("tok")
            for g in range(4):
                d, n = chunk_of(g)
                pe.wait_ge(*told("tg", g + 1))
                b = C(f"grow{g}")
                F(nc.tensor.matmul(ps[b][:, :], ones, g_X[:, g, :], start=True, stop=True), b)
                b = C(f"kk{g}")
                for hh in range(DN_H):
                    kk = k_n[:, hh, P * n:P * (n + 1)]
                    mm = nc.tensor.matmul(ps[b][:, P * hh:P * (hh + 1)], kk, kk, start=True, stop=True)
                F(mm, b)
                if lat:
                    b = C(f"qk{g}")
                    if g == 0:
                        pe.wait_ge(S("lat_qn"), 2)
                    for hh in range(DN_H):
                        mm = nc.tensor.matmul(ps[b][:, P * hh:P * (hh + 1)], k_n[:, hh, P * n:P * (n + 1)],
                                              q_n[:, hh, P * n:P * (n + 1)], start=True, stop=True)
                    F(mm, b)
                fill(f"T{g}")
            for g in range(4):
                pe.wait_ge(*told("T", g + 1))
                b = C(f"x0{g}")
                for hh in range(DN_H):
                    mm = nc.tensor.transpose(ps[b][:, P * hh:P * (hh + 1)], h4(g_T[:, g, :])[:, hh, :], ident)
                F(mm, b)
            for lv in range(1, LEVELS):
                for g in range(4):
                    d, n = chunk_of(g)
                    pe.wait_ge(*told("X", 4 * (lv - 1) + g + 1))
                    b = C(f"z{lv}{g}")
                    xs = lvl_cols(h4(g_X[:, g, :]), d, lv)
                    for hh in range(DN_H):
                        mm = nc.tensor.matmul(ps[b][:, 64 * hh:64 * (hh + 1)], h4(g_A[:, g, :])[:, hh, :],
                                              xs[:, hh], start=True, stop=True)
                    F(mm, b)
                fill(f"z{lv}")
                for g in range(4):
                    pe.wait_ge(*told("Z", 4 * (lv - 1) + g + 1))
                    if lv > 1:
                        pe.wait_ge(*told("T2", 4 * (lv - 2) + g + 1))
                    b = C(f"xz{lv}{g}")
                    for hh in range(DN_H):
                        mm = nc.tensor.matmul(ps[b][:, 64 * hh:64 * (hh + 1)], h4(g_T[:, g, :])[:, hh, :],
                                              z_sm[:, g, 64 * hh:64 * (hh + 1)], start=True, stop=True)
                    F(mm, b)
                fill(f"x{lv}")
                if lv < LEVELS - 1:
                    for g in range(4):
                        pe.wait_ge(*told("X", 4 * lv + g + 1))
                        b = C(f"t{lv}{g}")
                        for hh in range(DN_H):
                            mm = nc.tensor.transpose(ps[b][:, P * hh:P * (hh + 1)], h4(g_X[:, g, :])[:, hh, :], ident)
                        F(mm, b)
            for g in range(4):
                pe.wait_ge(*told("X", 4 * (LEVELS - 1) + g + 1))
                pe.wait_ge(*told("vb", g + 1))
                b = C(f"u{g}")
                for hh in range(DN_H):
                    mm = nc.tensor.matmul(ps[b][:, P * hh:P * (hh + 1)], h4(g_X[:, g, :])[:, hh, :],
                                          h4(scr_vb(g))[:, hh, :], start=True, stop=True)
                F(mm, b)
                if lat or g in (1, 2):
                    b = C(f"w{g}")
                    for hh in range(DN_H):
                        mm = nc.tensor.matmul(ps[b][:, P * hh:P * (hh + 1)], h4(scr_kb(g))[:, hh, :],
                                              h4(g_X[:, g, :])[:, hh, :], start=True, stop=True)
                    F(mm, b)
                fill(f"u{g}")
            ns = 0
            for step in range(2):
                for d in range(2):
                    g = group_of(d, step)
                    if lat or step == 1:
                        if step == 1:
                            pe.wait_ge(*told("state", d + 1))
                        elif lat:
                            pe.wait_ge(S("dn_state"), 4)
                        pe.wait_ge(*told("uw", 4))
                        b = C(f"ws{step}{d}")
                        for hh in range(DN_H):
                            mm = nc.tensor.matmul(ps[b][:, P * hh:P * (hh + 1)], h4(g_T[:, g, :])[:, hh, :],
                                                  state[:, d, hh, :], start=True, stop=True)
                        F(mm, b)
                for d in range(2):
                    g = group_of(d, step)
                    vnew = h4(g_A[:, g, :])
                    pe.wait_ge(*told("uw", 4))
                    if lat or step == 1:
                        ns += 1
                        pe.wait_ge(*told("vnew", ns))
                    if lat:
                        if step == 0 and d == 0:
                            pe.wait_ge(S("lat_qg"), 4)
                            pe.wait_ge(S("lat_attn"), 4)
                        b = C(f"o{step}{d}")
                        for hh in range(DN_H):
                            o = ps[b][:, P * hh:P * (hh + 1)]
                            nc.tensor.matmul(o, state[:, d, hh, :], h4(g_q[:, g, :])[:, hh, :], start=True, stop=False)
                            mm = nc.tensor.matmul(o, vnew[:, hh, :], h4(g_dec[:, g, :])[:, hh, :],
                                                  start=False, stop=True)
                        F(mm, b)
                    if step == 0 or not lat:
                        pe.wait_ge(*told("kd", 4))
                        b = C(f"s{step}{d}")
                        for hh in range(DN_H):
                            mm = nc.tensor.matmul(ps[b][:, P * hh:P * (hh + 1)], h4(g_kd[:, g, :])[:, hh, :],
                                                  vnew[:, hh, :], start=True, stop=True)
                        F(mm, b)
            return l

        def scr_vb(g):
            return g_vb[:, g % 2, :]

        def scr_kb(g):
            return g_kb[:, g % 2, :]

        g_vb = sil.rearrange("p a b -> p (a b)")[:, 2048:3072].rearrange("p (g n) -> p g n", g=2)
        g_kb = z_kb = Arena(DELTA_END)(2, 512)

        def act_delta(act, part, w, l0, sec, fill):
            lat = part == "lat"
            told = lambda name, n: (S("dn_" + name), n + (CTX_TOLD[name] if lat else 0))
            W = lambda use: banks.wait_full(act, sec, f"{part}_{use}")
            bank = lambda use: banks.bank(sec, f"{part}_{use}")
            free = lambda ins, b: ins.then_inc(banks.free[b], 1)
            l = l0
            ahead = 2 if lat else 1
            for n in range(1, ahead):
                split_hi(act, w, l + n)
            for i, (name, c) in enumerate(tiles_of(part)):
                if not lat:
                    split_hi(act, w, l + ahead)
                b = bank(f"{name}{c}")
                act.wait_ge(pieces_done, w.pieces(l, 1))
                if i >= 2:
                    act.wait_ge(*told("silu", i - 1))
                tile = conv_names[name] + 2 * c
                for m in range(2):
                    nc.scalar.activation(conv[i % 2][:, T * m:T * (m + 1)], ps[b][:, T * m:T * (m + 1)],
                                         ACT.Identity, scale=vcol("dn_conv_w_2", 12 + tile + m)).then_inc(
                                             S("dn_conv1"), 1)
                if lat and i < len(tiles_of(part)) - 1:
                    split_hi(act, w, l + ahead)
                act.wait_ge(*told("conv", i + 1))
                nc.scalar.activation(sil[:, tile:tile + 2, :], conv[i % 2].rearrange("p (m t) -> p m t", m=2),
                                     ACT.Silu).then_inc(S("dn_silu"), 1)
                l += 1
            ln_exp_tables()
            fill("ba")
            act.wait_ge(*told("ba", 1))
            nc.scalar.activation(ba_t1, ba_t1, ACT.Exp, scale=-1.0)
            nc.scalar.activation(ba_t2, ba_t2, ACT.Exp, scale=-1.0)
            act.drain()
            nc.scalar.activation(ba_t2, ba_t2, ACT.Ln, bias=1.0).then_inc(S("dn_ba2"), 1)
            for i in range(4 if lat else 2):
                b = W(f"l2{i}")
                if i >= 1:
                    act.wait_ge(*(told("kn", i) if not lat else told("kn", i - 2) if i > 2 else (S("lat_qn"), i)))
                free(nc.scalar.activation(rstd_b[:, :], ps[b][:, :], ACT.Ln, bias=eps_col), b)
                act.drain()
                if lat and i < 2:
                    nc.scalar.activation(rstd_b[:, :], rstd_b[:, :], ACT.Exp, scale=-0.5, bias=lnq_col).then_inc(
                        S("dn_rs"), 1)
                else:
                    nc.scalar.activation(rstd_b[:, :], rstd_b[:, :], ACT.Exp, scale=-0.5).then_inc(S("dn_rs"), 1)
                fill("norm", 1)
            fill("norm")
            act.wait_ge(*told("gcol", 1))
            nc.scalar.activation(eg_col, gcol, ACT.Exp)
            nc.scalar.activation(kd_col, kd_col, ACT.Exp)
            nc.scalar.activation(et_col, gtot, ACT.Exp)
            act.drain().then_inc(S("dn_ecol"), 1)
            for n in range(TT):
                b = W(f"kt{n}")
                free(nc.scalar.activation(ktok[:, n], h4(ps[b][:, :]), ACT.Copy), b)
                b = W(f"vt{n}")
                free(nc.scalar.activation(vtok[:, n], h4(ps[b][:, :]), ACT.Copy), b)
            act.drain().then_inc(S("dn_tok"), 1)
            fill("tok")
            for g in range(4):
                if lat:
                    b = W(f"grow{g}")
                    nc.scalar.activation(g_q[:, g, :], ps[b][:, :], ACT.Exp).then_inc(S("lat_egrow"), 1)
                act.wait_ge(*told("dl", g + 1))
                nc.scalar.activation(scr[1], scr[1], ACT.Exp, scale=-1.0).then_inc(S("dn_el"), 1)
                if lat:
                    act.wait_ge(S("lat_du"), g + 1)
                    nc.scalar.activation(g_dec[:, g, :], g_dec[:, g, :], ACT.Exp).then_inc(S("lat_eu"), 1)
                fill(f"T{g}")
            fill("end")
            for g in range(4):
                b = W(f"x0{g}")
                free(nc.scalar.activation(g_X[:, g, :], ps[b][:, :], ACT.Copy), b)
                act.drain().then_inc(S("dn_X0"), 1)
            for lv in range(1, LEVELS):
                fill(f"z{lv}")
                fill(f"x{lv}")
                for g in range(4 if lv < LEVELS - 1 else 0):
                    b = W(f"t{lv}{g}")
                    free(nc.scalar.activation(g_T[:, g, :], ps[b][:, :], ACT.Copy), b)
                    act.drain().then_inc(S("dn_T2"), 1)
            for g in range(4):
                b = W(f"u{g}")
                free(nc.scalar.activation(g_A[:, g, :], ps[b][:, :], ACT.Copy), b)
                if lat or g in (1, 2):
                    b = W(f"w{g}")
                    free(nc.scalar.activation(g_T[:, g, :], ps[b][:, :], ACT.Copy), b)
                act.drain().then_inc(S("dn_uw"), 1)
                fill(f"u{g}")

        def dve_delta(dve, part, w, l0, sec, fill):
            lat = part == "lat"
            told = lambda name, n: (S("dn_" + name), n + (CTX_TOLD[name] if lat else 0))
            W = lambda use: banks.wait_full(dve, sec, f"{part}_{use}")
            bank = lambda use: banks.bank(sec, f"{part}_{use}")
            free = lambda ins, b: ins.then_inc(banks.free[b], 1)
            row = GRID_W if lat else T
            l = l0
            for i, (name, c) in enumerate(tiles_of(part)):
                split_lo(dve, w, l + 1)
                b = bank(f"{name}{c}")
                tile = conv_names[name] + 2 * c
                view = lambda v: v.rearrange("p (r w) -> p r w", w=row)
                dve.wait_ge(*told("conv1", 2 * i + 2))
                for m in range(2):
                    y, x = view(conv[i % 2][:, T * m:T * (m + 1)]), view(ps[b][:, T * m:T * (m + 1)])
                    nc.vector.scalar_tensor_tensor(y[:, :, 1:row], x[:, :, 0:row - 1], vcol("dn_conv_w_2", tile + m),
                                                   y[:, :, 1:row], ALU.mult, ALU.add)
                dve.drain()
                for m in range(2):
                    y, x = view(conv[i % 2][:, T * m:T * (m + 1)]), view(ps[b][:, T * m:T * (m + 1)])
                    ins = nc.vector.scalar_tensor_tensor(y[:, :, 0:row - 1], x[:, :, 1:row],
                                                         vcol("dn_conv_w_2", 24 + tile + m), y[:, :, 0:row - 1],
                                                         ALU.mult, ALU.add)
                free(ins, b)
                dve.drain().then_inc(S("dn_conv"), 1)
                l += 1
            fill("ba")
            b = W("ba")
            ba = ps[b][:, 0:32].rearrange("p (n c) -> p n c", n=2)
            two = lambda v: v.unsqueeze(1).broadcast_to([P, 2, 8])
            nc.vector.tensor_scalar(ba_t1, ba[:, :, 0:8], -88.0, None, ALU.max)
            free(nc.vector.tensor_tensor(ba_g, ba[:, :, 8:16], two(dn_rows[:, 8:16]), ALU.add), b)
            dve.drain()
            nc.vector.tensor_scalar(ba_t2, ba_g, -1.0, None, ALU.mult)
            dve.drain()
            nc.vector.tensor_tensor(ba_t2, ba_t2, ba_g, ALU.max)
            dve.drain().then_inc(S("dn_ba"), 1)
            nq = 4 if lat else 2
            first = 0 if lat else 4
            dve.wait_ge(*told("silu", len(tiles_of(part))))
            for i in range(nq):
                v = sil[:, first + 2 * i:first + 2 * i + 2, :]
                if i >= 2:
                    W(f"l2{i - 2}")
                nc.vector.tensor_tensor(scr[i % 2].rearrange("p (m t) -> p m t", m=2), v, v, ALU.mult).then_inc(
                    S("dn_sq"), 1)
            dve.wait_ge(*told("ba2", 1))
            nc.vector.tensor_scalar(ba_t1, ba_t1, 1.0, None, ALU.add)
            nc.vector.scalar_tensor_tensor(ba_g, ba_g, 0.0, ba_t2, ALU.max, ALU.add)
            dve.drain()
            nc.vector.reciprocal(ba_beta, ba_t1)
            nc.vector.tensor_tensor(ba_g, ba_g, two(neg_a[:, :]), ALU.mult)
            dve.drain().then_inc(S("dn_g"), 1)
            for i in range(nq):
                v = sil[:, first + 2 * i:first + 2 * i + 2, :]
                dve.wait_ge(*told("rs", i + 1))
                nc.vector.tensor_tensor(v, v, rstd_b[:, :].rearrange("p (m t) -> p m t", m=2), ALU.mult).then_inc(
                    S("lat_qn" if lat and i < 2 else "dn_kn"), 1)
                fill("norm", 1)
            fill("norm")
            b = W("cum")
            both = ps[b][:, 0:32].rearrange("p (s g c) -> p s g c", s=2, g=4)
            nc.vector.tensor_copy(gcol, both[:, 0])
            free(nc.vector.tensor_copy(gtot, both[:, 1]), b)
            dve.drain()
            nc.vector.tensor_tensor(kd_col, gtot, gcol, ALU.subtract)
            dve.drain().then_inc(S("dn_gcol"), 1)
            dve.wait_ge(*told("ecol", 1))
            for g in range(4):
                nc.vector.tensor_tensor(bg_col[:, g, :], beta_of(g), eg_col[:, g, :], ALU.mult)
            dve.drain().then_inc(S("dn_bcol"), 1)
            fill("tok")
            for g in range(4):
                d, n = chunk_of(g)
                b = W(f"grow{g}")
                if lat:
                    dve.wait_ge(S("lat_egrow"), g + 1)
                free(nc.vector.tensor_tensor(h4(scr[0]), h4(ps[b][:, :]), per_head(gcol[:, g, :]), ALU.subtract), b)
                dve.drain()
                nc.vector.tensor_tensor(h4(scr[1]), h4(scr[0]), all_heads(col(f"lo{d}", 0, P)), ALU.max).then_inc(
                    S("dn_dl"), 1)
                if lat:
                    nc.vector.tensor_tensor(h4(g_dec[:, g, :]), h4(scr[0]), all_heads(col(f"up{d}", 0, P)),
                                            ALU.min).then_inc(S("lat_du"), 1)
                b = W(f"kk{g}")
                dve.wait_ge(*told("el", g + 1))
                for hh in range(DN_H):
                    one = slice(P * hh, P * (hh + 1))
                    ins = nc.vector.scalar_tensor_tensor(g_A[:, g, one], ps[b][:, one], beta_of(g)[:, hh:hh + 1],
                                                         scr[1][:, one], ALU.mult, ALU.mult)
                free(ins, b)
                dve.drain().then_inc(S("dn_A"), 1)
                if lat:
                    b = W(f"qk{g}")
                    dve.wait_ge(S("lat_eu"), g + 1)
                    free(nc.vector.tensor_tensor(g_dec[:, g, :], ps[b][:, :], g_dec[:, g, :], ALU.mult), b)
                    dve.drain().then_inc(S("lat_attn"), 1)
                fill(f"T{g}")
            for g in range(4):
                dve.wait_ge(*told("X0", g + 1))
                dve.drain().then_inc(S("dn_X"), 1)
            for lv in range(1, LEVELS):
                for g in range(4):
                    d, n = chunk_of(g)
                    b = W(f"z{lv}{g}")
                    m = col(f"lvl{d}", 64 * (lv - 1), 64)
                    free(nc.vector.tensor_tensor(z_sm[:, g, :].rearrange("p (h c) -> p h c", h=DN_H),
                                                 ps[b][:, 0:256].rearrange("p (h c) -> p h c", h=DN_H),
                                                 all_heads(m), ALU.mult), b)
                    dve.drain().then_inc(S("dn_Z"), 1)
                fill(f"z{lv}")
                for g in range(4):
                    d, n = chunk_of(g)
                    b = W(f"xz{lv}{g}")
                    z4 = lvl_shape(ps[b][:, 0:256], lv)
                    for hh in range(DN_H):
                        xs = lvl_cols(h4(g_X[:, g, :]), d, lv)[:, hh]
                        ins = nc.vector.tensor_tensor(xs, xs, z4[:, hh], ALU.subtract)
                    free(ins, b)
                    dve.drain().then_inc(S("dn_X"), 1)
                fill(f"x{lv}")
            fill("u0")
            nv = 0
            for step in range(2):
                for d in range(2):
                    g = group_of(d, step)
                    if lat or step == 1:
                        b = W(f"ws{step}{d}")
                        dve.wait_ge(*told("uw", 4))
                        free(nc.vector.tensor_tensor(g_A[:, g, :], g_A[:, g, :], ps[b][:, :], ALU.subtract), b)
                        dve.drain().then_inc(S("dn_vnew"), 1)
                for d in range(2):
                    g = group_of(d, step)
                    if lat:
                        b = W(f"o{step}{d}")
                        n = g % 2
                        o = tok(o_n, n)
                        if step == 0:
                            free(nc.vector.tensor_copy(o, h4(ps[b][:, :])), b)
                        else:
                            free(nc.vector.tensor_tensor(o, o, h4(ps[b][:, :]), ALU.add), b)
                        dve.drain()
                    if step == 0 or not lat:
                        b = W(f"s{step}{d}")
                        st = state[:, d]
                        if step == 0 and not lat:
                            free(nc.vector.tensor_copy(st, h4(ps[b][:, :])), b)
                        else:
                            nc.vector.tensor_tensor(st, st, per_head(et_col[:, g, :]), ALU.mult)
                            dve.drain()
                            free(nc.vector.tensor_tensor(st, st, h4(ps[b][:, :]), ALU.add), b)
                        dve.drain().then_inc(S("dn_state"), 1)

        o_n = v_n

        def pool_delta(pool, part):
            lat = part == "lat"
            told = lambda name, n: (S("dn_" + name), n + (CTX_TOLD[name] if lat else 0))
            g_v = nc.gpsimd
            pool.wait_ge(*told("g", 1))
            for g in range(4):
                d, n = chunk_of(g)
                g_v.tensor_tensor(h4(g_X[:, g, :]), all_heads(col(f"cum{d}", 0, P)),
                                  per_head(ba_g[:, n, 4 * d:4 * d + 4]), ALU.mult).then_inc(S("dn_tg"), 1)
            for g in range(4):
                d, n = chunk_of(g)
                pool.wait_ge(*told("A", g + 1))
                g_v.tensor_tensor(h4(scr[2]), h4(g_A[:, g, :]), all_heads(col(f"pair{d}", 0, P)), ALU.mult)
                pool.drain()
                g_v.tensor_tensor(h4(g_T[:, g, :]), all_heads(ident), h4(scr[2]), ALU.subtract)
                pool.drain().then_inc(S("dn_T"), 1)
            pool.wait_ge(*told("ecol", 1))
            pool.wait_ge(*told("tok", 1))
            if lat:
                pool.wait_ge(S("lat_qn"), 2)
                for g in range(4):
                    d, n = chunk_of(g)
                    pool.wait_ge(S("lat_egrow"), g + 1)
                    g_v.tensor_tensor(h4(g_q[:, g, :]), tok(q_n, n), h4(g_q[:, g, :]), ALU.mult).then_inc(
                        S("lat_qg"), 1)
                pool.wait_ge(S("lat_attn"), 4)
                pool.drain()
            for g in range(4):
                d, n = chunk_of(g)
                g_v.tensor_tensor(h4(g_kd[:, g, :]), ktok[:, n], per_head(kd_col[:, g, :]), ALU.mult).then_inc(
                    S("dn_kd"), 1)
            pool.wait_ge(*told("bcol", 1))
            for g in range(4):
                d, n = chunk_of(g)
                if g >= 2:
                    pool.wait_ge(*told("uw", g - 1))
                g_v.tensor_tensor(h4(scr_vb(g)), vtok[:, n], per_head(beta_of(g)), ALU.mult)
                g_v.tensor_tensor(h4(scr_kb(g)), ktok[:, n], per_head(bg_col[:, g, :]), ALU.mult)
                pool.drain().then_inc(S("dn_vb"), 1)

        L = Arena()
        q_r, k_r = L(6, T), L(6, T)
        v_t = L(TT, 768)
        z_raw = [L(2, T) for _ in range(2)]
        z_cos = [L(2, T) for _ in range(2)]
        z_sin = [L(2, T) for _ in range(2)]
        tab_c, tab_s = L(T), L(T)
        prob = L(12, 384)
        probT = L(4, 384)
        stat = L(8, 24)
        mx, sm, nb, dm, ex, wl, fac = (stat[:, i, :].rearrange("p (g b i q) -> p g b i q", g=3, b=2, i=2)
                                       for i in range(7))
        top = stat[:, 7, 0:8].rearrange("p (b n) -> p b n", b=2)
        tot = stat[:, 7, 8:16].rearrange("p (b n) -> p b n", b=2)
        rtot = stat[:, 7, 16:24].rearrange("p (b n) -> p b n", b=2)
        PADW = 16
        win = [L(2, PADW + T) for _ in range(5)]
        p_tok = L(TT, 256)
        red = L(T)
        relu = [L(2, T) for _ in range(2)]
        relu2 = [L(2, T) for _ in range(2)]
        sq = prob.rearrange("p a b -> p (a b)")[:, 0:KT * T].rearrange("p (k t) -> p k t", k=KT)
        update = relu + relu2
        rstd_col = rstd_b[:, 0:2]
        inv_ms = rstd_b[:, T:2 * T]

        def up_at(j):
            return 14 + j if j < 2 else 13 + 2 * j

        def down_at(j):
            return 16 + 2 * j if j < UPS - 1 else 45

        KIND = {up_at(j): ("up", j) for j in range(UPS)} | {down_at(j): ("down", j) for j in range(UPS)}

        def layer_where(layer):
            w = Where(C_LAYER, layer, LAYER_CHUNKS, "layer")
            return w

        pre_w = Where(0)
        post_w = Where(C_POST, sec="post")

        def more(w, l):
            return w.c0 + l + 1 < C_END

        first_tables = K["mask"][0]
        rows_ab = scr[0][:, 0:256]
        pos_i = scr[0][0:1, 256:512].bitcast(I32)
        w_ba = scr[2][:, 0:128].rearrange("p (k n) -> p k n", k=KT)
        pos_f = scr[2][0:1, 128:384]
        dn_row = scr[2][0:1, 384:400]
        silu_c = sg[:, 160:176].rearrange("p (j k) -> p j k", j=2)
        pool_w = sb("pool_blocks", [P, 2, P])

        two_k = lambda g, i: g.rearrange("p a b -> p (a b)")[:, 1024 * i:1024 * (i + 1)].rearrange(
            "p (k t) -> p k t", k=4)
        sc_y = two_k(g_X, 1)
        h_sq = g_A.rearrange("p a b -> p (a b)").rearrange("p (k t) -> p k t", k=KT)
        fn_ch = g_dec.rearrange("p a b -> p (a b)").rearrange("p (t g n) -> p t g n", t=2, g=4)
        gate = g_q.rearrange("p a b -> p (a b)").rearrange("p (k t) -> p k t", k=KT)
        merged = pre_x
        y_rows = xtok
        mt = xc
        ff_s = [scr[0].rearrange("p (m t) -> p m t", m=2), scr[1].rearrange("p (m t) -> p m t", m=2)]
        ff_p = [z_kb[:, i, :].rearrange("p (m t) -> p m t", m=2) for i in range(2)]

        @block.tensor
        def _(pe):
            claim = lambda sec, use, layer=0: banks.claim(pe, sec, use, layer)
            full = lambda mm, b: mm.then_inc(banks.full[b], 1)
            tr = lambda o, x: nc.tensor.transpose(o, x, ident)
            mods = [0]

            def mod_columns(m):
                pe.wait_ge(S("mod_copied"), m + 1)
                for i in range(2):
                    c = 2 * (2 * m + i)
                    mm = nc.tensor.matmul(ps[3][:, c:c + 2], mod_rows[0:4, m % 2, P * i:P * (i + 1)],
                                          col("mod_sum", 0, 2)[0:4, :], start=True, stop=True)
                mm.then_inc(S("mod_cols"), 1)

            def mod_chunk():
                m = mods[0]
                mods[0] += 1
                if 2 <= m < MOD_FIRST or m >= MOD_FIRST + 2:
                    mod_columns(m - 2)
                l = m if m < MOD_FIRST else m + CTX_CHUNKS
                o = ps[6 + m % 2][0:4, 0:256]
                for half in range(2):
                    slot = (2 * l + half) % PIECES
                    pe.wait_ge(lo_ready, pre_w.pieces(l, half))
                    for k in range(4):
                        f = 4 * half + k
                        for w in (whi, wlo):
                            mm = nc.tensor.matmul(o, mod_in[:, f, :], w[:, slot, 256 * k:256 * (k + 1)],
                                                  start=f == 0 and w is whi, stop=f == KT - 1 and w is wlo)
                    mm.then_inc(pieces_done, 1)

            pe.wait_ge(S("consts"), 16)
            pe.wait_ge(S("rows_landed"), 16 * 2)
            b = claim("pre", "vec")
            nc.tensor.transpose(ps[b][:, 0:ROWS_A], rows_ab[0:ROWS_A, 0:P], ident[0:ROWS_A, 0:ROWS_A])
            nb_rows = NV - ROWS_A
            full(nc.tensor.transpose(ps[b][:, ROWS_A:NV], rows_ab[0:nb_rows, P:2 * P], ident[0:nb_rows, 0:nb_rows]), b)

            def features_first(name, src):
                pe.wait_ge(S(f"{name}_landed"), 16)
                for c in range(4):
                    b = claim("pre", f"{name}{c}")
                    for i in range(2):
                        for t in range(TT):
                            at = P * (2 * c + i)
                            mm = tr(ps[b][:, T * i + P * t:T * i + P * (t + 1)], src[:, t, at:at + P])
                    full(mm, b)

            features_first("ctx", ctok)
            pe.wait_ge(S("pos_ready"), 1)
            b = claim("pre", "rows")
            nc.tensor.matmul(ps[b][:, 0:T], ones[0:1, :], pos_f, start=True, stop=True)
            full(nc.tensor.matmul(ps[b][:, T:T + 16], ones[0:1, :], dn_row, start=True, stop=True), b)
            pe.wait_ge(S("mod_in"), 1)
            pe.wait_ge(S("xc_ready"), 4)
            for _ in range(2):
                mod_chunk()
            pe.wait_ge(S("pre_ssq"), 1)
            b = claim("pre", "norm")
            full(nc.tensor.matmul(ps[b][:, 0:T], ones, z_n[:, 0, :], start=True, stop=True), b)
            for _ in range(2, MOD_FIRST):
                mod_chunk()
            for m in range(MOD_FIRST - 2, MOD_FIRST):
                mod_columns(m)
            features_first("x", xtok)
            pe_delta(pe, "ctx", pre_w, MOD_FIRST, "pre", filler("ctx", mod_chunk))
            for m in range(MOD_CHUNKS - 2, MOD_CHUNKS):
                mod_columns(m)

            with pe.Fori(0, DEPTH) as layer:
                w = layer_where(layer)
                W = lambda use: banks.wait_full(pe, "layer", use, layer)
                C = lambda use: claim("layer", use, layer)
                wait = lambda name, n, per: pe.wait_ge(S(name), w.nth(n, per))

                def ssq(use, n):
                    wait("ssq_in", n, 3)
                    b = C(use)
                    mm = nc.tensor.matmul(ps[b][:, 0:T], ones, red, start=True, stop=True)
                    if n == 1:
                        for t in range(TT):
                            mm = nc.tensor.matmul(ps[b][:, T + 2 * t:T + 2 * t + 2], red[:, P * t:P * (t + 1)],
                                                  ones[:, 0:2], start=True, stop=True)
                    full(mm, b)

                def rotate(s):
                    wait("z_raw", s + 1, 6)
                    b = C(f"rot{s}")
                    full(nc.tensor.matmul(ps[b][:, :], col("rot", 0, P),
                                          z_raw[s % 2].rearrange("p m t -> p (m t)"), start=True, stop=True), b)

                def scores(n):
                    for hd in HEADS[4 * n:4 * n + 4]:
                        wait("qk_ready", 2 * (hd // HPG) + 2, 6)
                        b = C(f"s{hd}")
                        lo, m = HEAD * (hd % 2), hd // 2
                        qh, kh = q_r[lo:lo + HEAD, m, :], k_r[lo:lo + HEAD, m, :]
                        nc.tensor.matmul(ps[b][:, 0:P], qh[:, 0:P], kh[:, 0:P], start=True, stop=True)
                        full(nc.tensor.matmul(ps[b][:, P:P + T], qh[:, P:T], kh, start=True, stop=True), b)

                for s in range(6):
                    b = C(f"qk{s}")
                    project(pe, w, s, lambda m: (b, T * m), KT, in_hi, in_lo,
                            (lambda f: wait("n1_act", f + 1, KT)) if s == 0 else None)
                    if s == 0:
                        wait("side_landed", 16 * 3, 16 * 3)
                        b = C("p")
                        for k in range(2):
                            for t in range(TT):
                                mm = tr(ps[b][:, T * k + P * t:T * k + P * (t + 1)], p_tok[:, t, P * k:P * (k + 1)])
                        full(mm, b)
                    else:
                        if s == 1:
                            ssq("ssq1", 1)
                        rotate(s - 1)
                b = C("v0")
                project_tokens(pe, w, 6, b)
                rotate(5)
                scores(0)
                b = C("v1")
                project_tokens(pe, w, 7, b)
                scores(1)
                b = C("u")
                project(pe, w, 8, lambda m: (b, T * m), KT, in_hi, in_lo)
                scores(2)
                for kind, x in ATT:
                    if kind == "T":
                        i = T_ORDER.index(x)
                        wait("prob_ready", i + 1, 12)
                        b = C(f"pT{x}")
                        e = prob[:, x, :]
                        tr(ps[b][:, 0:P], e[:, 0:P])
                        tr(ps[b][:, P:2 * P], e[:, P:2 * P])
                        full(tr(ps[b][:, 2 * P:3 * P], e[:, 2 * P:3 * P]), b)
                    elif kind == "V":
                        n = V_ORDER.index(x)
                        wait("probT_ready", 2 * n + 2, 12)
                        wait("v_ready", x // 2 + 1, 3)
                        b = C(f"pv{x}")
                        for i in range(2):
                            hd = 2 * x + i
                            pt = probT[:, T_ORDER.index(hd) % 4, :]
                            vh = v_t[:, :, HEAD * hd:HEAD * (hd + 1)]
                            o = ps[b][HEAD * i:HEAD * (i + 1), :]
                            nc.tensor.matmul(o[:, 0:T], vh[:, 0, :], pt[:, 0:T], start=True, stop=False,
                                             skip_group_check=True)
                            mm = nc.tensor.matmul(o[:, P:T], vh[:, 1, :], pt[:, T:T + P], start=False, stop=True,
                                                  skip_group_check=True)
                        full(mm, b)
                    elif kind == "v2":
                        b = C("v2")
                        project_tokens(pe, w, 9, b)
                    else:
                        wait("pool_y", 1, 1)
                        b = C("pool")
                        for i in range(2):
                            mm = nc.tensor.matmul(ps[b][:, T * i:T * (i + 1)], pool_w[:, i, :],
                                                  win[0][:, i, PADW:], start=True, stop=True)
                        full(mm, b)
                for c in range(4):
                    b = C(f"out{c}")
                    if c == 0:
                        wait("cat_act", 7, 7)
                    project(pe, w, 10 + c, lambda m: (b, T * m), KT, all_hi, all_lo)
                for s in range(14, 46):
                    kind, j = KIND[s]
                    if kind == "up":
                        b = C(f"up{j}")
                        project(pe, w, s, lambda m: (b, T * m), KT, all_hi, all_lo,
                                (lambda f: wait("n2_act", f + 1, KT)) if j == 0 else None)
                        if j == SSQ2_AT:
                            ssq("ssq2", 2)
                    else:
                        if j == 0:
                            for b in range(4):
                                C(f"down{b}")
                        wait("relu_act", j + 1, UPS)
                        project(pe, w, s, lambda m: (m // 2, T * (m % 2)), 2, tiles(yhi, 2 * (j % 2), 2),
                                tiles(ylo, 2 * (j % 2), 2), first=j == 0, last=j == UPS - 1)
                wait("p_act", 1, 1)
                for c in range(2):
                    for i in range(2):
                        C(f"ple{2 * c + i}")
                    project(pe, w, 46 + c, lambda m: (4 + 2 * c + m // 2, T * (m % 2)), 2, tiles(phi, 0, 2), tiles(plo, 0, 2))
                for c in range(4):
                    if c == 2:
                        ssq("ssq3", 3)
                    b = C(f"gate{c}")
                    project(pe, w, 48 + c, lambda m: (b, T * m), KT, all_hi, all_lo,
                            (lambda f: wait("n3_act", f + 1, KT)) if c == 0 else None)

            w = post_w
            C = lambda use: claim("post", use)

            def sum_tiles(use, src, signal, before, per):
                b = C(use)
                for k in range(KT):
                    if k % per == 0:
                        pe.wait_ge(S(signal), before + k // per + 1)
                    mm = nc.tensor.matmul(ps[b][:, 0:T], ones, src[:, k, :], start=k == 0, stop=k == KT - 1)
                full(mm, b)

            b = C("norm1")
            for k in range(KT):
                if k % 2 == 0:
                    if k < 6:
                        pe.wait_ge(S("post_sq"), k // 2 + 1)
                    else:
                        pe.wait_ge(S("post_sq_end"), 1)
                mm = nc.tensor.matmul(ps[b][:, 0:T], ones, pre_x[:, k, :], start=k == 0, stop=k == KT - 1)
            full(mm, b)
            sum_tiles("final", h_sq, "sq_tiles", 0, KT)
            n_tiles = len(lat_tiles)
            left = [0]

            def lat_fill():
                i = left[0]
                left[0] += 1
                b = C(LAT_FILL[i])
                project(pe, w, n_tiles + i, lambda m: (b, T * m), KT, all_hi, all_lo)

            pe_delta(pe, "lat", w, 0, "post", filler("lat", lat_fill))
            l = n_tiles + len(LAT_FILL)
            for g in range(4):
                pe.wait_ge(S("fn_u"), g // 2 + 1)
                for t in range(TT):
                    b = C(f"fch{g}{t}")
                    full(nc.tensor.matmul(ps[b][:, 0:T], fn_u[g // 2][:, g % 2, P * t:P * (t + 1)], col("dft_ch", 0, T),
                                          start=True, stop=True), b)
            for i in range(2):
                pe.wait_ge(S("o_sq"), i + 1)
                b = C(f"onorm{i}")
                full(nc.tensor.matmul(ps[b][:, :], ones, scr[i], start=True, stop=True), b)
            for c in range(2):
                pe.wait_ge(S("fn_ch"), 4 * (c + 1))
                b = C(f"fpos{c}")
                for i in range(2):
                    for t in range(TT):
                        o = ps[b][:, T * i:T * (i + 1)]
                        nc.tensor.matmul(o, fn_ch[:, t, 2 * c + i, 0:P], col("dft_cos", T * t, T),
                                         start=t == 0, stop=False, skip_group_check=True)
                        mm = nc.tensor.matmul(o, fn_ch[:, t, 2 * c + i, P:2 * P], col("dft_nsin", T * t, T),
                                              start=False, stop=t == TT - 1, skip_group_check=True)
                full(mm, b)
            for n in range(3):
                for c in range(4):
                    b = C(f"gate{n}{c}")
                    project(pe, w, l, lambda m: (b, T * m), KT, all_hi, all_lo)
                    l += 1
                pe.wait_ge(S("branch_act"), 2 * (n + 1))
                for i in range(2):
                    y0, y1 = C(f"y{n}{2 * i}"), C(f"y{n}{2 * i + 1}")
                    project(pe, w, l, lambda m: ((y0, y1)[m // 2], T * (m % 2)), 4, tiles(yhi, 0, 4), tiles(ylo, 0, 4))
                    l += 1
            for c in range(4):
                b = C(f"wo{c}")
                project(pe, w, l, lambda m: (b, T * m), KT, all_hi, all_lo,
                        (lambda f: pe.wait_ge(S("merged_act"), f + 1)) if c == 0 else None)
                l += 1
            sum_tiles("norm2", pre_x, "sq_tiles", 1, 2)
            nff = FF2 // 256

            def ffn_out(j, l):
                if j == 0:
                    for b in range(4):
                        C(f"ffo{b}")
                pe.wait_ge(S("ff_act"), j + 1)
                project(pe, w, l, lambda m: (m // 2, T * (m % 2)), 2, tiles(yhi, 2 * (j % 2), 2),
                        tiles(ylo, 2 * (j % 2), 2), first=j == 0, last=j == nff - 1)

            for j in range(nff):
                for x in "ab":
                    b = C(f"ff{x}{j}")
                    project(pe, w, l, lambda m: (b, T * m), KT, all_hi, all_lo,
                            (lambda f: pe.wait_ge(S("n2_act_2"), f + 1)) if j == 0 and x == "a" else None)
                    l += 1
                if j:
                    ffn_out(j - 1, l)
                    l += 1
            ffn_out(nff - 1, l)
            sum_tiles("final2", pre_x, "sq_tiles", 5, 2)
            for half in range(2):
                for t in range(TT):
                    c = 2 * half + t
                    pe.wait_ge(S("y_cols"), 4 * (half + 1))
                    b = C(f"y_out{c}")
                    for k in range(4):
                        mm = tr(ps[b][:, P * k:P * (k + 1)], h[:, 4 * half + k, P * t:P * (t + 1)])
                    full(mm, b)

        @block.scalar
        def _(act):
            full = lambda sec, use, layer=0: banks.wait_full(act, sec, use, layer)
            free = lambda ins, b: ins.then_inc(banks.free[b], 1)

            def rms(b, n, scale, out, power=-0.5, bias=eps_col):
                free(nc.scalar.activation(out, ps[b][:, 0:n], ACT.Ln, scale=scale, bias=bias), b)
                act.drain()
                return nc.scalar.activation(out, out, ACT.Exp, scale=power)

            act.dma_start(ctok, a["ctx_2"][0].rearrange("(t p) d -> p t d", p=P)).then_inc(S("ctx_landed"), 16)
            act.dma_start(pos_i, a["positions"]).then_inc(S("small_landed"), 16)
            act.dma_start(dn_row, a["dn_row"]).then_inc(S("small_landed"), 16)
            act.dma_start(w_ba, k_all(w_in2, BA2, 16)).then_inc(S("small_landed"), 16)
            act.dma_start(xtok, a["x"][0].rearrange("(t p) d -> p t d", p=P)).then_inc(S("x_landed"), 16)
            act.dma_start(kt[:, first_tables:NK], a["consts"][:, first_tables:NK]).then_inc(S("tables"), 16)

            done_chunk = [0]

            def mod_step():
                m = done_chunk[0]
                done_chunk[0] += 1
                split_hi(act, pre_w, (m if m < MOD_FIRST else m + CTX_CHUNKS) + 1)
                if m not in (0, MOD_FIRST):
                    mod_copy(m - 1)
                if m == MOD_CHUNKS - 6:
                    for k in range(KT):
                        nc.scalar.activation(in_hi[k], h[:, k, :], ACT.Identity,
                                             scale=vec[:, k:k + 1]).then_inc(S("n1_hi"), 1)

            def mod_copy(m):
                l = m if m < MOD_FIRST else m + CTX_CHUNKS
                act.wait_ge(pieces_done, pre_w.pieces(l, 1))
                nc.scalar.activation(mod_rows[0:4, m % 2, :], ps[6 + m % 2][0:4, 0:256],
                                     ACT.Copy).then_inc(S("mod_copied"), 1)

            split_hi(act, pre_w, 0)
            b = full("pre", "vec")
            free(nc.scalar.activation(vec[:, :], ps[b][:, 0:NV], ACT.Copy), b)
            act.drain().then_inc(S("vec_ready"), 1)
            cc = V["c_2"]
            nc.scalar.activation(silu_c, vec[:, cc:cc + 16].rearrange("p (j k) -> p j k", j=2), ACT.Silu)
            act.drain()
            ln_exp_tables()
            nc.scalar.activation(mod_in[:, :, 0:2], silu_c.rearrange("p j k -> p k j"), ACT.Copy).then_inc(S("silu_c"), 1)
            mod_step()
            act.wait_ge(S("small_landed"), 48)
            nc.scalar.activation(ba_hi[:, :, :], w_ba, ACT.Copy).then_inc(S("w_ba_hi"), 1)
            for c in range(4):
                b = full("pre", f"ctx{c}")
                free(nc.scalar.activation(xc[:, 2 * c:2 * c + 2, :], pair(b), ACT.Copy), b)
                act.drain().then_inc(S("xc_ready"), 1)
            mod_step()
            b = full("pre", "norm")
            rms(b, T, 1.0 / D, rstd[:, :]).then_inc(S("pre_rstd"), 1)
            act.wait_ge(S("rope_arg"), 1)
            nc.scalar.activation(neg_a[:, :], dn_rows[:, 0:8], ACT.Exp).then_inc(S("exp_a"), 1)
            for _ in range(2, MOD_FIRST):
                mod_step()
            mod_copy(MOD_FIRST - 1)
            for k in range(KT):
                act.wait_ge(S("dn_mt"), k + 1)
                nc.scalar.activation(xhi[:, k, :], mt[:, k, :], ACT.Identity,
                                     bias=modc[:, k, 1:2]).then_inc(S("dn_hi"), 1)
            for c in range(4):
                b = full("pre", f"x{c}")
                free(nc.scalar.activation(h[:, 2 * c:2 * c + 2, :], pair(b), ACT.Copy), b)
            act_delta(act, "ctx", pre_w, MOD_FIRST, "pre", filler("ctx", mod_step))
            mod_copy(MOD_CHUNKS - 1)
            act.wait_ge(S("rope_arg"), 2)
            nc.scalar.activation(rope_s[:, :], rope_s[:, :], ACT.Sin)
            nc.scalar.activation(rope_c[:, :], rope_c[:, :], ACT.Sin)
            act.drain().then_inc(S("rope_done"), 1)
            ln_exp_tables()

            with act.Fori(0, DEPTH) as layer:
                w = layer_where(layer)
                W = lambda use: full("layer", use, layer)
                bank = lambda use: banks.bank("layer", use)
                wait = lambda name, n, per: act.wait_ge(S(name), w.nth(n, per))
                done = lambda s: act.wait_ge(pieces_done, w.pieces(s, 1))

                def norm_hi(name, at, ready, tiles=range(KT), to=all_hi):
                    for k in tiles:
                        ready(k)
                        nc.scalar.activation(to[k], h[:, k, :], ACT.Identity,
                                             scale=cur_vec[:, at + k:at + k + 1]).then_inc(S(name + "_hi"), 1)

                def square_tiles():
                    nc.scalar.activation(sq, h[:, :, :], ACT.Square).then_inc(S("sq_ready"), 1)

                split_hi(act, w, 1)
                act.wait_ge(S("cur_vec"), layer + 1)
                square_tiles()
                b = W("p")
                nc.scalar.activation(phi[:, :, :], pair(b), ACT.Copy).then_inc(S("p_hi"), 1)
                for s in range(6):
                    if s:
                        split_hi(act, w, s + 1)
                    done(s)
                    if s == 1:
                        b = W("ssq1")
                        free(nc.scalar.activation(rstd_w[:, :], ps[b][:, 0:T + 4], ACT.Ln, scale=1.0 / D, bias=eps_col), b)
                        act.drain()
                        nc.scalar.activation(rstd_w[:, :], rstd_w[:, :], ACT.Exp, scale=-0.5).then_inc(S("rstd_1"), 1)
                    if s >= 2:
                        wait("z_cos", s - 1, 6)
                        W(f"rot{s - 2}")
                    free(nc.scalar.activation(z_raw[s % 2], pair(bank(f"qk{s}")), ACT.Copy), bank(f"qk{s}"))
                    act.drain().then_inc(S("z_raw"), 1)

                def values(c):
                    done((6, 7, 9)[c])
                    b = bank(f"v{c}")
                    for t in range(TT):
                        ins = nc.scalar.activation(v_t[:, t, 256 * c:256 * (c + 1)], ps[b][:, T * t:T * (t + 1)],
                                                   ACT.Copy, scale=rstd_w[:, T + 2 * t:T + 2 * t + 1])
                    free(ins, b)
                    act.drain().then_inc(S("v_ready"), 1)

                def exps(first, last):
                    for n in range(first, last):
                        hd = HEADS[n]
                        wait("max_ready", n + 1, 12)
                        g, batch, i = hd // HPG, n // 6, hd % 2
                        for t in range(TT):
                            e = prob[:, hd, P * t:P * t + P * (t + 1)]
                            nc.scalar.activation(e, e, ACT.Exp, scale=QSCALE, bias=nb[:, g, batch, i, t:t + 1],
                                                 accum_out=sm[:, g, batch, i, t:t + 1])
                        if n % 6 == 5:
                            wait("top_ready", batch + 1, 2)
                            nc.scalar.activation(ex[:, :, batch], dm[:, :, batch], ACT.Exp, scale=QSCALE)
                            act.drain().then_inc(S("exp_ready"), 1)

                split_hi(act, w, 7)
                values(0)
                split_hi(act, w, 8)
                exps(0, 4)
                values(1)
                split_hi(act, w, 9)
                exps(4, 8)
                split_hi(act, w, 10)
                exps(8, 12)
                for kind, x in ATT:
                    if kind == "T":
                        i = T_ORDER.index(x)
                        if i >= 4:
                            W(f"pv{V_ORDER[(i - 4) // 2]}")
                        b = W(f"pT{x}")
                        free(nc.scalar.activation(probT[:, i % 4, :], ps[b][:, 0:384], ACT.Copy), b)
                        act.drain().then_inc(S("probT_ready"), 1)
                        if i == 3:
                            split_hi(act, w, 11)
                    elif kind == "V":
                        b = W(f"pv{x}")
                        nc.scalar.activation(xhi[:, 2 + x, :], ps[b][:, 0:T], ACT.Copy).then_inc(S("cat_hi"), 1)
                    elif kind == "v2":
                        values(2)
                    else:
                        b = W("pool")
                        for i in range(2):
                            ins = nc.scalar.activation(xhi[:, i, :], ps[b][:, T * i:T * (i + 1)], ACT.Copy,
                                                       scale=cur_vec[:, 24 + i:25 + i])
                        ins.then_inc(S("cat_hi"), 1)
                for c in range(1, 4):
                    split_hi(act, w, 11 + c)
                done(13)
                norm_hi("n2", KT, lambda k: wait("h2_ready", k // 2 + 1, 4) if k % 2 == 0 else None)
                for s in range(14, 46):
                    split_hi(act, w, s + 1)
                    kind, j = KIND[s]
                    if kind == "down":
                        continue
                    done(s)
                    b = bank(f"up{j}")
                    free(nc.scalar.activation(relu[j % 2], pair(b), ACT.Relu), b)
                    act.drain().then_inc(S("relu"), 1)
                    wait("relu2", j + 1, UPS)
                    nc.scalar.activation(yhi[:, 2 * (j % 2):2 * (j % 2) + 2, :], relu2[j % 2],
                                         ACT.Copy).then_inc(S("relu_hi"), 1)
                    if j == SSQ2_AT - 2:
                        square_tiles()
                    if j == SSQ2_AT:
                        b = W("ssq2")
                        rms(b, T, 1.0 / D, inv_ms, -1.0).then_inc(S("inv_ms"), 1)
                split_hi(act, w, 47)
                split_hi(act, w, 48)
                for c in range(4):
                    norm_hi("n3", 2 * KT, lambda k: wait("h3_ready", k // 2 + 1, 4) if k % 2 == 0 else None,
                            range(2 * c, 2 * c + 2))
                    if c == 1:
                        split_hi(act, w, 49)
                square_tiles()
                split_hi(act, w, 50)
                def next_input(c):
                    norm_hi("n1", LV, lambda k: wait("h1_ready", k // 2 + 1, 4) if k % 2 == 0 else None,
                            range(2 * c, 2 * c + 2), in_hi)

                b = W("ssq3")
                rms(b, T, 1.0 / D, rstd[:, :]).then_inc(S("rstd_3"), 1)
                for c in range(4):
                    if c == 3:
                        split_hi(act, w, 52)
                    wait("gate_in", c + 1, 4)
                    nc.scalar.activation(update[c], update[c], ACT.Sigmoid).then_inc(S("gate_out"), 1)
                    if c == 0:
                        split_hi(act, w, 51)
                    elif c < 3:
                        next_input(c - 1)
                ln_exp_tables()
                done(51)
                next_input(2)
                next_input(3)

            w = post_w
            W = lambda use: full("post", use)
            bank = lambda use: banks.bank("post", use)
            done = lambda l: act.wait_ge(pieces_done, w.pieces(l, 1))
            nxt = lambda l: split_hi(act, w, l + 1) if more(w, l) else None
            act.wait_ge(S("h1_ready"), 4 * DEPTH)
            nc.scalar.activation(h_sq, h[:, :, :], ACT.Square).then_inc(S("sq_tiles"), 1)
            rms(W("norm1"), T, 1.0 / D, rstd[:, :], bias=col("eps2")).then_inc(S("post_rstd"), 1)
            for k in range(KT):
                act.wait_ge(S("dn_mt"), CTX_TOLD["mt"] + k + 1)
                nc.scalar.activation(xhi[:, k, :], mt[:, k, :], ACT.Identity,
                                     bias=modc[:, k, 0:1]).then_inc(S("dn_hi"), 1)
            rms(W("final"), T, 1.0 / D, rope_c[:, :]).then_inc(S("post_rstd"), 1)

            def square_pair(c, n):
                act.wait_ge(S("h_res"), n)
                nc.scalar.activation(pre_x[:, 2 * c:2 * c + 2, :], h[:, 2 * c:2 * c + 2, :],
                                     ACT.Square).then_inc(S("sq_tiles"), 1)

            n_tiles = len(lat_tiles)
            left = [0]

            def lat_fill():
                i = left[0]
                left[0] += 1
                if i < len(LAT_FILL):
                    nxt(n_tiles + i)
                if i:
                    lat_copy(i - 1)

            def lat_copy(i):
                name, c = LAT_FILL[i][:2], int(LAT_FILL[i][-1])
                if name == "sc" and c >= 4:
                    return
                done(n_tiles + i)
                b = bank(LAT_FILL[i])
                two = slice(2 * (c % 2), 2 * (c % 2) + 2)
                if name == "fn":
                    free(nc.scalar.activation(fn_u[c], pair(b), ACT.Copy), b)
                    act.drain().then_inc(S("fn_u"), 1)
                elif name == "sc":
                    free(nc.scalar.activation((sc_b, sc_p)[c // 2][:, two, :], pair(b), ACT.Copy), b)
                    if c == 3:
                        act.drain().then_inc(S("sc_bc"), 1)
                else:
                    free(nc.scalar.activation(z_n[:, two, :], pair(b), ACT.Copy), b)

            act_delta(act, "lat", w, 0, "post", filler("lat", lat_fill))
            l = n_tiles + len(LAT_FILL)
            act.wait_ge(S("sc_p"), 1)
            for k in range(4):
                nc.scalar.activation(sc_y[:, k, :], sc_p[:, k, :], ACT.Identity, scale=vcol("sc_conv_w_2", 4 + k))
            act.drain().then_inc(S("sc_conv1"), 1)
            for g in range(4):
                for t in range(TT):
                    b = W(f"fch{g}{t}")
                    free(nc.scalar.activation(fn_ch[:, t, g, :], ps[b][:, 0:T], ACT.Copy), b)
                    act.drain().then_inc(S("fn_ch"), 1)
            for i in range(2):
                b = W(f"onorm{i}")
                if i:
                    act.wait_ge(S("o_normed"), 1)
                rms(b, 512, 1.0 / P, rstd_b[:, :]).then_inc(S("o_rstd"), 1)
            nc.scalar.activation(z_n, z_n, ACT.Silu).then_inc(S("lat_z"), 1)
            for c in range(2):
                b = W(f"fpos{c}")
                nc.scalar.activation(yhi[:, 2 * c:2 * c + 2, :], pair(b), ACT.Copy).then_inc(S("branch_hi"), 1)
            for n, br in enumerate((2, 1, 0)):
                for c in range(4):
                    nxt(l)
                    done(l)
                    b = bank(f"gate{n}{c}")
                    if n and c == 0:
                        act.wait_ge(S("y_merged"), 4 * n)
                    for m in range(2):
                        ins = nc.scalar.activation(gate[:, 2 * c + m, :], ps[b][:, T * m:T * (m + 1)], ACT.Sigmoid,
                                                   bias=vcol("b_gate_2", KT * br + 2 * c + m))
                    if n == 2 and c == 3:
                        ln_exp_tables()
                    free(ins, b)
                    act.drain().then_inc(S("gate_sig"), 1)
                    if n and c == 0:
                        src = (sc_y, o_n)[n - 1]
                        act.wait_ge(S("sc_done") if n == 1 else S("o_done"), 1)
                        for i in range(2):
                            nc.scalar.activation(yhi[:, 2 * i:2 * i + 2, :], src[:, 2 * i:2 * i + 2, :],
                                                 ACT.Copy).then_inc(S("branch_hi"), 1)
                    l += 1
                for i in range(2):
                    nxt(l)
                    l += 1
            for k in range(KT):
                act.wait_ge(S("y_merged"), 8 + k // 2 + 1)
                nc.scalar.activation(xhi[:, k, :], merged[:, k, :], ACT.Copy).then_inc(S("merged_hi"), 1)
            for c in range(4):
                nxt(l)
                square_pair(c, c + 1)
                l += 1
            rms(W("norm2"), T, 1.0 / D, rstd[:, :]).then_inc(S("post_rstd"), 1)
            for k in range(KT):
                act.wait_ge(S("n2_mt"), k + 1)
                nc.scalar.activation(xhi[:, k, :], mt[:, k, :], ACT.Identity,
                                     bias=modc[:, 24 + k, 0:1]).then_inc(S("n2_hi_2"), 1)
            for j in range(FF2 // 256):
                nxt(l)
                done(l)
                b = bank(f"ffa{j}")
                if j >= 2:
                    act.wait_ge(S("ff_p"), j - 1)
                free(nc.scalar.activation(ff_s[j % 2], pair(b), ACT.Silu), b)
                act.drain().then_inc(S("ff_s"), 1)
                if j == FF2 // 256 - 1:
                    ln_exp_tables()
                l += 1
                nxt(l)
                act.wait_ge(S("ff_p"), j + 1)
                nc.scalar.activation(yhi[:, 2 * (j % 2):2 * (j % 2) + 2, :], ff_p[j % 2], ACT.Copy).then_inc(
                    S("ff_hi"), 1)
                l += 1
                if j:
                    nxt(l)
                    l += 1
            nxt(l)
            for c in range(4):
                square_pair(c, 4 + c + 1)
            rms(W("final2"), T, 1.0 / D, rstd[:, :]).then_inc(S("post_rstd"), 1)
            for c in range(4):
                if c % 2 == 0:
                    b = W(f"y_out{c}")
                    free(nc.scalar.activation(y_rows[:, c % 2, 512 * (c // 2):512 * (c // 2 + 1)], ps[b][:, :],
                                              ACT.Copy), b)
                    act.drain().then_inc(S(f"y_rows{c // 2}"), 1)

        @block.vector
        def _(dve):
            v = nc.vector
            full = lambda sec, use, layer=0: banks.wait_full(dve, sec, use, layer)
            free = lambda ins, b: ins.then_inc(banks.free[b], 1)

            def squares(src, dst, out, name):
                v.tensor_tensor(dst, src, src, ALU.mult)
                dve.drain()
                v.tensor_reduce(out, dst.rearrange("p k t -> p t k"), AX.X, ALU.add).then_inc(S(name), 1)

            def modulated(src, gain, shift, name, act_name, before=0):
                for k in range(KT + 2):
                    if k < KT:
                        v.scalar_tensor_tensor(mt[:, k, :], src[:, k, :], gain(k), rstd[:, :], ALU.mult,
                                               ALU.mult).then_inc(S(name[0]), 1)
                    if k >= 2:
                        dve.wait_ge(S(name[1]), before + k - 1)
                        v.scalar_tensor_tensor(xlo[:, k - 2, :], mt[:, k - 2, :], shift(k - 2),
                                               xhi[:, k - 2, :].bitcast(F32), ALU.add,
                                               ALU.subtract).then_inc(S(act_name), 1)

            def rotary_angles():
                turns = rstd_b[:, 0:T]
                v.tensor_scalar(turns, rope_s[:, :], 1.0 / TWO_PI, MAGIC, ALU.mult, ALU.add)
                dve.drain()
                v.tensor_scalar(turns, turns, MAGIC, None, ALU.subtract)
                for part in (PI_A, PI_B, PI_C):
                    dve.drain()
                    v.scalar_tensor_tensor(rope_s[:, :], turns, -part, rope_s[:, :], ALU.mult, ALU.add)
                dve.drain()
                v.tensor_scalar(rope_c[:, :], rope_s[:, :], np.pi / 2, None, ALU.add)
                dve.drain()
                v.tensor_scalar(turns, rope_c[:, :], np.pi, TWO_PI, ALU.is_gt, ALU.mult)
                dve.drain()
                v.tensor_tensor(rope_c[:, :], rope_c[:, :], turns, ALU.subtract)
                dve.drain()
                edge = 3.1415925
                v.tensor_scalar(rope_c[:, :], rope_c[:, :], edge, -edge, ALU.min, ALU.max)
                v.tensor_scalar(rope_s[:, :], rope_s[:, :], edge, -edge, ALU.min, ALU.max)
                dve.drain().then_inc(S("rope_arg"), 1)

            done_chunk = [0]

            def mod_step():
                m = done_chunk[0]
                done_chunk[0] += 1
                split_lo(dve, pre_w, (m if m < MOD_FIRST else m + CTX_CHUNKS) + 1)
                if m == MOD_CHUNKS - 4:
                    rotary_angles()
                if m == MOD_CHUNKS - 5:
                    for k in range(KT):
                        dve.wait_ge(S("n1_hi"), k + 1)
                        v.scalar_tensor_tensor(in_lo[k], h[:, k, :], vec[:, k:k + 1], in_hi[k].bitcast(F32),
                                               ALU.mult, ALU.subtract).then_inc(S("n1_act"), 1)

            dve.wait_ge(S("silu_c"), 1)
            v.tensor_tensor(mod_in[:, :, 2:4], silu_c.rearrange("p j k -> p k j"), mod_in[:, :, 0:2].bitcast(F32),
                            ALU.subtract).then_inc(S("mod_in"), 1)
            split_lo(dve, pre_w, 0)
            dve.wait_ge(S("small_landed"), 48)
            v.tensor_copy(pos_f, pos_i).then_inc(S("pos_ready"), 1)
            mod_step()
            dve.wait_ge(S("xc_ready"), 4)
            squares(xc, pre_x, z_n[:, 0, :], "pre_ssq")
            dve.wait_ge(S("w_ba_hi"), 1)
            v.tensor_tensor(ba_lo[:, :, :], w_ba, ba_hi[:, :, :].bitcast(F32), ALU.subtract).then_inc(S("w_ba_split"), 2)
            mod_step()
            b = full("pre", "rows")
            v.tensor_copy(dn_rows[:, :], ps[b][:, T:T + 16])
            free(v.tensor_scalar(rope_s[:, :], ps[b][:, 0:T], col("inv_freq"), None, ALU.mult), b)
            dve.drain().then_inc(S("rope_arg"), 1)
            mod_step()
            mod_step()

            dve.wait_ge(S("exp_a"), 1)
            v.tensor_scalar(neg_a[:, :], neg_a[:, :], -1.0, None, ALU.mult)
            for _ in range(4, MOD_FIRST):
                mod_step()

            def modulation(lo, hi):
                bm = vec[:, V["b_mod_2"] + lo:V["b_mod_2"] + hi].unsqueeze(2).broadcast_to([P, hi - lo, 2])
                return v.tensor_tensor(modc[:, lo:hi, :], ps[3][:, 2 * lo:2 * hi].rearrange("p (m j) -> p m j", j=2),
                                       bm, ALU.add)

            def gain_of(i, norm, tile, j):
                n = V[norm]
                v.scalar_tensor_tensor(gains[:, i, :], modc[:, tile:tile + KT, j], 1.0, vec[:, n:n + KT], ALU.add, ALU.mult)

            dve.wait_ge(S("mod_cols"), MOD_FIRST)
            dve.wait_ge(S("vec_ready"), 1)
            modulation(0, 16)
            dve.drain()
            gain_of(0, "norm1_g_2", 8, 0)
            gain_of(1, "norm1_g_2", 8, 1)
            dve.drain()
            dve.wait_ge(S("pre_rstd"), 1)
            modulated(xc, lambda k: gains[:, 1, k:k + 1], lambda k: modc[:, k, 1:2], ("dn_mt", "dn_hi"), "dn_act")
            dve.wait_ge(S("tables"), 16)
            dve_delta(dve, "ctx", pre_w, MOD_FIRST, "pre", filler("ctx", mod_step))
            dve.wait_ge(S("mod_cols"), MOD_CHUNKS)
            free(modulation(16, 48), 3)
            dve.drain()
            gain_of(2, "norm2_g_2", 32, 0)
            fn = vec[:, V["final_norm"]:V["final_norm"] + KT]
            v.tensor_tensor(final_g[:, 0, :], fn, gains[:, 0, :], ALU.mult)
            v.tensor_tensor(final_g[:, 1, :], fn, fn, ALU.mult)
            dve.drain()
            v.tensor_scalar(final_g[:, 1, :], final_g[:, 1, :], EPS, None, ALU.add)
            for x in win:
                v.memset(x[:, :, 0:PADW], 0.0)
            dve.drain().then_inc(S("pads"), 1)

            with dve.Fori(0, DEPTH) as layer:
                w = layer_where(layer)
                W = lambda use: full("layer", use, layer)
                bank = lambda use: banks.bank("layer", use)
                wait = lambda name, n, per: dve.wait_ge(S(name), w.nth(n, per))
                done = lambda s: dve.wait_ge(pieces_done, w.pieces(s, 1))

                def norm_lo(name, at, tiles=range(KT), hi=all_hi, lo=all_lo, before=0):
                    for k in tiles:
                        wait(name + "_hi", before + k + 1, KT)
                        v.scalar_tensor_tensor(lo[k], h[:, k, :], cur_vec[:, at + k:at + k + 1],
                                               hi[k].bitcast(F32), ALU.mult, ALU.subtract).then_inc(
                                                   S(name + "_act"), 1)

                def sum_squares(n):
                    wait("sq_ready", n, 3)
                    v.tensor_reduce(red, sq.rearrange("p k t -> p t k"), AX.X, ALU.add).then_inc(S("ssq_in"), 1)

                of_layers = lambda c: vec[:, c:c + DEPTH * LV].rearrange("p (l n) -> p l n", l=DEPTH)
                dve.drain()
                v.tensor_copy(cur_vec[:, 0:LV], of_layers(0)[:, layer, :])
                v.tensor_copy(cur_vec[:, LV:LV + KT], of_layers(LV)[:, layer, 0:KT])
                dve.drain().then_inc(S("cur_vec"), 1)
                split_lo(dve, w, 1)
                sum_squares(1)
                b = W("p")
                wait("p_hi", 1, 1)
                free(v.tensor_tensor(plo[:, :, :], pair(b), phi[:, :, :].bitcast(F32), ALU.subtract), b)
                dve.drain().then_inc(S("p_act"), 1)

                def rotated(s):
                    b = W(f"rot{s}")
                    free(v.tensor_tensor(z_sin[s % 2], pair(b), wide(tab_s, 2), ALU.mult), b)
                    dve.drain()
                    wait("z_cos", s + 1, 6)
                    dst = (k_r, q_r)[s % 2][:, 2 * (s // 2):2 * (s // 2) + 2, :]
                    v.tensor_tensor(dst, z_sin[s % 2], z_cos[s % 2], ALU.add).then_inc(S("qk_ready"), 1)

                def maxima(first, last):
                    for n in range(first, last):
                        hd = HEADS[n]
                        b = W(f"s{hd}")
                        g, batch, i = hd // HPG, n // 6, hd % 2
                        mask = col("mask", 384 * g, 384)
                        v.tensor_tensor(prob[:, hd, 0:P], ps[b][:, 0:P], mask[:, 0:P], ALU.add)
                        ins = v.tensor_tensor_reduce(prob[:, hd, P:384], ps[b][:, P:384], mask[:, P:384], 1.0, -3e38,
                                                     ALU.add, ALU.max, mx[:, g, batch, i, 1:2])
                        dve.drain()
                        v.tensor_reduce(mx[:, g, batch, i, 0:1], prob[:, hd, 0:P], AX.X, ALU.max)
                        free(ins, b)
                        dve.drain()
                        v.tensor_scalar(nb[:, g, batch, i, :], mx[:, g, batch, i, :], -QSCALE, None,
                                        ALU.mult).then_inc(S("max_ready"), 1)
                        if n % 6 == 5:
                            greatest(batch)

                def greatest(batch):
                    flat = lambda x, g: x[:, g, batch].rearrange("p i q -> p (i q)")
                    v.tensor_tensor(top[:, batch], flat(mx, 0), flat(mx, 1), ALU.max)
                    dve.drain()
                    v.tensor_tensor(top[:, batch], top[:, batch], flat(mx, 2), ALU.max)
                    dve.drain()
                    for g in range(3):
                        v.tensor_tensor(flat(dm, g), flat(mx, g), top[:, batch], ALU.subtract)
                    dve.drain().then_inc(S("top_ready"), 1)

                def weights(batch):
                    flat = lambda x, g: x[:, g, batch].rearrange("p i q -> p (i q)")
                    wait("exp_ready", batch + 1, 2)
                    for g in range(3):
                        v.tensor_tensor(flat(wl, g), flat(ex, g), flat(sm, g), ALU.mult)
                    dve.drain()
                    v.tensor_tensor(tot[:, batch], flat(wl, 0), flat(wl, 1), ALU.add)
                    dve.drain()
                    v.tensor_tensor(tot[:, batch], tot[:, batch], flat(wl, 2), ALU.add)
                    dve.drain()
                    v.reciprocal(rtot[:, batch], tot[:, batch])
                    dve.drain()
                    for g in range(3):
                        v.tensor_tensor(flat(fac, g), flat(ex, g), rtot[:, batch], ALU.mult)
                    dve.drain()
                    for hd in heads(batch):
                        g, i = hd // HPG, hd % 2
                        for t in range(TT):
                            e = prob[:, hd, P * t:P * t + P * (t + 1)]
                            ins = v.tensor_scalar(e, e, fac[:, g, batch, i, t:t + 1], None, ALU.mult)
                        ins.then_inc(S("prob_ready"), 1)

                for s in range(1, 6):
                    split_lo(dve, w, s + 1)
                    if s == 1:
                        wait("rstd_1", 1, 1)
                        v.tensor_tensor(tab_c, rope_c[:, :], rstd_w[:, 0:T], ALU.mult)
                        v.tensor_tensor(tab_s, rope_s[:, :], rstd_w[:, 0:T], ALU.mult)
                        dve.drain().then_inc(S("tab_ready"), 1)
                    rotated(s - 1)
                split_lo(dve, w, 7)
                rotated(5)
                split_lo(dve, w, 8)
                maxima(0, 4)
                split_lo(dve, w, 9)
                maxima(4, 8)
                weights(0)
                done(8)
                b = bank("u")
                free(v.tensor_tensor(win[0][:, :, PADW:], pair(b), wide(rstd_w[:, 0:T], 2), ALU.mult), b)
                dve.drain().then_inc(S("u_ready"), 1)
                maxima(8, 12)
                split_lo(dve, w, 10)
                weights(1)
                for n, (kind, x) in enumerate([kx for kx in ATT if kx[0] in ("V", "pool")]):
                    if n == 3:
                        split_lo(dve, w, 11)
                    wait("cat_hi", n + 1, 7)
                    if kind == "V":
                        b = bank(f"pv{x}")
                        free(v.tensor_tensor(xlo[:, 2 + x, :], ps[b][:, 0:T], xhi[:, 2 + x, :].bitcast(F32),
                                             ALU.subtract), b)
                    else:
                        b = bank("pool")
                        for i in range(2):
                            ins = v.scalar_tensor_tensor(xlo[:, i, :], ps[b][:, T * i:T * (i + 1)],
                                                         cur_vec[:, 24 + i:25 + i], xhi[:, i, :].bitcast(F32),
                                                         ALU.mult, ALU.subtract)
                        free(ins, b)
                    dve.drain().then_inc(S("cat_act"), 1)
                dve.drain().then_inc(S("side_free"), 1)
                for c in range(4):
                    if c:
                        split_lo(dve, w, 11 + c)
                    done(10 + c)
                    b = bank(f"out{c}")
                    hc = h[:, 2 * c:2 * c + 2, :]
                    free(v.tensor_tensor(hc, hc, pair(b), ALU.add), b)
                    dve.drain().then_inc(S("h2_ready"), 1)
                norm_lo("n2", KT)
                split_lo(dve, w, 15)
                for s in range(14, 46):
                    if s > 14:
                        split_lo(dve, w, s + 1)
                    kind, j = KIND[s]
                    if kind == "down":
                        continue
                    wait("relu", j + 1, UPS)
                    v.tensor_tensor(relu2[j % 2], relu[j % 2], relu[j % 2], ALU.mult).then_inc(S("relu2"), 1)
                    wait("relu_hi", j + 1, UPS)
                    y2 = slice(2 * (j % 2), 2 * (j % 2) + 2)
                    v.tensor_tensor(ylo[:, y2, :], relu2[j % 2], yhi[:, y2, :].bitcast(F32), ALU.subtract).then_inc(
                        S("relu_act"), 1)
                    if j == SSQ2_AT - 1:
                        sum_squares(2)
                split_lo(dve, w, 47)
                wait("inv_ms", 1, 1)
                done(45)
                for c in range(4):
                    b = bank(f"down{c}")
                    free(v.tensor_tensor(update[c], pair(b), wide(inv_ms, 2), ALU.mult), b)
                    dve.drain().then_inc(S("h3_in"), 1)
                    if c == 1:
                        split_lo(dve, w, 48)
                        norm_lo("n3", 2 * KT, range(0, 2))
                norm_lo("n3", 2 * KT, range(2, 8))
                split_lo(dve, w, 49)
                sum_squares(3)
                split_lo(dve, w, 50)
                wait("rstd_3", 1, 1)

                def gate_in(c):
                    done(48 + c)
                    b = bank(f"gate{c}")
                    free(v.tensor_tensor(update[c], pair(b), wide(rstd[:, :], 2), ALU.mult), b)
                    dve.drain().then_inc(S("gate_in"), 1)

                def gated(c):
                    wait("gate_out", c + 1, 4)
                    b = bank(f"ple{c}")
                    hc = h[:, 2 * c:2 * c + 2, :]
                    free(v.tensor_tensor(update[c], update[c], pair(b), ALU.mult), b)
                    dve.drain()
                    v.tensor_tensor(hc, hc, update[c], ALU.add)
                    dve.drain().then_inc(S("h1_ready"), 1)

                def next_input(c):
                    norm_lo("n1", LV, range(2 * c, 2 * c + 2), in_hi, in_lo, KT)

                gate_in(0)
                gate_in(1)
                gated(0)
                split_lo(dve, w, 51)
                gated(1)
                gate_in(2)
                next_input(0)
                gated(2)
                next_input(1)
                gate_in(3)
                split_lo(dve, w, 52)
                gated(3)
                next_input(2)
                next_input(3)

            w = post_w
            W = lambda use: full("post", use)
            bank = lambda use: banks.bank("post", use)
            done = lambda l: dve.wait_ge(pieces_done, w.pieces(l, 1))
            nxt = lambda l: split_lo(dve, w, l + 1) if more(w, l) else None
            for k in range(6, 8):
                v.scalar_tensor_tensor(pre_x[:, k, :], h[:, k, :], final_g[:, 1, k:k + 1], h[:, k, :], ALU.mult, ALU.mult)
            dve.drain().then_inc(S("post_sq_end"), 1)
            dve.wait_ge(S("post_rstd"), 1)
            modulated(h, lambda k: final_g[:, 0, k:k + 1], lambda k: modc[:, k, 0:1], ("dn_mt", "dn_hi"), "dn_act", 8)

            def final_norm():
                dve.wait_ge(S("post_rstd"), 2)
                for k in range(KT):
                    v.scalar_tensor_tensor(h[:, k, :], h[:, k, :], vcol("final_norm", k), rope_c[:, :], ALU.mult, ALU.mult)

            n_tiles = len(lat_tiles)
            left = [0]

            def lat_fill():
                i = left[0]
                left[0] += 1
                nxt(n_tiles + i)
                if i == 4:
                    final_norm()
                if i and LAT_FILL[i - 1] in ("sc4", "sc5"):
                    c = int(LAT_FILL[i - 1][-1])
                    done(n_tiles + i - 1)
                    if c == 4:
                        dve.wait_ge(S("sc_bc"), 1)
                    b = bank(LAT_FILL[i - 1])
                    s2 = slice(2 * (c % 2), 2 * (c % 2) + 2)
                    free(v.tensor_tensor(sc_p[:, s2, :], pair(b), sc_p[:, s2, :], ALU.mult), b)
                    if c == 5:
                        dve.drain().then_inc(S("sc_p"), 1)

            dve_delta(dve, "lat", w, 0, "post", filler("lat", lat_fill))
            l = n_tiles + len(LAT_FILL)
            for i in range(2):
                o2 = o_n[:, 2 * i:2 * i + 2, :]
                v.tensor_tensor(ff_s[i], o2, o2, ALU.mult).then_inc(S("o_sq"), 1)
            grid = lambda x: x.rearrange("p (r w) -> p r w", w=GRID_W)
            dve.wait_ge(S("sc_conv1"), 1)
            for tap in (0, 2):
                for k in range(4):
                    x, y = grid(sc_p[:, k, :]), grid(sc_y[:, k, :])
                    to, of = (slice(1, GRID_W), slice(0, GRID_W - 1)) if tap == 0 else (slice(0, GRID_W - 1), slice(1, GRID_W))
                    v.scalar_tensor_tensor(y[:, :, to], x[:, :, of], vcol("sc_conv_w_2", 4 * tap + k), y[:, :, to],
                                           ALU.mult, ALU.add)
                dve.drain()
            v.tensor_tensor(sc_y, sc_y, sc_b, ALU.mult).then_inc(S("sc_done"), 1)
            for i in range(2):
                o2 = o_n[:, 2 * i:2 * i + 2, :]
                dve.wait_ge(S("o_rstd"), i + 1)
                v.tensor_tensor(o2, o2, rstd_b[:, :].rearrange("p (m t) -> p m t", m=2), ALU.mult).then_inc(
                    S("o_normed"), 1)
            dve.drain()
            dve.wait_ge(S("lat_z"), 1)
            v.scalar_tensor_tensor(o_n, o_n, vcol("dn_onorm_g_2"), z_n, ALU.mult, ALU.mult).then_inc(S("o_done"), 1)
            dve.drain()
            for c in range(2):
                b = bank(f"fpos{c}")
                dve.wait_ge(S("branch_hi"), c + 1)
                free(v.tensor_tensor(ylo[:, 2 * c:2 * c + 2, :], pair(b), yhi[:, 2 * c:2 * c + 2, :].bitcast(F32),
                                     ALU.subtract), b)
                dve.drain().then_inc(S("branch_act"), 1)
            def merged_lo(c):
                for k in (2 * c, 2 * c + 1):
                    dve.wait_ge(S("merged_hi"), k + 1)
                    v.tensor_tensor(xlo[:, k, :], merged[:, k, :], xhi[:, k, :].bitcast(F32), ALU.subtract).then_inc(
                        S("merged_act"), 1)

            for n in range(3):
                for c in range(4):
                    nxt(l)
                    if n and c == 0:
                        src = (sc_y, o_n)[n - 1]
                        for i in range(2):
                            dve.wait_ge(S("branch_hi"), 2 * n + i + 1)
                            s2 = slice(2 * i, 2 * i + 2)
                            v.tensor_tensor(ylo[:, s2, :], src[:, s2, :], yhi[:, s2, :].bitcast(F32),
                                            ALU.subtract).then_inc(S("branch_act"), 1)
                    l += 1
                for i in range(2):
                    nxt(l)
                    done(l)
                    dve.wait_ge(S("gate_sig"), 4 * (n + 1))
                    for c in (2 * i, 2 * i + 1):
                        b = bank(f"y{n}{c}")
                        s2 = slice(2 * c, 2 * c + 2)
                        if n == 0:
                            free(v.tensor_tensor(merged[:, s2, :], pair(b), gate[:, s2, :], ALU.mult), b)
                        else:
                            free(v.tensor_tensor(ff_s[c % 2], pair(b), gate[:, s2, :], ALU.mult), b)
                            dve.drain()
                            v.tensor_tensor(merged[:, s2, :], merged[:, s2, :], ff_s[c % 2], ALU.add)
                        dve.drain().then_inc(S("y_merged"), 1)
                        if n == 2 and c:
                            merged_lo(c - 1)
                    l += 1
            merged_lo(3)

            def residual(b, c, tile):
                for m in range(2):
                    k = 2 * c + m
                    ins = v.scalar_tensor_tensor(h[:, k, :], ps[b][:, T * m:T * (m + 1)], modc[:, tile + k, 0:1],
                                                 h[:, k, :], ALU.mult, ALU.add)
                free(ins, b)
                dve.drain().then_inc(S("h_res"), 1)

            for c in range(4):
                nxt(l)
                done(l)
                residual(bank(f"wo{c}"), c, 16)
                l += 1
            dve.wait_ge(S("post_rstd"), 3)
            modulated(h, lambda k: gains[:, 2, k:k + 1], lambda k: modc[:, 24 + k, 0:1], ("n2_mt", "n2_hi_2"), "n2_act_2")
            for j in range(FF2 // 256):
                nxt(l)
                l += 1
                nxt(l)
                done(l)
                dve.wait_ge(S("ff_s"), j + 1)
                b = bank(f"ffb{j}")
                if j >= 2:
                    dve.drain()
                free(v.tensor_tensor(ff_p[j % 2], ff_s[j % 2], pair(b), ALU.mult), b)
                dve.drain().then_inc(S("ff_p"), 1)
                dve.wait_ge(S("ff_hi"), j + 1)
                y2 = slice(2 * (j % 2), 2 * (j % 2) + 2)
                v.tensor_tensor(ylo[:, y2, :], ff_p[j % 2], yhi[:, y2, :].bitcast(F32), ALU.subtract).then_inc(
                    S("ff_act"), 1)
                l += 1
                if j:
                    nxt(l)
                    l += 1
            done(l)
            for b in range(4):
                residual(b, b, 40)
            dve.wait_ge(S("post_rstd"), 4)
            for k in range(KT):
                v.scalar_tensor_tensor(h[:, k, :], h[:, k, :], vcol("final_g_2", k), rstd[:, :], ALU.mult,
                                       ALU.mult).then_inc(S("y_cols"), 1)
            for c in range(4):
                if c % 2 == 1:
                    b = W(f"y_out{c}")
                    free(v.tensor_copy(y_rows[:, c % 2, 512 * (c // 2):512 * (c // 2 + 1)], ps[b][:, :]), b)
                    dve.drain().then_inc(S(f"y_rows{c // 2}"), 1)

        @block.gpsimd
        def _(pool):
            g = nc.gpsimd
            g.memset(pool_w[:, :, :], 0.0).then_inc(S("side_free"), 1)
            pool.wait_ge(S("tables"), 16)
            pool_delta(pool, "ctx")
            pool.wait_ge(S("pads"), 1)
            with pool.Fori(0, DEPTH) as layer:
                pool.wait_ge(S("tab_ready"), layer + 1)
                for s in range(6):
                    pool.wait_ge(S("z_raw"), layer * 6 + s + 1)
                    if s >= 2:
                        pool.wait_ge(S("qk_ready"), layer * 6 + s - 1)
                    g.tensor_tensor(z_cos[s % 2], z_raw[s % 2], wide(tab_c, 2), ALU.mult).then_inc(S("z_cos"), 1)
                pool.wait_ge(S("u_ready"), layer + 1)
                for n in range(4):
                    sh = 1 << n
                    g.tensor_tensor(win[n + 1][:, :, PADW:], win[n][:, :, PADW:], win[n][:, :, PADW - sh:PADW + T - sh],
                                    ALU.add)
                    pool.drain()
                cnt = col("inv_cnt", 0, 2 * T).rearrange("p (i t) -> p i t", i=2)
                for n in range(4):
                    i, e = n // 2, slice(HEAD * (n % 2), HEAD * (n % 2 + 1))
                    g.tensor_tensor(win[n + 1][e, i, PADW:], win[n + 1][e, i, PADW:], cnt[e, i, :], ALU.mult)
                pool.drain()
                for n in range(4):
                    i, e = n // 2, slice(HEAD * (n % 2), HEAD * (n % 2 + 1))
                    g.tensor_tensor(win[0][e, i, PADW:], win[n + 1][e, i, PADW:], win[0][e, i, PADW:], ALU.subtract)
                pool.drain().then_inc(S("pool_y"), 1)
                for c in range(4):
                    hc = h[:, 2 * c:2 * c + 2, :]
                    pool.wait_ge(S("h3_in"), layer * 4 + c + 1)
                    g.tensor_tensor(hc, hc, update[c], ALU.add).then_inc(S("h3_ready"), 1)
            for c in range(3):
                pool.wait_ge(S("h1_ready"), 4 * (DEPTH - 1) + c + 1)
                for k in range(2 * c, 2 * c + 2):
                    g.tensor_scalar(pre_x[:, k, :], h[:, k, :], final_g[:, 1, k:k + 1], None, ALU.mult)
                pool.drain()
                g.tensor_tensor(pre_x[:, 2 * c:2 * c + 2, :], pre_x[:, 2 * c:2 * c + 2, :], h[:, 2 * c:2 * c + 2, :],
                                ALU.mult).then_inc(S("post_sq"), 1)
            pool_delta(pool, "lat")

        @block.sync
        def _(sp):
            def load(slot, src, n=CH):
                shape = src.shape
                dst = raw[:, slot, 0:n].rearrange("p (k n) -> p k n", k=shape[1])
                sp.dma_start(dst, src).then_inc(landed[slot], 16)

            sp.dma_start(rows_ab[0:ROWS_A, 0:P], a["vec_rows"][0:ROWS_A, :]).then_inc(S("rows_landed"), 16)
            sp.dma_start(rows_ab[0:NV - ROWS_A, P:2 * P], a["vec_rows"][ROWS_A:NV, :]).then_inc(S("rows_landed"), 16)
            sp.dma_start(kt[:, 0:first_tables], a["consts"][:, 0:first_tables]).then_inc(S("consts"), 16)
            for l, src in enumerate(pre_src):
                if l >= RAW:
                    sp.wait_ge(lo_ready, 2 * (l - RAW + 1))
                load(l % RAW, src)
            with sp.Fori(0, DEPTH) as layer:
                sp.wait_ge(S("side_free"), layer + 1)
                sp.wait_ge(S("consts"), 16)
                sp.dma_start(p_tok, a["p"][layer, 0].rearrange("(t q) d -> q t d", q=P)).then_inc(S("side_landed"), 16)
                for s in range(2):
                    e = slice(HEAD * s, HEAD * (s + 1))
                    sp.dma_start(pool_w[e, :, e], a["pool_w"][layer].rearrange("(i s) c d -> s c i d", s=2)[s]).then_inc(
                        S("side_landed"), 16)
                for l, src in enumerate(layer_src(layer)):
                    if l != 8:
                        sp.wait_ge(lo_ready, layer * (2 * LAYER_CHUNKS) + 2 * (C_LAYER + l + (l == 7) - RAW + 1))
                    load(l % RAW, src, CH // 2 if half_chunk(l) else CH)
            for l, src in enumerate(post_src):
                sp.wait_ge(lo_ready, 2 * (C_POST + l - RAW + 1))
                load(l % RAW, src)
            for c in range(2):
                sp.wait_ge(S(f"y_rows{c}"), 2)
                sp.dma_start(out[0].rearrange("(t p) d -> p t d", p=P)[:, :, 512 * c:512 * (c + 1)],
                             y_rows[:, :, 512 * c:512 * (c + 1)]).then_inc(S("stored"), 16)
            sp.wait_ge(S("stored"), 32)


_INS = ["x", "p", "positions", "w_in", "pool_w", "w_out", "w_up", "w_down", "w_gate", "w_ple", "ctx_2", "w_mod_2", "w_in_2",
        "w_dn_out_2", "w_sc_out_2", "w_fn_out_2", "w_gate_2", "w_o_2", "w_ffn_in_2", "w_ffn_out_2"]


def kernel(**inputs):
    import concourse.bacc as bacc
    from concourse.bass_utils import run_bass_kernel_spmd

    arrays = {name: np.ascontiguousarray(inputs[name]) for name in _INS}
    rows = [np.asarray(inputs[n])[l] for l in range(DEPTH) for n, _ in LAYER_VECS]
    rows += [np.asarray(inputs[n]) for n, _ in TILE_A + TILE_B]
    arrays["vec_rows"] = np.concatenate([r.reshape(-1, P) for r in rows], 0)
    arrays["dn_row"] = np.concatenate([np.asarray(inputs[n]).reshape(1, -1) for n in ("dn_a_log_2", "dn_dt_bias_2")], 1)
    arrays["consts"] = const_tables()
    nc = bacc.Bacc("TRN2", target_bir_lowering=False, num_devices=1, dynamic_dma_scratch_size=1024)
    aps = {n: nc.dram_tensor("in_" + n, v.shape, mybir.dt.from_np(v.dtype), kind="ExternalInput").ap()
           for n, v in arrays.items()}
    out = nc.dram_tensor("out", (1, T, D), F32, kind="ExternalOutput").ap()
    two_blocks(nc, aps, out)
    r = run_bass_kernel_spmd(nc, [{"in_" + n: v for n, v in arrays.items()}], core_ids=[0])
    return r.results[0]["out"]
```
